# Optimizing a Trainium2 kernel written in Bass

```python
import jax
import jax.numpy as jnp
from jax import lax
import numpy as np

D_MODEL = 1024
BATCH = 1
SEQ = 128
DEPTH = 2
DEC_BATCH = 1
DEC_SEQ = 256
PAST_LEN = 128

GRID_W = 64
N_EVEN = (DEPTH + 1) // 2
N_ODD = DEPTH // 2
EPS = 1e-6
GLA_HEADS = 4
GLA_DK = D_MODEL // 16
GLA_DV = D_MODEL // 8
GLA_RANK = 16
GLA_CHUNK = 64
GLA_GATE_TAU = 16.0
GMLP_GROUPS = 4
GMLP_DIM = D_MODEL // 8
GMLP_CHUNK = 128
ATT_HEADS = 8
ATT_KV_HEADS = 2
HEAD_DIM = D_MODEL // ATT_HEADS
Q_BLOCK = 128
ROPE_THETA = 10000.0
MOE_GROUPS = 4
MOE_PER_GROUP = 8
N_EXPERTS = MOE_GROUPS * MOE_PER_GROUP
MOE_TOPK = 2
D_EXPERT = D_MODEL // 4

GLA_QK_W = GLA_HEADS * GLA_DK
GLA_V_W = GLA_HEADS * GLA_DV
GMLP_W = GMLP_GROUPS * GMLP_DIM
EVEN_SPLITS = (GLA_QK_W, 2 * GLA_QK_W, 2 * GLA_QK_W + GLA_V_W, 2 * GLA_QK_W + 2 * GLA_V_W,
               2 * GLA_QK_W + 2 * GLA_V_W + GLA_RANK, 2 * GLA_QK_W + 2 * GLA_V_W + 2 * GLA_RANK,
               2 * GLA_QK_W + 2 * GLA_V_W + 2 * GLA_RANK + GMLP_W)
EVEN_IN = 2 * GLA_QK_W + 2 * GLA_V_W + 2 * GLA_RANK + 2 * GMLP_W
EVEN_MIX = GLA_V_W + GMLP_W
ATT_Q_W = ATT_HEADS * HEAD_DIM
ATT_KV_W = ATT_KV_HEADS * HEAD_DIM
ODD_IN = ATT_Q_W + 2 * ATT_KV_W

kernel_name = 'hybrid_gla_gmlp_gqa_hmoe_flow_step'

F32 = jnp.float32

def rms_norm(x, g):
    x32 = x.astype(F32)
    y = x32 * lax.rsqrt(jnp.mean(x32 * x32, axis=-1, keepdims=True) + EPS)
    return (y * g.astype(F32)).astype(x.dtype)

def layer_norm(x):
    x32 = x.astype(F32)
    xc = x32 - jnp.mean(x32, axis=-1, keepdims=True)
    return (xc * lax.rsqrt(jnp.mean(xc * xc, axis=-1, keepdims=True) + EPS)).astype(x.dtype)

def adaln(cond, w, b):
    mod = jax.nn.silu(cond) @ w + b
    return [a[:, None, :] for a in jnp.split(mod, 6, axis=-1)]

def modulate(h, shift, scale):
    return h * (1 + scale) + shift

def gla_chunk_scan(q, k, v, log_a, s0):
    B, T, H, DK = q.shape
    DV = v.shape[-1]
    n = T // GLA_CHUNK

    def chunks(a):
        return a.astype(F32).reshape(B, n, GLA_CHUNK, H, a.shape[-1]).transpose(1, 0, 3, 2, 4)

    lower = jnp.tril(jnp.ones((GLA_CHUNK, GLA_CHUNK), bool))[:, :, None]

    def step(S, inp):
        qi, ki, vi, ai = inp
        b = jnp.cumsum(ai, axis=2)
        diff = jnp.where(lower, b[:, :, :, None, :] - b[:, :, None, :, :], -jnp.inf)
        att = jnp.einsum('bhtd,bhsd,bhtsd->bhts', qi, ki, jnp.exp(diff))
        o = jnp.einsum('bhts,bhsv->bhtv', att, vi) + jnp.einsum('bhtd,bhdv->bhtv', qi * jnp.exp(b), S)
        b_end = b[:, :, -1, :]
        S = jnp.exp(b_end)[..., None] * S + jnp.einsum(
            'bhsd,bhsv->bhdv', ki * jnp.exp(b_end[:, :, None, :] - b), vi)
        return S, o

    S, o = lax.scan(step, s0.astype(F32), (chunks(q), chunks(k), chunks(v), chunks(log_a)))
    return o.transpose(1, 0, 3, 2, 4).reshape(B, T, H, DV), S

def even_mixer(h, s_f, s_b, w_in, w_gate_up, b_gate_up, gla_g, w_s, b_s, w_out):
    B, T, _ = h.shape
    q, k, v, g, a_f, a_b, u, vg = jnp.split(h @ w_in, EVEN_SPLITS, axis=-1)
    q = q.reshape(B, T, GLA_HEADS, GLA_DK) * GLA_DK ** -0.5
    k = k.reshape(B, T, GLA_HEADS, GLA_DK)
    v = v.reshape(B, T, GLA_HEADS, GLA_DV)

    def log_decay(a, d):
        z = (a @ w_gate_up[d] + b_gate_up[d]).astype(F32)
        return (jax.nn.log_sigmoid(z) / GLA_GATE_TAU).reshape(B, T, GLA_HEADS, GLA_DK)

    def rev(t):
        return t[:, ::-1]

    o_f, st_f = gla_chunk_scan(q, k, v, log_decay(a_f, 0), s_f)
    o_b, st_b = gla_chunk_scan(rev(q), rev(k), rev(v), rev(log_decay(a_b, 1)), s_b)
    o = rms_norm(o_f + rev(o_b), gla_g) * jax.nn.silu(g.reshape(B, T, GLA_HEADS, GLA_DV).astype(F32))
    o = o.reshape(B, T, GLA_V_W).astype(h.dtype)
    n = T // GMLP_CHUNK
    vg = layer_norm(jax.nn.gelu(vg).reshape(B, n, GMLP_CHUNK, GMLP_GROUPS, GMLP_DIM))
    sg = jnp.einsum('gts,bnsgc->bntgc', w_s, vg) + b_s.T[None, None, :, :, None]
    ob = (jax.nn.gelu(u) * sg.reshape(B, T, GMLP_W)).astype(h.dtype)
    y = jnp.concatenate([o, ob], axis=-1) @ w_out
    return y, st_f, st_b

def attn_qkv(h, w_in, gq, gk):
    B, T, _ = h.shape
    q, k, v = jnp.split(h @ w_in, (ATT_Q_W, ATT_Q_W + ATT_KV_W), axis=-1)
    q = rms_norm(q.reshape(B, T, ATT_HEADS, HEAD_DIM), gq)
    k = rms_norm(k.reshape(B, T, ATT_KV_HEADS, HEAD_DIM), gk)
    return q, k, v.reshape(B, T, ATT_KV_HEADS, HEAD_DIM)

def axial_rope(T):
    rows = T // GRID_W
    row = jnp.repeat(jnp.arange(rows), GRID_W).astype(F32)
    col = jnp.tile(jnp.arange(GRID_W), rows).astype(F32)
    n_freq = HEAD_DIM // 4
    inv = ROPE_THETA ** (-jnp.arange(n_freq, dtype=F32) / n_freq)
    ang = jnp.concatenate([row[:, None] * inv, col[:, None] * inv], axis=-1)
    return jnp.cos(ang)[None, :, None, :], jnp.sin(ang)[None, :, None, :]

def apply_rope(x, cos, sin):
    x32 = x.astype(F32)
    x1, x2 = x32[..., 0::2], x32[..., 1::2]
    out = jnp.stack([x1 * cos - x2 * sin, x1 * sin + x2 * cos], axis=-1).reshape(x.shape)
    return out.astype(x.dtype)

def attend(q, k, v):
    B, Tq, H, HD = q.shape
    G = H // ATT_KV_HEADS
    nb = Tq // Q_BLOCK
    qb = q.reshape(B, nb, Q_BLOCK, ATT_KV_HEADS, G, HD).swapaxes(0, 1)
    k32, v32 = k.astype(F32), v.astype(F32)

    def one_block(qi):
        s = jnp.einsum('bqhgd,bkhd->bhgqk', qi.astype(F32), k32) * HD ** -0.5
        p = jax.nn.softmax(s, axis=-1)
        return jnp.einsum('bhgqk,bkhd->bqhgd', p, v32)

    o = lax.map(one_block, qb)
    return o.swapaxes(0, 1).reshape(B, Tq, H * HD).astype(q.dtype)

def hier_moe(h, w_rg, b_rg, w_re, b_re, w_g, w_u, w_d):
    B, T, D = h.shape
    x = h.reshape(B * T, D)
    g_prob = jax.nn.softmax((x @ w_rg + b_rg).astype(F32), axis=-1)
    g_p, g_i = lax.top_k(g_prob, 1)
    e_logits = (x @ w_re + b_re).astype(F32).reshape(-1, MOE_GROUPS, MOE_PER_GROUP)
    e_sel = jnp.take_along_axis(e_logits, g_i[:, :, None], axis=1)[:, 0]
    e_v, e_i = lax.top_k(e_sel, MOE_TOPK)
    gate = jax.nn.softmax(e_v, axis=-1) * g_p
    expert = g_i * MOE_PER_GROUP + e_i
    combine = jnp.sum(jax.nn.one_hot(expert, N_EXPERTS, dtype=F32) * gate[..., None], axis=1)
    hid = jax.nn.silu(jnp.einsum('nd,edf->nef', x, w_g)) * jnp.einsum('nd,edf->nef', x, w_u)
    hid = hid * combine[:, :, None].astype(hid.dtype)
    y = hid.reshape(B * T, N_EXPERTS * D_EXPERT) @ w_d.reshape(N_EXPERTS * D_EXPERT, D)
    return y.reshape(B, T, D).astype(h.dtype)

def setup_inputs(seed: int = 0) -> dict:
    key = jax.random.key(seed)
    keys = iter(jax.random.split(key, 40))

    def nrm(shape, scale):
        return jax.random.normal(next(keys), shape, F32) * scale

    D = D_MODEL
    return {
        'x_prompt': nrm((BATCH, SEQ, D), 1.0),
        'x_sample': nrm((DEC_BATCH, DEC_SEQ, D), 1.0),
        'state_gla': nrm((DEC_BATCH, N_EVEN, 2, GLA_HEADS, GLA_DK, GLA_DV), 1.0),
        'cache_k': nrm((DEC_BATCH, N_ODD, PAST_LEN, ATT_KV_HEADS, HEAD_DIM), 1.0),
        'cache_v': nrm((DEC_BATCH, N_ODD, PAST_LEN, ATT_KV_HEADS, HEAD_DIM), 1.0),
        'c': nrm((DEC_BATCH, D), 1.0),
        'c_ctx': nrm((D,), 1.0),
        'w_mod': nrm((DEPTH, D, 6 * D), 0.5 * D ** -0.5),
        'b_mod': nrm((DEPTH, 6 * D), 0.02),
        'norm1_g': 1.0 + nrm((DEPTH, D), 0.02),
        'norm2_g': 1.0 + nrm((DEPTH, D), 0.02),
        'w_in_even': nrm((N_EVEN, D, EVEN_IN), D ** -0.5),
        'w_gate_up': nrm((N_EVEN, 2, GLA_RANK, GLA_QK_W), GLA_RANK ** -0.5),
        'b_gate_up': nrm((N_EVEN, 2, GLA_QK_W), 0.02),
        'gla_norm_g': 1.0 + nrm((N_EVEN, GLA_DV), 0.02),
        'w_spatial': nrm((N_EVEN, GMLP_GROUPS, GMLP_CHUNK, GMLP_CHUNK), GMLP_CHUNK ** -0.5),
        'b_spatial': nrm((N_EVEN, GMLP_GROUPS, GMLP_CHUNK), 0.02),
        'w_out_even': nrm((N_EVEN, EVEN_MIX, D), EVEN_MIX ** -0.5),
        'w_in_odd': nrm((N_ODD, D, ODD_IN), D ** -0.5),
        'q_norm_g': 1.0 + nrm((N_ODD, HEAD_DIM), 0.02),
        'k_norm_g': 1.0 + nrm((N_ODD, HEAD_DIM), 0.02),
        'w_out_odd': nrm((N_ODD, ATT_Q_W, D), ATT_Q_W ** -0.5),
        'w_router_group': nrm((DEPTH, D, MOE_GROUPS), D ** -0.5),
        'b_router_group': nrm((DEPTH, MOE_GROUPS), 0.01),
        'w_router_expert': nrm((DEPTH, D, N_EXPERTS), D ** -0.5),
        'b_router_expert': nrm((DEPTH, N_EXPERTS), 0.01),
        'w_exp_gate': nrm((DEPTH, N_EXPERTS, D, D_EXPERT), D ** -0.5),
        'w_exp_up': nrm((DEPTH, N_EXPERTS, D, D_EXPERT), D ** -0.5),
        'w_exp_down': nrm((DEPTH, N_EXPERTS, D_EXPERT, D), D_EXPERT ** -0.5),
        'final_norm_g': 1.0 + nrm((D,), 0.02),
    }

def reference(x_prompt, x_sample, state_gla, cache_k, cache_v, c, c_ctx, w_mod, b_mod, norm1_g, norm2_g,
              w_in_even, w_gate_up, b_gate_up, gla_norm_g, w_spatial, b_spatial, w_out_even,
              w_in_odd, q_norm_g, k_norm_g, w_out_odd, w_router_group, b_router_group,
              w_router_expert, b_router_expert, w_exp_gate, w_exp_up, w_exp_down, final_norm_g):
    def channel_sublayer(x, m, l):
        h = modulate(rms_norm(x, norm2_g[l]), m[3], m[4])
        y = hier_moe(h, w_router_group[l], b_router_group[l], w_router_expert[l], b_router_expert[l],
                     w_exp_gate[l], w_exp_up[l], w_exp_down[l])
        return x + m[5] * y

    def even_params(i):
        return (w_in_even[i], w_gate_up[i], b_gate_up[i], gla_norm_g[i], w_spatial[i], b_spatial[i],
                w_out_even[i])

    xc = x_prompt
    Bc = xc.shape[0]
    gla_states, ctx_k, ctx_v = [], [], []
    for l in range(DEPTH):
        i = l // 2
        m = adaln(c_ctx[None], w_mod[l], b_mod[l])
        h = modulate(rms_norm(xc, norm1_g[l]), m[0], m[1])
        if l % 2 == 0:
            zero = jnp.zeros((Bc, GLA_HEADS, GLA_DK, GLA_DV), F32)
            y, st_f, st_b = even_mixer(h, zero, zero, *even_params(i))
            gla_states.append(jnp.stack([st_f, st_b], axis=1))
        else:
            q, k, v = attn_qkv(h, w_in_odd[i], q_norm_g[i], k_norm_g[i])
            y = attend(q, k, v) @ w_out_odd[i]
            ctx_k.append(k)
            ctx_v.append(v)
        xc = xc + m[2] * y
        xc = channel_sublayer(xc, m, l)
    y_prompt = rms_norm(xc, final_norm_g)
    new_state_gla = jnp.stack(gla_states, axis=1).astype(x_prompt.dtype)
    new_cache_k = jnp.stack(ctx_k, axis=1)
    new_cache_v = jnp.stack(ctx_v, axis=1)

    xs = x_sample
    cos, sin = axial_rope(xs.shape[1])
    for l in range(DEPTH):
        i = l // 2
        m = adaln(c, w_mod[l], b_mod[l])
        h = modulate(rms_norm(xs, norm1_g[l]), m[0], m[1])
        if l % 2 == 0:
            y, _, _ = even_mixer(h, state_gla[:, i, 0], state_gla[:, i, 1], *even_params(i))
        else:
            q, k, v = attn_qkv(h, w_in_odd[i], q_norm_g[i], k_norm_g[i])
            q = apply_rope(q, cos, sin)
            k = apply_rope(k, cos, sin)
            keys = jnp.concatenate([cache_k[:, i].astype(k.dtype), k], axis=1)
            vals = jnp.concatenate([cache_v[:, i].astype(v.dtype), v], axis=1)
            y = attend(q, keys, vals) @ w_out_odd[i]
        xs = xs + m[2] * y
        xs = channel_sublayer(xs, m, l)
    y_sample = rms_norm(xs, final_norm_g)

    return (y_prompt, y_sample, new_state_gla, new_cache_k, new_cache_v)


_drawn_inputs = setup_inputs


def setup_inputs(seed=0):
    import zlib

    import numpy as np

    out = dict(_drawn_inputs(seed))
    spreads = {}
    factors = {'state_gla': 4.659,
     'cache_k': 3.353,
     'cache_v': 3.163,
     'norm2_g': 3.252,
     'b_gate_up': 6.239,
     'gla_norm_g': 7.458,
     'b_spatial': 7.14,
     'q_norm_g': 8.0,
     'k_norm_g': 2.975,
     'b_router_group': 5.475,
     'b_router_expert': 5.414,
     'final_norm_g': 2.927}
    for name, (base, spread) in spreads.items():
        noise = np.random.default_rng([zlib.crc32(name.encode()), seed]).standard_normal(out[name].shape)
        drawn = base * np.exp(spread * noise) if base else spread * noise
        out[name] = jnp.asarray(drawn.astype(out[name].dtype))
    for name, factor in factors.items():
        out[name] = (out[name] * factor).astype(out[name].dtype)
    return out
```

```python
from contextlib import ExitStack

import numpy as np

import concourse.bass as bass
from concourse import mybir

P = 128
D = 1024
KC = D // P
NB = 3
T = NB * P
EPS = 1e-6
COLS = 512
RING = 6
GLA_HEADS, GLA_DK, GLA_DV, GLA_RANK = 4, 64, 128, 16
GLA_TAU = 16.0
QK_W = GLA_HEADS * GLA_DK
V_W = GLA_HEADS * GLA_DV
GROUPS = 4
ATT_HEADS, KV_HEADS, HD = 8, 2, 128
N_EXP, PER_GROUP, MOE_GROUPS = 32, 8, 4
F_EXP = D // 4
PAIRS = N_EXP // 2
HALF = 64
MAX_ROUNDS = T // HALF
GRID_W = 64
BIG = 1e30

ALU = mybir.AluOpType
ACT = mybir.ActivationFunctionType
AX = mybir.AxisListType
F32 = mybir.dt.float32
U32 = mybir.dt.uint32
U8 = mybir.dt.uint8
F32R = mybir.dt.float32r
LEVELS = [64, 32, 16, 8, 4, 2, 1]


def shape_constants():
    i = np.arange(P)
    masks = np.zeros((P, len(LEVELS), P), np.float32)
    for n, m in enumerate(LEVELS):
        same = (i[:, None] // (2 * m)) == (i[None, :] // (2 * m))
        other = (i[:, None] // m) != (i[None, :] // m)
        masks[:, n, :] = same & other
    pick = np.zeros((P, 2 + 2 * 32), np.float32)
    for j in range(4):
        for s in range(2):
            pick[32 * j + s, s] = 1.0
    for r in range(32):
        pick[[r, 32 + r], 2 + 2 * r:4 + 2 * r] = 1.0
    n_freq = HD // 4
    t = np.arange(2 * P)
    inv = (10000.0 ** (-np.arange(n_freq, dtype=np.float32) / n_freq)).astype(np.float32)
    row = (t // GRID_W).astype(np.float32)[:, None] * inv
    col = (t % GRID_W).astype(np.float32)[:, None] * inv
    ang = np.concatenate([row, col], axis=-1)
    rope = np.stack([np.cos(ang), np.sin(ang)], axis=1).astype(np.float32)
    rope = np.ascontiguousarray(rope.reshape(2, P, 2, HD // 2).transpose(1, 0, 2, 3))
    return {
        "k_ident": np.eye(P, dtype=np.float32),
        "k_before": (i[:, None] < i[None, :]).astype(np.float32),
        "k_iota": np.broadcast_to(i.astype(np.float32), (P, P)).copy(),
        "k_masks": masks,
        "k_pick": pick,
        "k_rope": rope,
    }


MOD_FRONT = [(0, 0), (0, 1), (0, 2), (0, 3), (0, 8), (0, 9), (1, 2), (1, 3), (1, 8), (1, 9)]
MOD_EVEN = [(0, 4), (0, 5), (0, 6), (0, 7), (0, 10), (0, 11), (1, 0), (1, 1)]
MOD_ODD = [(1, 4), (1, 5), (1, 6), (1, 7), (1, 10), (1, 11)]
MOD_REST = MOD_EVEN + MOD_ODD
MODS = MOD_FRONT + MOD_REST
FRONT = len(MOD_FRONT)
EVEN_PLAN = ["part", "g0", "sum", "part", "g1", "sum", 0, "part", "g2", "sum", 1, "part", "vg0", "sum", 2, "part", "vg1", "sum", 3,
             "part", "vg2", "sum", 4, "part", "u0", "sum", 5, "part", "u1", "sum", 6, "u2", 7]


def weight_chunks():
    first = [("mod", i) for i in range(FRONT)] + [("even_in", 0), ("even_in", 1)]
    i = FRONT
    for step in EVEN_PLAN:
        if step == "part":
            first.append(("mod", i))
            i += 1
        elif step in ("g0", "vg0", "u0"):
            first.append(("even_in", {"g0": 2, "vg0": 3, "u0": 4}[step]))
    assert i == FRONT + len(MOD_EVEN)
    first += [("even_out", n) for n in range(2)]
    second = [("odd_in", n) for n in (2, 0, 1)] + [("mod", m) for m in range(i, len(MODS))] + [("odd_out", n) for n in range(2)]
    return first, second


FIRST, SECOND = weight_chunks()
CHUNKS = FIRST + SECOND
ROOTS = ["norm_0", "ln", "gla", "norm_1", "norm_2", "qk", "norm_3", "norm_4"]
TURNS = [0, "cat", 1, 2, 3]
EVEN_COLS = [0, 2 * QK_W, 2 * QK_W + V_W, 2 * QK_W + 2 * V_W + 2 * GLA_RANK + 512, 2 * QK_W + 2 * V_W + 2 * GLA_RANK]
A_COL = 2 * QK_W + 2 * V_W


def slot_of(j):
    return (j - len(FIRST)) % RING


def scaled(i):
    return MODS[i][1] // 2 in (1, 4)


def fills_of(j):
    return sum(slot_of(i) == slot_of(j) for i in range(j + 1))


def last_in(slot, upto):
    return max(j for j in range(upto) if slot_of(j) == slot)


def build(nc, d, outs):
    ctx = ExitStack()
    sems = {}

    def S(name):
        if name not in sems:
            sems[name] = ctx.enter_context(nc.semaphore(name))
        return sems[name]

    address = {}

    def sb(name, cols, dt=F32, parts=P):
        address[name] = (nc.sbuf_base + 31) // 32 * 32
        return ctx.enter_context(nc.sbuf_tensor(name, [parts, cols], dt))

    with ctx:
        ring = sb("ring", RING * 4096)
        x_t = sb("x", NB * D)
        h_t = sb("h", NB * D)
        ht_t = sb("ht", KC * T)
        gs_t = sb("shift_scale", 4 * D)
        gt_t = sb("gate_rows", 2 * D)
        ar = sb("arena", 11264)
        ident = sb("ident", P)
        before = sb("before", P)
        iota = sb("iota", P)
        masks = sb("masks", len(LEVELS) * P, U8)
        ones = sb("ones", P)
        pick = sb("pick", 2 + 2 * 32)
        mod_bias = sb("mod_bias", COLS, F32R, parts=64)
        pick_bias = sb("pick_bias", 2 * 32, F32R, parts=64)
        cond_t = sb("cond_silu", KC * 32)
        small = sb("small", 264)
        psum = ctx.enter_context(nc.psum_tensor("psum", [P, 8, 512], F32))
        mod_rows = nc.dram_tensor("mod_rows", (2, 6, 2, D), F32, kind="Internal").ap()

        X = x_t[:, :].rearrange("p (b n) -> p b n", b=NB)
        H = h_t[:, :].rearrange("p (b n) -> p b n", b=NB)
        HT = ht_t[:, :].rearrange("p (k t) -> p k t", k=KC)
        GS = gs_t[:, :].rearrange("p (a s n) -> p a s n", a=2, s=2)
        GT = gt_t[:, :].rearrange("p (s n) -> p s n", s=2)
        RC = ring[:, :].rearrange("p (r k n) -> p r k n", r=RING, k=KC)
        RG = ring[:, :].rearrange("p (r e k n) -> p r e k n", r=RING, e=2, k=KC)
        RD = ring[:, :].rearrange("p (r e k n) -> p r e k n", r=RING, e=2, k=2)
        RS = ring[:, :].rearrange("p (r e n) -> p r e n", r=RING, e=2)

        def bank(b):
            return psum[:, b, :]

        def rounded(name, base, col, cols):
            t = nc.alloc_sbuf_tensor_at(name, [P, cols], F32R, offset=address[base] + 4 * col)
            return t[:, :]

        class View:

            def __init__(self, base):
                self.at, self.base = 0, base

            def __call__(self, cols, pattern=None, parts=P, **sizes):
                v = self.base[0:parts, self.at:self.at + cols]
                self.at += cols
                return v.rearrange(pattern, **sizes) if pattern else v

        sm = View(small)
        ss, ms, rs, rt = sm(3), sm(3), sm(3), sm(3)
        b_gate = sm(4)
        b_spat = sm(4)
        gla_ms, gla_rs, gla_rt = sm(12), sm(12), sm(12)
        ln_rs, ln_rt, ln_v = sm(12), sm(12), sm(12)
        dec_f, dec_b = sm(2), sm(2)
        att_max, att_sum = sm(24, "p (i h) -> p i h", i=6), sm(24, "p (i h) -> p i h", i=6)
        q_ms, q_rs, q_rt = sm(30), sm(30), sm(30)

        cond_silu = cond_t[:, :].rearrange("p (k m) -> p k m", m=32)
        vm = View(ar)
        mod_part = [vm(COLS) for _ in range(2)]
        front_row = [vm(COLS, parts=2) for _ in range(FRONT)]

        ve = View(ar)
        QK = ve(4 * T, "p (c t) -> p c t", c=4)
        BF = ve(2 * T, "p (c t) -> p c t", c=2)
        BB = ve(2 * T, "p (c t) -> p c t", c=2)
        ATT = ve(12 * P, "p (i t) -> p i t", i=12)
        V = ve(NB * 512, "p (b n) -> p b n", b=NB)
        SG = ve(NB * 512, "p (b n) -> p b n", b=NB)
        VG = ve(NB * 512, "p (b n) -> p b n", b=NB)
        U = ve(NB * 512, "p (b n) -> p b n", b=NB)
        WST = ve(GROUPS * P, "p (g t) -> p g t", g=GROUPS)
        bias_raw = U[0:64, 1, :]
        cond = WST.rearrange("p g t -> p (g t)")[:, 0:KC * 2].rearrange("p (k s) -> p k s", s=2)
        WA = VG[:, 0:1, 0:256].rearrange("p o (k n) -> p (o k) n", k=KC)
        WS_RAW = U[:, 0, :].rearrange("p (g s) -> p g s", g=GROUPS)
        EX = [H[:, :, :].rearrange("p b n -> p (b n)")[:, i * 1536:(i + 1) * 1536].rearrange("p (c t) -> p c t", c=4) for i in range(2)]
        MASKS_F32 = SG.rearrange("p b n -> p (b n)")[:, 0:len(LEVELS) * P]
        vz = View(gs_t)
        Z = vz(4 * T, "p (c t) -> p c t", c=4)
        EZ = vz(4 * T, "p (c t) -> p c t", c=4)
        AT = vz(T, parts=32)
        WGU = vz(512, parts=32)
        GLAG = vz(P)
        v2 = View(gs_t)
        E2 = v2(8 * 256, "p (a c t) -> p a c t", a=4, c=2)
        KDT = v2(8 * P, "p (i t) -> p i t", i=8)
        vs = View(gt_t)
        S0 = vs(1024, "p (a h v) -> p a h v", a=2, h=4)
        S1 = vs(1024, "p (a h v) -> p a h v", a=2, h=4)
        O = ATT.rearrange("p i t -> p (i t)").rearrange("p (b n) -> p b n", b=NB)
        OSQ = QK.rearrange("p c t -> p (c t)")
        ST_OUT = BF.rearrange("p c t -> p (c t)")[:, 0:512].rearrange("p (a c v) -> p a c v", a=2, c=2)
        BN = BB.rearrange("p c t -> p (c t)")[:, 0:12 * 8].rearrange("p (i n) -> p i n", i=12)
        UPD = [QK.rearrange("p c t -> p (c t)")[:, i * 512:(i + 1) * 512] for i in range(2)]

        vo = View(ar)
        QKV = vo(NB * 1536, "p (b n) -> p b n", b=NB)
        KT = vo(KV_HEADS * 4 * P, "p (g b t) -> p g b t", g=KV_HEADS, b=4)
        CK = vo(256)
        CV = vo(256)
        ROPE = vo(256, "p (b c n) -> p b c n", b=2, c=2)
        GQ, GK = vo(P), vo(P)
        PR0 = vo(1536)
        SQ_QK = vo(1280, "p (h n) -> p h n", h=10)
        RT1, RT2 = (SQ_QK.rearrange("p h n -> p (h n)")[:, i * 640:(i + 1) * 640].rearrange("p (h n) -> p h n", h=10) for i in range(2))
        RT3, RT4 = (PR0[:, i * 640:(i + 1) * 640].rearrange("p (h n) -> p h n", h=10) for i in range(2))
        UPD_O = [RT1.rearrange("p h n -> p (h n)")[:, 0:512], RT2.rearrange("p h n -> p (h n)")[:, 0:512]]
        QT = H[:, :, :].rearrange("p b n -> p (b n)").rearrange("p (h t) -> p h t", h=8)
        vg_ = View(gs_t)
        PR = [PR0.rearrange("p (h n) -> p h n", h=4), vg_(1536, "p (h n) -> p h n", h=4)]
        PT = vg_(1536, "p (k n) -> p k n", k=3)
        OT = HT

        vx = View(ar)
        XT = vx(KC * P, "p (k s) -> p k s", k=KC)
        XS = vx(D)
        Y_LO = rounded("y_low", "arena", vx.at, D)
        Y = vx(D)
        Y_HI = rounded("y_top", "arena", vx.at, D)
        vx(D)
        SGM = [vx(256) for _ in range(2)]
        HID = [vx(256) for _ in range(2)]
        HTS = [vx(256, "p (k s) -> p k s", k=2) for _ in range(2)]
        WR = vx(KC * 36, "p (k n) -> p k n", k=KC)
        BR = vx(8)[0:36, 0:1]
        PW = [vx(NB * P, "p (b s) -> p b s", b=NB) for _ in range(2)]
        PP = [rounded(f"places_{v}", "arena", vx.at + v * NB * P, NB * P).rearrange("p (b s) -> p b s", b=NB) for v in range(2)]
        vx(2 * NB * P)
        PTMP = vx(NB * P, "p (b s) -> p b s", b=NB)
        PWT = vx(NB * P, "p (b t) -> p b t", b=NB)
        PPT = rounded("slots_t", "arena", vx.at, NB * P).rearrange("p (b t) -> p b t", b=NB)
        vx(NB * P)
        w_slot = vx(1)
        LT = vx(T, parts=36)
        LG = vx(NB * 36, "p (b n) -> p b n", b=NB)
        g_max, g_idx, g_sum, g_prob = vx(3), vx(3), vx(3), vx(3)
        g_tmp = vx(12, "p (b n) -> p b n", b=NB)
        e_mask = vx(NB * 32, "p (b n) -> p b n", b=NB)
        top_v = vx(NB * 8, "p (b n) -> p b n", b=NB)
        top_i = vx(NB * 8, "p (b n) -> p b n", b=NB)
        top_f = vx(NB * 2, "p (b n) -> p b n", b=NB)
        gates = vx(6, "p (j b) -> p j b", j=2)
        oh = [vx(NB * 32, "p (b n) -> p b n", b=NB) for _ in range(2)]
        oh_sum = vx(NB * 32, "p (b n) -> p b n", b=NB)
        cnt = vx(NB * 32, "p (b n) -> p b n", b=NB)
        pos = vx(6, "p (j b) -> p j b", j=2)
        i_a, i_b, i_c = vx(6), vx(6), vx(6)
        srel = vx(6, "p (j b) -> p j b", j=2)
        n_max, n_rounds, n_tmp = vx(1), vx(1), vx(5)
        rounds = vx(1)
        H_HI = rounded("h_top", "shift_scale", 0, NB * D).rearrange("p (b n) -> p b n", b=NB)
        H_LO = rounded("h_low", "h", 0, NB * D).rearrange("p (b n) -> p b n", b=NB)
        ACC = ht_t[:, :].rearrange("p (b n) -> p b n", b=NB)
        UPD_M = [XT.rearrange("p k s -> p (k s)"), XS]
        iota32 = iota[:, 0:32]

        def col_src(j):
            name, n = CHUNKS[j]
            if name == "mod":
                l, c = MODS[n]
                return d["w_mod"][l].rearrange("(p k) n -> p k n", k=KC)[:, :, c * COLS:(c + 1) * COLS]
            if name == "even_in":
                c = EVEN_COLS[n]
                return d["w_in_even"][0].rearrange("(p k) n -> p k n", k=KC)[:, :, c:c + COLS]
            if name == "even_out":
                return d["w_out_even"][0].rearrange("(p k) n -> p k n", k=KC)[:, :, n * COLS:(n + 1) * COLS]
            if name == "odd_in":
                return d["w_in_odd"][0].rearrange("(p k) n -> p k n", k=KC)[:, :, n * COLS:(n + 1) * COLS]
            return d["w_out_odd"][0].rearrange("(k p) n -> p k n", k=KC)[:, :, n * COLS:(n + 1) * COLS]

        def rest_buffers(i):
            slot = slot_of(CHUNKS.index(("mod", i)))
            return RC[:, slot, 0, :], RC[0:2, slot, 1, :]

        def rounds_of(eng, l):
            eng.wait_ge(S("rounds_ready"), l + 1)
            return eng.value_load(rounds[0:1, 0:1].bitcast(U32), min_val=0, max_val=MAX_ROUNDS - 1) + 1

        def used_up(eng, j):
            name, n = CHUNKS[j]
            if name == "mod" and n < FRONT:
                eng.wait_ge(S("mod_part_ps"), n + 1)
            elif name == "mod":
                eng.wait_ge(S("rest_stored"), 16 * (n - FRONT + 1))
            elif name == "even_in":
                eng.wait_ge(S(("qk_ps", "v_ps", "g_ps", "vg_ps", "u_ps")[n]), (4, 3, 3, 3, 3)[n])
            elif name == "even_out":
                eng.wait_ge(S("even_out_ps"), NB * (n + 1))
            elif name == "odd_in":
                eng.wait_ge(S("odd_in_ps"), NB * ((2, 0, 1).index(n) + 1))
            else:
                eng.wait_ge(S("odd_out_ps"), NB * (n + 1))

        block = ctx.enter_context(nc.Block())

        @block.sync
        def _(sp):
            def load_chunk(j):
                sp.dma_start(RC[:, slot_of(j)], col_src(j)).then_inc(S(f"chunk_in_{slot_of(j)}"), 16)

            def load_experts(l, a, first_expert, slot):
                w = d[("w_exp_gate", "w_exp_up", "w_exp_down")[a]][l].rearrange("e (p k) n -> p e (k n)", p=P)
                sp.dma_start(RS[:, slot], w[:, bass.ds(first_expert, 2), :]).then_inc(S(f"moe{l}_in_{slot}"), 16)

            with nc.allow_non_contiguous_dma(reason="small vectors by channel"):
                sp.dma_start(cond[:, :, 0:1].rearrange("p k s -> p (k s)"), d["c_ctx"].rearrange("(p k) -> p k", k=KC)).then_inc(S("cond_in"), 16)
                sp.dma_start(cond[:, :, 1:2].rearrange("p k s -> p (k s)"), d["c"][0].rearrange("(p k) -> p k", k=KC)).then_inc(S("cond_in"), 16)
            sp.dma_start(pick[:, :], d["k_pick"]).then_inc(S("mod_small"), 16)
            for r in (0, 32):
                sp.dma_start(bias_raw[r:r + 24, :], d["b_mod"].rearrange("l (n c) -> (l n) c", c=COLS)).then_inc(S("mod_small"), 16)
                for part in range(2):
                    gains = d[("norm1_g", "norm2_g")[part]].rearrange("l (h c) -> (l h) c", c=COLS)
                    sp.dma_start(bias_raw[r + 24 + 4 * part:r + 28 + 4 * part, :], gains).then_inc(S("mod_small"), 16)
            for j in range(len(FIRST)):
                if j == 3:
                    sp.dma_start(X[:, 0, :], d["x_prompt"][0]).then_inc(S("x_loaded"), 16)
                    sp.dma_start(X[:, 1:3, :], d["x_sample"][0].rearrange("(b p) n -> p b n", p=P)).then_inc(S("x_loaded"), 16)
                if j >= RING:
                    used_up(sp, j - RING)
                load_chunk(j)

            def experts(l, before_first):
                for u in range(2):
                    for a in range(3):
                        before_first(3 * u + a)
                        load_experts(l, a, 2 * u, 3 * u + a)
                R = rounds_of(sp, l)
                with sp.Fori(1, R * (PAIRS // 2)) as i:
                    for u in range(2):
                        first_expert = sp.snap(((i * 2 + u) % PAIRS) * 2)
                        multiplied = sp.snap(i * 2 + (u - 1))
                        down_multiplied = sp.snap(i * 4 + (2 * u - 2))
                        sp.wait_ge(S(f"moe{l}_gate_up"), multiplied)
                        sp.sem_inc(S("slots_freed"), 1)
                        load_experts(l, 0, first_expert, 3 * u)
                        load_experts(l, 1, first_expert, 3 * u + 1)
                        sp.wait_ge(S(f"moe{l}_down"), down_multiplied)
                        sp.sem_inc(S("slots_freed"), 1)
                        load_experts(l, 2, first_expert, 3 * u + 2)
                return R

            R = experts(0, lambda slot: used_up(sp, last_in(slot, len(FIRST))))
            sp.wait_ge(S("moe0_gate_up"), R * PAIRS - 1)
            for j in range(2):
                load_chunk(len(FIRST) + j)
            sp.wait_ge(S("moe0_down"), R * (2 * PAIRS) - 2)
            load_chunk(len(FIRST) + 2)
            sp.wait_ge(S("moe0_gate_up"), R * PAIRS)
            for j in range(3, 5):
                load_chunk(len(FIRST) + j)
            sp.wait_ge(S("moe0_down"), R * (2 * PAIRS))
            load_chunk(len(FIRST) + 5)
            for j in range(RING, len(SECOND)):
                used_up(sp, len(FIRST) + j - RING)
                load_chunk(len(FIRST) + j)

            experts(1, lambda slot: used_up(sp, last_in(slot, len(CHUNKS))))

        @block.gpsimd
        def _(pool):
            def load(dst, src, sem="consts"):
                pool.dma_start(dst, src).then_inc(S(sem), 16)

            def load_rows(u, part, dst, sem):
                n = dst.shape[1]
                l = u // 2
                src = mod_rows[l, 3 * (u % 2) + part[0]:3 * (u % 2) + part[1]].rearrange("a s n -> (a s n)")
                pool.dma_start(dst, src.rearrange("(o n) -> o n", o=1).broadcast_to([P, n])).then_inc(S(sem), 16)

            load(ident[:, :], d["k_ident"])
            load(before[:, :], d["k_before"])
            load(iota[:, :], d["k_iota"])
            load(MASKS_F32, d["k_masks"].rearrange("p l t -> p (l t)"), "masks_in")
            def load_router(l):
                with nc.allow_non_contiguous_dma(reason="router weights"):
                    load(WR[:, :, 0:4], d["w_router_group"][l].rearrange("(p k) n -> p k n", k=KC), "router_in")
                    load(WR[:, :, 4:36], d["w_router_expert"][l].rearrange("(p k) n -> p k n", k=KC), "router_in")
                    load(BR[0:4, :], d["b_router_group"][l].rearrange("(n o) -> n o", o=1), "router_in")
                    load(BR[4:36, :], d["b_router_expert"][l].rearrange("(n o) -> n o", o=1), "router_in")

            with nc.allow_non_contiguous_dma(reason="small vectors by channel"):
                load(b_gate, d["b_gate_up"][0].rearrange("a (c p) -> p (a c)", p=P))
                load(b_spat, d["b_spatial"][0].rearrange("g t -> t g"))

            def store_mod(i, row, sem):
                l, n = MODS[i]
                part, half = divmod(n, 2)
                pool.dma_start(mod_rows[l, part, :, half * COLS:(half + 1) * COLS], row).then_inc(S(sem), 16)

            load(WA, d["w_in_even"][0].rearrange("(p k) n -> p k n", k=KC)[:, :, A_COL:A_COL + 2 * GLA_RANK], "even_small")
            load(WS_RAW, d["w_spatial"][0].rearrange("g t s -> t g s"), "even_small")
            pool.memset(S0.rearrange("p a h v -> p (a h v)"), 0.0).then_inc(S("pool_zeros"), 1)
            pool.memset(S1.rearrange("p a h v -> p (a h v)"), 0.0).then_inc(S("pool_zeros"), 1)
            pool.wait_ge(S("pool_zeros"), 2)
            for a in range(2):
                for h in range(GLA_HEADS):
                    r = 64 * (h % 2)
                    load(S0[r:r + 64, a, h, :], d["state_gla"][0, 0, a, h], "state_in")
            for i in range(4, FRONT):
                pool.wait_ge(S("front_row_ready"), i + 1)
                store_mod(i, front_row[i], "front_stored")

            pool.wait_ge(S("h_ready"), NB)
            pool.memset(WGU, 0.0).then_inc(S("pool_zeros"), 1)
            pool.wait_ge(S("pool_zeros"), 3)
            for a in range(2):
                load(WGU[a * GLA_RANK:(a + 1) * GLA_RANK, a * QK_W:(a + 1) * QK_W], d["w_gate_up"][0, a], "even_small")
            load(GLAG, d["gla_norm_g"][0].rearrange("(o n) -> o n", o=1).broadcast_to([P, P]), "even_small")

            def store_rest(mods):
                for i in mods:
                    pool.wait_ge(S("rest_row_ready"), i - FRONT + 1)
                    store_mod(i, rest_buffers(i)[1], "rest_stored")
                    pool.wait_ge(S("rest_stored"), 16 * (i - FRONT + 1))

            store_rest(range(FRONT, FRONT + len(MOD_EVEN)))
            pool.wait_ge(S("states_ready"), 1)
            for a in range(2):
                for hh in range(2):
                    dst = outs["new_state_gla"][0, 0, a, hh::2].rearrange("c d v -> d c v")
                    pool.dma_start(dst, ST_OUT[64 * hh:64 * hh + 64, a]).then_inc(S("stored"), 16)
            pool.wait_ge(S("gla_out"), 3)
            load_rows(0, (2, 3), gt_t[:, :], "gate_in")
            load_router(0)
            pool.wait_ge(S("gla_gain_ready"), 1)
            load_rows(1, (0, 2), gs_t[:, :], "rows_in")

            def experts(l):
                u = 2 * l + 1
                pool.wait_ge(S("x_updated"), NB * u)
                load_rows(u, (2, 3), gt_t[:, :], "gate_in")
                pool.wait_ge(S("turned"), 6 * (TURNS.index(u) + 1))
                pool.wait_ge(S("h_top"), l + 1)
                pool.tensor_tensor(H_LO, H, H_HI, ALU.subtract).then_inc(S("h_split"), 1)
                R = rounds_of(pool, l)
                pool.wait_ge(S(f"moe{l}_xs_ps"), R * (PAIRS * 2) + 2)
                pool.sem_inc(S("rows_free"), 1)

            experts(0)
            load_rows(2, (0, 2), gs_t[:, :], "rows_in")
            pool.wait_ge(S("x_updated"), NB * 2)
            load(CK, d["cache_k"][0, 0].rearrange("t g n -> t (g n)"), "odd_small")
            load(CV, d["cache_v"][0, 0].rearrange("t g n -> t (g n)"), "odd_small")
            load(ROPE, d["k_rope"], "odd_small")
            load(GQ, d["q_norm_g"][0].rearrange("(o n) -> o n", o=1).broadcast_to([P, P]), "odd_small")
            load(GK, d["k_norm_g"][0].rearrange("(o n) -> o n", o=1).broadcast_to([P, P]), "odd_small")
            store_rest(range(FRONT + len(MOD_EVEN), len(MODS)))
            load_rows(2, (2, 3), gt_t[:, :], "gate_in")
            pool.wait_ge(S("qk_normed"), 1)
            pool.dma_start(outs["new_cache_k"][0, 0].rearrange("t g n -> t (g n)"), QKV[:, 0, 1024:1280]).then_inc(S("stored"), 16)
            pool.dma_start(outs["new_cache_v"][0, 0].rearrange("t g n -> t (g n)"), QKV[:, 0, 1280:1536]).then_inc(S("stored"), 16)
            pool.wait_ge(S("probs_t_used"), 6)
            load_rows(3, (0, 2), gs_t[:, :], "rows_in")
            load_router(1)
            pool.wait_ge(S("stored"), 16 * 6)
            experts(1)
            load(GS[:, 0, 0, :], d["final_norm_g"].rearrange("(o n) -> o n", o=1).broadcast_to([P, D]), "rows_in")
            for b in range(NB):
                pool.wait_ge(S("h_ready"), NB * 4 + b + 1)
                dst = outs["y_prompt"][0] if b == 0 else outs["y_sample"][0, (b - 1) * P:b * P]
                pool.dma_start(dst, H[:, b, :]).then_inc(S("stored"), 16)
            pool.wait_ge(S("stored"), 16 * 9)

        @block.tensor
        def _(pe):
            def chunk(name, n):
                j = CHUNKS.index((name, n))
                pe.wait_ge(S(f"chunk_in_{slot_of(j)}"), 16 * fills_of(j))
                return RC[:, slot_of(j)]

            def turn(b, ready, count):
                pe.wait_ge(S(ready), count)
                for half in range(2):
                    for kk in range(4):
                        t = pe.transpose(psum[:, 2 * b + half, kk * P:(kk + 1) * P], H[:, b, 4 * half + kk:D:KC], ident[:, :])
                    t.then_inc(S("turned"), 1)

            def project(to, b, w):
                for k in range(KC):
                    mm = pe.matmul(bank(to), HT[:, k, b * P:(b + 1) * P], w[:, k, :], start=(k == 0), stop=(k == KC - 1))
                return mm

            def mod_products(i):
                w = chunk("mod", i)
                if i < FRONT:
                    to = i % 2
                    if i >= 2:
                        pe.wait_ge(S("mod_part_sb"), i - 1)
                elif i < FRONT + len(MOD_EVEN):
                    to = 4
                    if i > FRONT:
                        pe.wait_ge(S("rest_row_ready"), i - FRONT)
                else:
                    to = 6
                    pe.wait_ge(S("mod_part_sb"), i)
                for r in range(2):
                    for j in range(4):
                        k = 4 * r + j
                        mm = pe.matmul(psum[32 * j:32 * j + 32, to, :], cond_silu[:, k, :], w[:, k, :], start=(r == 0), stop=(r == 1))
                mm.then_inc(S("mod_part_ps"), 1)

            def mod_sum(i):
                l, n = MODS[i]
                row = 12 * l + n
                gain = 24 + 4 * (n // 6) + 2 * l + n % 2
                pe.wait_ge(S("mod_part_sb"), i + 1)
                if i < FRONT:
                    to, part = 2 + i % 2, mod_part[i % 2]
                    if i >= 2:
                        pe.wait_ge(S("front_row_ready"), i - 1)
                    if scaled(i):
                        pe.matmul(psum[0:2, 4 + i % 2, :], pick_bias[:, 2 * gain:2 * gain + 2], mod_bias[:, :], start=True, stop=True)
                else:
                    to, part = 4 if i < FRONT + len(MOD_EVEN) else 7, rest_buffers(i)[0]
                    if i >= FRONT + len(MOD_EVEN):
                        pe.wait_ge(S("rest_row_ready"), i - FRONT)
                pe.matmul(psum[0:2, to, :], pick[:, 0:2], part, start=True, stop=False)
                pe.matmul(psum[0:2, to, :], pick_bias[:, 2 * row:2 * row + 2], mod_bias[:, :], start=False, stop=True).then_inc(S("mod_sum_ps"), 1)

            def spread(i):
                pe.wait_ge(S("front_row_ready"), i + 1)
                pe.wait_ge(S("consts"), 16 * 5)
                for s in range(2):
                    if i >= 1:
                        pe.wait_ge(S("spread_sb"), 2 * (i - 1) + s + 1)
                    pe.matmul(bank(6 + s), ident[0:2, s:s + 1].broadcast_to([2, P]), front_row[i], start=True, stop=True).then_inc(S("spread_ps"), 1)

            pe.wait_ge(S("bias_ready"), 2)
            pe.wait_ge(S("cond_ready"), 1)
            for i in range(FRONT):
                mod_products(i)
                if i >= 1:
                    mod_sum(i - 1)
                if 2 <= i < 6:
                    spread(i - 2)
            mod_sum(FRONT - 1)

            pe.wait_ge(S("even_small"), 32)
            for g in range(GROUPS):
                t = pe.transpose(psum[:, 7, g * P:(g + 1) * P], WS_RAW[:, g, :], ident[:, :])
            t.then_inc(S("sides_turned"), 1)
            pe.wait_ge(S("front_row_ready"), FRONT)
            for b in range(NB):
                turn(b, "h_ready", b + 1)
            pe.wait_ge(S("ht_ready"), 6)
            w = chunk("even_in", 0)
            for c in range(4):
                for k in range(KC):
                    mm = pe.matmul(psum[:, c, 0:T], w[:, k, c * P:(c + 1) * P], HT[:, k, :], start=(k == 0), stop=(k == KC - 1))
                mm.then_inc(S("qk_ps"), 1)
            for k in range(KC):
                mm = pe.matmul(psum[0:32, 4, 0:T], WA[:, k, :], HT[:, k, :], start=(k == 0), stop=(k == KC - 1))
            mm.then_inc(S("decay_in_ps"), 1)
            pe.wait_ge(S("spatial_ready"), 1)
            w = chunk("even_in", 1)
            project(5, 0, w).then_inc(S("v_ps"), 1)
            pe.wait_ge(S("decay_in_ready"), 1)
            pe.wait_ge(S("even_small"), 16 * 5)
            pe.wait_ge(S("qk_ready"), 4)
            for j in range(4):
                pe.matmul(psum[:, j, 0:T], WGU[:, j * P:(j + 1) * P], AT[:, :], start=True, stop=True).then_inc(S("decay_ps"), 1)
            for b in (1, 2):
                project(5 + b, b, w).then_inc(S("v_ps"), 1)

            def scores(n):
                src = QK if n == 0 else EX[(n - 1) % 2]
                if n == 0:
                    pe.wait_ge(S("z_ready"), 4)
                else:
                    pe.wait_ge(S("decayed_ready"), n)
                    pe.wait_ge(S("att_merged"), 2 * n)
                for r in range(2):
                    rows = slice(64 * r, 64 * r + 64)
                    for i in range(6):
                        b, c = divmod(i, 2)
                        mm = pe.matmul(psum[:, 2 * r + i // 4, (i % 4) * P:(i % 4 + 1) * P], src[rows, 2 + c, b * P:(b + 1) * P],
                                       src[rows, c, b * P:(b + 1) * P], start=True, stop=True)
                mm.then_inc(S("scores_ps"), 1)

            mod = FRONT
            for step in EVEN_PLAN:
                if step == "part":
                    mod_products(mod)
                    continue
                if step == "sum":
                    mod_sum(mod)
                    mod += 1
                    continue
                if isinstance(step, int):
                    scores(step)
                    continue
                name, b = step[:-1], int(step[-1])
                before_it = {"g": "v", "vg": "g", "u": "vg"}[name]
                if b == 0:
                    w = chunk("even_in", {"g": 2, "vg": 3, "u": 4}[name])
                pe.wait_ge(S(f"{before_it}_ready"), b + 1)
                project(5 + b, b, w).then_inc(S(f"{name}_ps"), 1)

            pe.wait_ge(S("u_ready"), 3)
            pe.wait_ge(S("rest_row_ready"), len(MOD_EVEN))
            pe.wait_ge(S("to_end_ready"), 1)
            for a in range(2):
                for jc in range(4):
                    t = pe.transpose(psum[:, 4 + a, jc * P:(jc + 1) * P], E2[:, 2 + a, jc % 2, (jc // 2) * P:(jc // 2 + 1) * P], ident[:, :])
            t.then_inc(S("sides_turned"), 1)
            pe.wait_ge(S("kdt_ready"), 1)
            for a in range(2):
                for j in range(2):
                    blk = j if a == 0 else 2 * j
                    for h in range(GLA_HEADS):
                        c, r = divmod(h, 2)
                        mm = pe.matmul(psum[64 * r:64 * r + 64, 6 + a, (2 * j + c) * P:(2 * j + c + 1) * P],
                                       KDT[:, 4 * a + 2 * j + c, 64 * r:64 * r + 64], V[:, blk, h * P:(h + 1) * P], start=True, stop=True)
            mm.then_inc(S("state_ps"), 1)
            pe.wait_ge(S("att_merged"), 16)
            pe.wait_ge(S("states_ready"), 2)
            for b in range(NB):
                for h in range(GLA_HEADS):
                    c, r = divmod(h, 2)
                    to = psum[:, b, h * P:(h + 1) * P]
                    mm = pe.matmul(to, ATT[:, 6 * r + 2 * b + c, :], V[:, b, h * P:(h + 1) * P], start=True, stop=(b == 0))
                    if b > 0:
                        fwd = (S0 if b == 1 else S1)[:, 0, h, :]
                        bwd = (S1 if b == 1 else S0)[:, 1, h, :]
                        pe.matmul(to, E2[:, 0, c, (b - 1) * P:b * P], fwd, start=False, stop=False)
                        mm = pe.matmul(to, E2[:, 1, c, (b - 1) * P:b * P], bwd, start=False, stop=True)
                mm.then_inc(S("gla_out"), 1)
            pe.wait_ge(S("vg_normed"), 1)
            for g in range(GROUPS):
                pe.matmul(psum[:, 3 + g, 0:T], WST[:, g, :], VG[:, :, g * P:(g + 1) * P], start=True, stop=True).then_inc(S("spatial_ps"), 1)
            for b in range(NB):
                turn(b, "cat_ready", 1)
            pe.wait_ge(S("ht_ready"), 6 * 2)
            for n in range(2):
                w = chunk("even_out", n)
                for b in range(NB):
                    project((6 + 3 * n + b) % 8, b, w).then_inc(S("even_out_ps"), 1)

            def experts(l):
                u = 2 * l + 1

                def M(name):
                    return S(f"moe{l}_{name}")

                for b in range(NB):
                    turn(b, "h_ready", NB * u + b + 1)
                pe.wait_ge(S("ht_ready"), 6 * (TURNS.index(u) + 1))
                pe.wait_ge(S("router_in"), 16 * 4 * (l + 1))
                for k in range(KC):
                    mm = pe.matmul(psum[0:36, 6, 0:T], WR[:, k, :], HT[:, k, :], start=(k == 0), stop=(k == KC - 1))
                mm.then_inc(S("logits_ps"), 1)
                pe.wait_ge(S("logits_t"), l + 1)
                for b in range(NB):
                    t = pe.transpose(psum[:, 7, b * 36:(b + 1) * 36], LT[:, b * P:(b + 1) * P], ident[0:36, 0:36])
                t.then_inc(S("logits_turned"), 1)
                pe.wait_ge(S("chosen"), l + 1)
                for b in range(NB):
                    for a in range(b + 1):
                        pe.matmul(psum[:, 6, b * 32:(b + 1) * 32], (before if a == b else ones)[:, :], oh_sum[:, a, :],
                                  start=(a == 0), stop=(a == b))
                for a in range(NB):
                    mm = pe.matmul(psum[:, 6, 96:128], ones[:, :], oh_sum[:, a, :], start=(a == 0), stop=(a == NB - 1))
                mm.then_inc(S("counts_ps"), 1)

                def gather(q, v, first=False):
                    pe.wait_ge(M("places_ready"), q + 1)
                    if not first:
                        pe.wait_ge(M("x_sb"), q * 2)
                    for half in range(2):
                        cols = slice(half * 512, (half + 1) * 512)
                        for b in range(NB):
                            pe.matmul(bank(half), PP[v][:, b, :], H_HI[:, b, cols], start=(b == 0), stop=False)
                            mm = pe.matmul(bank(half), PP[v][:, b, :], H_LO[:, b, cols], start=False, stop=(b == NB - 1))
                        mm.then_inc(M("xs_ps"), 1)

                def turn_rows(q):
                    pe.wait_ge(M("xs_sb"), q * 2 + 2)
                    for half in range(2):
                        for kk in range(4):
                            t = pe.transpose(psum[:, half, kk * P:(kk + 1) * P], XS[:, 4 * half + kk:D:KC], ident[:, :])
                        t.then_inc(M("x_ps"), 1)

                def weights_back(q, v, first=False):
                    if not first:
                        pe.wait_ge(M("added"), q * 6)
                    for b in range(NB):
                        t = pe.transpose(psum[:, 7, b * P:(b + 1) * P], PW[v][:, b, :], ident[:, :])
                    t.then_inc(M("weights_ps"), 1)

                def combine(q, first=False):
                    pe.wait_ge(M("y_split"), q * 2 + 2)
                    pe.wait_ge(M("slots_t"), q + 1)
                    for c in range(6):
                        b, n = divmod(c, 2)
                        to = bank((6, 7, 4, 5, 6, 7)[c])
                        if c >= 4:
                            pe.wait_ge(M("added"), q * 6 + c - 3)
                        cols = slice(n * 512, (n + 1) * 512)
                        pe.matmul(to, PPT[:, b, :], Y_HI[:, cols], start=True, stop=False)
                        pe.matmul(to, PPT[:, b, :], Y_LO[:, cols], start=False, stop=True).then_inc(M("back_ps"), 1)

                def pair(q, v, first=False):
                    for a in range(2):
                        pe.wait_ge(M(f"in_{3 * v + a}"), landed(q, v))
                    pe.wait_ge(M("x_sb"), q * 2 + 2)
                    if not first:
                        pe.wait_ge(M("hidden"), q)
                    for k in range(KC):
                        for e in range(2):
                            mm = pe.matmul(psum[64 * e:64 * e + 64, 2, :], XT[:, k, 64 * e:64 * e + 64], RG[:, 3 * v:3 * v + 2, e, k, :],
                                           start=(k == 0), stop=(k == KC - 1))
                    mm.then_inc(M("gate_up"), 1)
                    gather(q + 1, 1 - v)
                    pe.wait_ge(M("hidden"), q + 1)
                    if not first:
                        pe.wait_ge(M("hidden_t"), q)
                    for k in range(2):
                        t = pe.transpose(psum[:, 3, k * P:(k + 1) * P], HID[v][:, k:256:2], ident[:, :])
                    t.then_inc(M("hidden_ps"), 1)
                    if not first:
                        combine(q - 1)
                    turn_rows(q + 1)
                    weights_back(q, v, first)
                    pe.wait_ge(M("hidden_t"), q + 1)
                    pe.wait_ge(M(f"in_{3 * v + 2}"), landed(q, v))
                    for n in range(2):
                        for k in range(2):
                            for e in range(2):
                                mm = pe.matmul(psum[64 * e:64 * e + 64, 4 + n, :], HTS[v][:, k, 64 * e:64 * e + 64],
                                               RD[:, 3 * v + 2, e, k, n * 512:(n + 1) * 512], start=(k == 0), stop=(k == 1))
                        mm.then_inc(M("down"), 1)

                def landed(q, v):
                    return (q - v) * 8 + 16

                pe.wait_ge(S("h_split"), l + 1)
                gather(0, 0, first=True)
                turn_rows(0)
                pair(0, 0, first=True)
                pair(1, 1)
                R = rounds_of(pe, l)
                with pe.Fori(1, R * (PAIRS // 2)) as i:
                    for v in range(2):
                        pair(i * 2 + v, v)
                combine(R * PAIRS - 1)

            experts(0)

            for b in range(NB):
                turn(b, "h_ready", NB * 2 + b + 1)
            pe.wait_ge(S("ht_ready"), 6 * (TURNS.index(2) + 1))
            for i, n in enumerate((2, 0, 1)):
                w = chunk("odd_in", n)
                for b in range(NB):
                    if 3 * i + b == 8:
                        pe.wait_ge(S("qkv_ready"), 1)
                    project((6 + 3 * i + b) % 8, b, w).then_inc(S("odd_in_ps"), 1)
            pe.wait_ge(S("odd_small"), 16 * 5)
            pe.wait_ge(S("qkv_ready"), 9)
            for g in range(KV_HEADS):
                t = pe.transpose(psum[:, 7, g * P:(g + 1) * P], CK[:, g * P:(g + 1) * P], ident[:, :])
            t.then_inc(S("sides_turned"), 1)
            pe.wait_ge(S("k_t_ready"), 1)
            for i in range(FRONT + len(MOD_EVEN), len(MODS)):
                mod_products(i)
                mod_sum(i)
            for b in range(NB):
                pe.wait_ge(S("qk_normed"), b + 1)
                base = 3 * (b % 2)
                if b == 2:
                    pe.wait_ge(S("q_t_ready"), 2)
                    pe.wait_ge(S("k_t_ready"), 2)
                for half in range(2):
                    for hh in range(4):
                        h = 4 * half + hh
                        t = pe.transpose(psum[:, base + half, hh * P:(hh + 1) * P], QKV[:, b, h * P:(h + 1) * P], ident[:, :])
                    t.then_inc(S("q_turned"), 1)
                for g in range(KV_HEADS):
                    t = pe.transpose(psum[:, base + 2, g * P:(g + 1) * P], QKV[:, b, D + g * P:D + (g + 1) * P], ident[:, :])
                t.then_inc(S("k_turned"), 1)

            def att_scores(i):
                b, g = divmod(i, 2)
                pe.wait_ge(S("exps_ready"), i)
                if i == 0:
                    pe.wait_ge(S("q_t_ready"), 6)
                    pe.wait_ge(S("k_t_ready"), 4)
                keys = KT[:, g, 0:1, :] if b == 0 else KT[:, g, 1:4, :]
                for hh in range(4):
                    mm = pe.matmul(psum[:, hh, 0:keys.shape[1] * P], QT[:, 4 * g + hh, b * P:(b + 1) * P], keys, start=True, stop=True)
                mm.then_inc(S("att_scores_ps"), 1)

            att_scores(0)
            for i in range(6):
                b, g = divmod(i, 2)
                blocks = 1 if b == 0 else 3
                if i < 5:
                    att_scores(i + 1)
                pe.wait_ge(S("probs_ready"), i + 1)
                if i >= 1:
                    pe.wait_ge(S("probs_t_ready"), i)
                for kb in range(blocks):
                    for hh in range(4):
                        t = pe.transpose(psum[:, 4 + kb, hh * P:(hh + 1) * P], PR[i % 2][:, hh, kb * P:(kb + 1) * P], ident[:, :])
                t.then_inc(S("probs_turned"), 1)
                pe.wait_ge(S("probs_t_ready"), i + 1)
                if i >= 1:
                    pe.wait_ge(S("att_out_ready"), i)
                for kb in range(blocks):
                    if b == 0:
                        vals = QKV[:, 0, 1280 + g * P:1280 + (g + 1) * P]
                    else:
                        vals = CV[:, g * P:(g + 1) * P] if kb == 0 else QKV[:, kb, 1280 + g * P:1280 + (g + 1) * P]
                    mm = pe.matmul(bank(7), vals, PT[:, kb, :], start=(kb == 0), stop=(kb == blocks - 1))
                mm.then_inc(S("probs_t_used"), 1)
            pe.wait_ge(S("att_out_ready"), 6)
            for n in range(2):
                w = chunk("odd_out", n)
                for b in range(NB):
                    project(3 * n + b, b, w).then_inc(S("odd_out_ps"), 1)

            experts(1)

        def att_out(act, i):
            b, g = divmod(i, 2)
            act.wait_ge(S("probs_t_used"), i + 1)
            act.copy(OT[:, 4 * g:4 * g + 4, b * P:(b + 1) * P], bank(7).rearrange("p (h t) -> p h t", h=4)).then_inc(S("att_out_ready"), 1)

        @block.scalar
        def _(act):
            def norm(u):
                norm_squares(u)
                inverse_root(f"norm_{u}", ms, rs)

            def norm_squares(u):
                if u == 0:
                    act.wait_ge(S("x_loaded"), 32)
                for b in range(NB):
                    if u > 0:
                        act.wait_ge(S("x_updated"), NB * (u - 1) + b + 1)
                    a = act.activation(H[:, b, :], X[:, b, :], ACT.Square, accum_out=ss[:, b:b + 1])
                a.then_inc(S("squares"), 1)

            def inverse_root(tag, v, y):
                n = ROOTS.index(tag) + 1
                act.wait_ge(S("mean_squares"), n)
                act.activation(y, v, ACT.Ln).then_inc(S("root_log"), 1)
                act.wait_ge(S("root_log"), n)
                act.activation(y, y, ACT.Exp, scale=-0.5).then_inc(S("root_guess"), 1)

            def ht_copies(u):
                for b in range(NB):
                    act.wait_ge(S("turned"), 6 * TURNS.index(u) + 2 * b + 1)
                    act.copy(HT[:, 0:4, b * P:(b + 1) * P], bank(2 * b).rearrange("p (k t) -> p k t", k=4)).then_inc(S("ht_ready"), 1)

            act.wait_ge(S("cond_in"), 32)
            act.wait_ge(S("cond_zero"), 1)
            act.activation(cond_silu[:, :, 0:2], cond, ACT.Silu).then_inc(S("cond_ready"), 1)
            for i in range(FRONT):
                act.wait_ge(S("mod_part_ps"), i + 1)
                if i >= 2:
                    act.wait_ge(S("mod_sum_ps"), i - 1)
                act.copy(mod_part[i % 2], bank(i % 2)).then_inc(S("mod_part_sb"), 1)
                if 2 <= i < 6:
                    part, half = divmod(i - 2, 2)
                    for s in range(2):
                        act.wait_ge(S("spread_ps"), 2 * (i - 2) + s + 1)
                        act.copy(GS[:, part, s, half * COLS:(half + 1) * COLS], bank(6 + s)).then_inc(S("spread_sb"), 1)
                if i == 6:
                    norm_squares(0)
                if i == 8:
                    inverse_root("norm_0", ms, rs)

            ht_copies(0)
            act.wait_ge(S("front_stored"), 16 * (FRONT - 4))
            for c in range(2):
                act.wait_ge(S("qk_ps"), c + 1)
                act.mul(QK[:, c, :], psum[:, c, 0:T], GLA_DK ** -0.5).then_inc(S("qk_ready"), 1)
            act.wait_ge(S("decay_in_ps"), 1)
            act.copy(AT, psum[0:32, 4, 0:T]).then_inc(S("decay_in_ready"), 1)

            def evacuate(name, dst, b):
                act.wait_ge(S(f"{name}_ps"), b + 1)
                act.copy(dst[:, b, :], bank(5 + b)).then_inc(S(f"{name}_ready"), 1)

            evacuate("v", V, 0)
            act.wait_ge(S("z_abs"), 1)
            act.activation(EZ, EZ, ACT.Exp, scale=-1.0).then_inc(S("z_logs"), 1)
            act.wait_ge(S("z_logs"), 1)
            act.activation(EZ, EZ, ACT.Ln, bias=1.0).then_inc(S("z_logs"), 1)
            evacuate("v", V, 1)
            evacuate("v", V, 2)
            act.wait_ge(S("masks_ready"), 1)

            def mod_copies(i, part_bank, sum_bank, which=("part", "sum")):
                if "part" in which:
                    act.wait_ge(S("mod_part_ps"), i + 1)
                    act.copy(rest_buffers(i)[0], bank(part_bank)).then_inc(S("mod_part_sb"), 1)
                if "sum" in which:
                    act.wait_ge(S("mod_sum_ps"), i + 1)
                    act.copy(rest_buffers(i)[1], psum[0:2, sum_bank, :]).then_inc(S("rest_row_ready"), 1)

            def level_exp(n):
                act.wait_ge(S("decays_ready"), n)
                act.activation(EX[(n - 1) % 2], EX[(n - 1) % 2], ACT.Exp, scale=1.0 / GLA_TAU).then_inc(S("decays_exp"), 1)

            def in_plan(steps, mod):
                for step in steps:
                    if step in ("part", "sum"):
                        mod_copies(mod, 4, 4, step)
                        mod += step == "sum"
                    elif isinstance(step, int):
                        if step < 7:
                            level_exp(step + 1)
                    else:
                        evacuate(step[:-1], {"g": SG, "vg": VG, "u": U}[step[:-1]], int(step[-1]))
                return mod

            before_levels = EVEN_PLAN.index(0)
            mod = in_plan(EVEN_PLAN[:before_levels], FRONT)
            act.wait_ge(S("sums_ready"), 1)
            act.activation(E2[:, 0], BF[:, :, P:T], ACT.Exp, scale=1.0 / GLA_TAU)
            act.activation(E2[:, 1], BB[:, :, P:T], ACT.Exp, scale=1.0 / GLA_TAU)
            act.activation(E2[:, 2:4], E2[:, 2:4], ACT.Exp, scale=1.0 / GLA_TAU)
            act.activation(dec_f.rearrange("p (c o) -> p c o", o=1), BF[:, :, 2 * P - 1:2 * P], ACT.Exp, scale=1.0 / GLA_TAU)
            act.activation(dec_b.rearrange("p (c o) -> p c o", o=1), BB[:, :, 2 * P:2 * P + 1], ACT.Exp, scale=1.0 / GLA_TAU).then_inc(S("to_end_exp"), 1)
            in_plan(EVEN_PLAN[before_levels:], mod)
            act.wait_ge(S("sides_turned"), 2)
            act.copy(KDT.rearrange("p i t -> p (i t)"), psum[:, 4:6, :].rearrange("p b n -> p (b n)")).then_inc(S("kdt_ready"), 1)
            act.wait_ge(S("vg_ready"), 3)
            act.wait_ge(S("u_ready"), 3)
            act.activation(VG, VG, ACT.Gelu_apprx_tanh).then_inc(S("activated"), 1)
            act.activation(U, U, ACT.Gelu_apprx_tanh).then_inc(S("activated"), 1)
            act.wait_ge(S("g_ready"), 3)
            act.activation(SG, SG, ACT.Silu).then_inc(S("activated"), 1)
            act.wait_ge(S("gla_out"), 3)
            act.copy(O.rearrange("p b n -> p (b n)"), psum[:, 0:3, :].rearrange("p b n -> p (b n)")).then_inc(S("o_ready"), 1)
            inverse_root("ln", ln_v, ln_rs)
            inverse_root("gla", gla_ms, gla_rs)
            ht_copies("cat")

            def experts(l):
                u = 2 * l + 1

                def M(name):
                    return S(f"moe{l}_{name}")

                norm(u)
                ht_copies(u)
                act.wait_ge(S("logits_ps"), l + 1)
                act.wait_ge(S("router_in"), 16 * 4 * (l + 1))
                act.activation(LT, psum[0:36, 6, 0:T], ACT.Identity, bias=BR).then_inc(S("logits_t"), 1)
                act.wait_ge(S("router_sub"), l + 1)
                act.activation(g_tmp, g_tmp, ACT.Exp)
                act.activation(top_f[:, :, 0:1], top_f[:, :, 1:2], ACT.Exp).then_inc(S("router_exp"), 1)

                def rows_copies(q, first=False):
                    for half in range(2):
                        act.wait_ge(M("xs_ps"), q * 2 + half + 1)
                        if not first and half == 0:
                            act.wait_ge(M("x_ps"), q * 2)
                        act.copy(XS[:, half * 512:(half + 1) * 512], bank(half)).then_inc(M("xs_sb"), 1)

                def x_copies(q, first=False):
                    for half in range(2):
                        act.wait_ge(M("x_ps"), q * 2 + half + 1)
                        if not first and half == 0:
                            act.wait_ge(M("gate_up"), q)
                        act.copy(XT[:, 4 * half:4 * half + 4, :], bank(half).rearrange("p (k s) -> p k s", k=4)).then_inc(M("x_sb"), 1)

                def weights_copy(q, first=False):
                    act.wait_ge(M("weights_ps"), q + 1)
                    if not first:
                        act.wait_ge(M("slots_t"), q)
                    act.activation(PWT, psum[:, 7, 0:T].rearrange("p (b t) -> p b t", b=NB), ACT.Copy, accum_out=w_slot).then_inc(M("weights_sb"), 1)

                def pair(q, v, first=False, second=False):
                    act.wait_ge(M("gate_up"), q + 1)
                    if not first and not second:
                        act.wait_ge(M("hidden"), q - 1)
                    act.activation(SGM[v], psum[:, 2, 0:256], ACT.Silu).then_inc(M("gated"), 1)
                    rows_copies(q + 1)
                    x_copies(q + 1)
                    weights_copy(q, first)
                    act.wait_ge(M("weights_sb"), q + 1)
                    for n in range(2):
                        act.wait_ge(M("down"), q * 2 + n + 1)
                        if not first and n == 0:
                            act.wait_ge(M("back_ps"), q * 6)
                        act.activation(Y[:, n * 512:(n + 1) * 512], bank(4 + n), ACT.Copy, scale=w_slot).then_inc(M("y_sb"), 1)

                rows_copies(0, first=True)
                x_copies(0, first=True)
                pair(0, 0, first=True)
                pair(1, 1, second=True)
                R = rounds_of(act, l)
                with act.Fori(1, R * (PAIRS // 2)) as i:
                    for v in range(2):
                        pair(i * 2 + v, v)

            experts(0)

            norm(2)
            ht_copies(2)
            for i in range(9):
                c, b = divmod(i, 3)
                n = (2, 0, 1)[c]
                act.wait_ge(S("odd_in_ps"), i + 1)
                act.copy(QKV[:, b, n * 512:(n + 1) * 512], bank((6 + i) % 8)).then_inc(S("qkv_ready"), 1)
            for i in range(FRONT + len(MOD_EVEN), len(MODS)):
                if i == len(MODS) - 4:
                    inverse_root("qk", q_ms, q_rs)
                mod_copies(i, 6, 7)
            for b in range(NB):
                for half in range(2):
                    act.wait_ge(S("q_turned"), 2 * b + half + 1)
                    act.copy(QT[:, 4 * half:4 * half + 4, b * P:(b + 1) * P],
                             bank(3 * (b % 2) + half).rearrange("p (h t) -> p h t", h=4)).then_inc(S("q_t_ready"), 1)
            for i in range(6):
                n = P if i < 2 else 3 * P
                act.wait_ge(S("max_ready"), i + 1)
                if i >= 2:
                    act.wait_ge(S("probs_turned"), i - 1)
                for hh in range(4):
                    a = act.activation(PR[i % 2][:, hh, 0:n], psum[:, hh, 0:n], ACT.Exp, bias=att_max[:, i, hh:hh + 1],
                                       scale=HD ** -0.5, accum_out=att_sum[:, i, hh:hh + 1])
                a.then_inc(S("exps_ready"), 1)
                if i >= 1:
                    att_out(act, i - 1)
            att_out(act, 5)
            experts(1)
            norm(4)

        @block.vector
        def _(dve):
            links = [0]

            def link(ins):
                links[0] += 1
                ins.then_inc(S("dve_links"), 1)
                dve.wait_ge(S("dve_links"), links[0])

            def inverse_root(tag, v, y, t):
                dve.wait_ge(S("root_guess"), ROOTS.index(tag) + 1)
                link(dve.tensor_tensor(t, y, y, ALU.mult))
                link(dve.tensor_tensor(t, t, v, ALU.mult))
                link(dve.tensor_scalar(t, t, -0.5, 1.5, ALU.mult, ALU.add))
                link(dve.tensor_tensor(y, y, t, ALU.mult))

            def norm(u):
                norm_means(u)
                norm_apply(u)

            def norm_means(u):
                dve.wait_ge(S("squares"), u + 1)
                if u > 0:
                    dve.wait_ge(S("x_updated"), NB * u)
                dve.tensor_scalar(ms, ss, 1.0 / D, EPS, ALU.mult, ALU.add).then_inc(S("mean_squares"), 1)

            def norm_apply(u):
                inverse_root(f"norm_{u}", ms, rs, rt)
                if u == 0:
                    dve.wait_ge(S("spread_sb"), 8)
                else:
                    dve.wait_ge(S("rows_in"), 16 * u)
                for b in range(NB):
                    s = min(b, 1)
                    gain = GS[:, 1, s, :] if u < 4 else GS[:, 0, 0, :]
                    a = dve.scalar_tensor_tensor(H[:, b, :], X[:, b, :], rs[:, b:b + 1], gain, ALU.mult, ALU.mult)
                    if u == 4:
                        a.then_inc(S("h_ready"), 1)
                        continue
                    link(a)
                    dve.tensor_tensor(H[:, b, :], H[:, b, :], GS[:, 0, s, :], ALU.add).then_inc(S("h_ready"), 1)

            def ht_copies(u):
                for b in range(NB):
                    dve.wait_ge(S("turned"), 6 * TURNS.index(u) + 2 * b + 2)
                    dve.tensor_copy(HT[:, 4:8, b * P:(b + 1) * P], bank(2 * b + 1).rearrange("p (k t) -> p k t", k=4)).then_inc(S("ht_ready"), 1)

            def update(u, ps, bank_of, buf):
                dve.wait_ge(S("gate_in"), 16 * (u + 1))
                for c in range(6):
                    n, b = divmod(c, 3)
                    cols = slice(n * 512, (n + 1) * 512)
                    dve.wait_ge(S(ps), c + 1)
                    link(dve.tensor_tensor(buf[c % 2], bank(bank_of(c)), GT[:, min(b, 1), cols], ALU.mult))
                    a = dve.tensor_tensor(X[:, b, cols], X[:, b, cols], buf[c % 2], ALU.add)
                    if n == 1:
                        a.then_inc(S("x_updated"), 1)

            dve.memset(ones[:, :], 1.0)
            dve.memset(cond_silu, 0.0).then_inc(S("cond_zero"), 1)
            dve.wait_ge(S("mod_small"), 16 * 7)
            dve.tensor_copy(pick_bias[:, :], pick[0:64, 2:2 + 2 * 32])
            dve.tensor_copy(mod_bias[:, :], bias_raw).then_inc(S("bias_ready"), 1)
            dve.wait_ge(S("bias_ready"), 1)
            dve.tensor_tensor(mod_bias[32:64, :], bias_raw[32:64, :], mod_bias[32:64, :], ALU.subtract).then_inc(S("bias_ready"), 1)
            for i in range(FRONT):
                if i == 7:
                    norm_means(0)
                dve.wait_ge(S("mod_sum_ps"), i + 1)
                sums = psum[0:2, 2 + i % 2, :]
                if scaled(i):
                    link(dve.tensor_copy(front_row[i], psum[0:2, 4 + i % 2, :]))
                    a = dve.scalar_tensor_tensor(front_row[i], sums, 1.0, front_row[i], ALU.add, ALU.mult)
                else:
                    a = dve.tensor_copy(front_row[i], sums)
                a.then_inc(S("front_row_ready"), 1)
            dve.wait_ge(S("masks_in"), 16)
            dve.tensor_copy(masks[:, :], MASKS_F32).then_inc(S("masks_ready"), 1)

            dve.wait_ge(S("sides_turned"), 1)
            dve.tensor_copy(WST.rearrange("p g t -> p (g t)"), bank(7)).then_inc(S("spatial_ready"), 1)
            norm_apply(0)
            ht_copies(0)
            dve.wait_ge(S("front_stored"), 16 * (FRONT - 4))
            for c in (2, 3):
                dve.wait_ge(S("qk_ps"), c + 1)
                dve.tensor_copy(QK[:, c, :], psum[:, c, 0:T]).then_inc(S("qk_ready"), 1)
            for j in range(4):
                dve.wait_ge(S("decay_ps"), j + 1)
                dve.tensor_scalar(Z[:, j, :], psum[:, j, 0:T], b_gate[:, j:j + 1], None, ALU.add).then_inc(S("z_ready"), 1)
            dve.wait_ge(S("z_ready"), 4)
            dve.scalar_tensor_tensor(EZ, Z, -1.0, Z, ALU.mult, ALU.max).then_inc(S("z_abs"), 1)
            dve.wait_ge(S("z_logs"), 2)
            link(dve.scalar_tensor_tensor(Z, Z, 0.0, EZ, ALU.min, ALU.subtract))
            for c in range(2):
                for b in range(NB):
                    blk = slice(b * P, (b + 1) * P)
                    dve.tensor_tensor_scan(BF[:, c, blk], ones[:, :], Z[:, c, blk], 0.0, ALU.mult, ALU.add)
                    a = dve.tensor_tensor_scan(BB[:, c, blk][:, ::-1], ones[:, :], Z[:, 2 + c, blk][:, ::-1], 0.0, ALU.mult, ALU.add)
            link(a)

            def blocks(v):
                return v.rearrange("p c (b t) -> p c b t", t=P)

            to_f = blocks(E2[:, 2])
            to_b = blocks(E2[:, 3])
            dve.tensor_tensor(to_f, blocks(BF)[:, :, 0:2, P - 1:P].broadcast_to([P, 2, 2, P]), blocks(BF)[:, :, 0:2, :], ALU.subtract)
            dve.tensor_tensor(to_b, blocks(BB)[:, :, 0:3:2, 0:1].broadcast_to([P, 2, 2, P]), blocks(BB)[:, :, 0:3:2, :], ALU.subtract).then_inc(S("sums_ready"), 1)

            def level_decays(n):
                m = LEVELS[n - 1]
                if n >= 3:
                    dve.wait_ge(S("scores_ps"), n - 1)

                def halves(v):
                    return v.rearrange("p c (a h m) -> p c a h m", h=2, m=m)

                ex, f, g = halves(EX[(n - 1) % 2]), halves(BF), halves(BB)
                shape = [P, 2, T // (2 * m), m]
                border_f = f[:, :, :, 0, m - 1:m].broadcast_to(shape)
                border_b = g[:, :, :, 1, 0:1].broadcast_to(shape)
                dve.tensor_tensor(ex[:, 0:2, :, 1, :], f[:, :, :, 1, :], border_f, ALU.subtract)
                dve.tensor_tensor(ex[:, 0:2, :, 0, :], g[:, :, :, 0, :], border_b, ALU.subtract)
                dve.tensor_tensor(ex[:, 2:4, :, 0, :], border_f, f[:, :, :, 0, :], ALU.subtract)
                dve.tensor_tensor(ex[:, 2:4, :, 1, :], border_b, g[:, :, :, 1, :], ALU.subtract).then_inc(S("decays_ready"), 1)

            def scores_of(r):
                return psum[:, 2 * r:2 * r + 2, :].rearrange("p b n -> p (b n)")[:, 0:6 * P].rearrange("p (i t) -> p i t", i=6)

            def merge(n):
                dve.wait_ge(S("scores_ps"), n + 1)
                if n >= 1:
                    dve.wait_ge(S("att_merged"), 2 * n)
                for r in range(2):
                    att = ATT[:, 6 * r:6 * r + 6, :]
                    if n == 0:
                        eye = ident[:, :].rearrange("p (o t) -> p o t", o=1).broadcast_to([P, 6, P])
                        a = dve.scalar_tensor_tensor(att, scores_of(r), 2.0, eye, ALU.mult, ALU.mult)
                    else:
                        mask = masks[:, (n - 1) * P:n * P].rearrange("p (o t) -> p o t", o=1).broadcast_to([P, 6, P])
                        a = dve.copy_predicated(att, mask, scores_of(r))
                    a.then_inc(S("att_merged"), 1)

            level_decays(1)
            dve.wait_ge(S("to_end_exp"), 1)
            for a_ in range(2):
                dve.tensor_tensor(E2[:, a_], E2[:, a_], QK[:, 0:2, P:T], ALU.mult)
            dve.tensor_tensor(to_f, to_f, blocks(QK[:, 2:4, :])[:, :, 0:2, :], ALU.mult)
            dve.tensor_tensor(to_b, to_b, blocks(QK[:, 2:4, :])[:, :, 0:3:2, :], ALU.mult).then_inc(S("to_end_ready"), 1)
            for n in range(1, 8):
                dve.wait_ge(S("decays_exp"), n)
                dve.tensor_tensor(EX[(n - 1) % 2], EX[(n - 1) % 2], QK, ALU.mult).then_inc(S("decayed_ready"), 1)
                merge(n - 1)
                if n < 7:
                    level_decays(n + 1)
            merge(7)

            dve.wait_ge(S("state_ps"), 1)
            dve.wait_ge(S("decays_exp"), 7)
            for a_ in range(2):
                a = dve.tensor_copy(ST_OUT[:, a_].rearrange("p c v -> p (c v)"), psum[:, 6 + a_, 0:256])
            a.then_inc(S("states_ready"), 1)
            dve.wait_ge(S("state_in"), 16 * 8)
            dve.wait_ge(S("pool_zeros"), 2)
            for a_ in range(2):
                for h in range(GLA_HEADS):
                    c, r = divmod(h, 2)
                    rows = slice(64 * r, 64 * r + 64)
                    dec = (dec_f, dec_b)[a_]
                    a = dve.scalar_tensor_tensor(S1[rows, a_, h, :], S0[rows, a_, h, :], dec[rows, c:c + 1],
                                                 psum[rows, 6 + a_, (2 + c) * P:(3 + c) * P], ALU.mult, ALU.add)
            a.then_inc(S("states_ready"), 1)

            dve.wait_ge(S("activated"), 1)
            for i in range(12):
                b, g = divmod(i, 4)
                a = dve.bn_stats(BN[:, i, 0:6], VG[:, b, g * P:(g + 1) * P])
            link(a)
            for i in range(12):
                a = dve.bn_aggr(BN[:, i, 6:8], BN[:, i, 0:6])
            link(a)
            dve.tensor_scalar(ln_v.rearrange("p (i o) -> p i o", o=1), BN[:, :, 7:8], EPS, None, ALU.add).then_inc(S("mean_squares"), 1)
            dve.wait_ge(S("o_ready"), 1)
            o_all = O.rearrange("p b n -> p (b n)")
            link(dve.tensor_tensor(OSQ, o_all, o_all, ALU.mult))
            link(dve.tensor_reduce(gla_ms, OSQ.rearrange("p (i v) -> p i v", v=P), AX.X, ALU.add))
            dve.tensor_scalar(gla_ms, gla_ms, 1.0 / GLA_DV, EPS, ALU.mult, ALU.add).then_inc(S("mean_squares"), 1)
            inverse_root("ln", ln_v, ln_rs, ln_rt)
            for i in range(12):
                b, g = divmod(i, 4)
                v = VG[:, b, g * P:(g + 1) * P]
                a = dve.tensor_scalar(v, v, BN[:, i, 6:7], ln_rs[:, i:i + 1], ALU.subtract, ALU.mult)
            a.then_inc(S("vg_normed"), 1)
            dve.wait_ge(S("activated"), 3)
            sg_all = SG.rearrange("p b (h v) -> p (b h) v", v=P)
            a = dve.tensor_tensor(sg_all, sg_all, GLAG.rearrange("p (o v) -> p o v", o=1).broadcast_to([P, 12, P]), ALU.mult)
            a.then_inc(S("gla_gain_ready"), 1)
            inverse_root("gla", gla_ms, gla_rs, gla_rt)
            o_heads = O.rearrange("p b (h v) -> p (b h) v", v=P)
            link(dve.tensor_tensor(o_heads, o_heads, gla_rs.rearrange("p (i o) -> p i o", o=1).broadcast_to([P, 12, P]), ALU.mult))
            dve.wait_ge(S("gla_gain_ready"), 1)
            dve.tensor_tensor(H[:, :, 0:512], O, SG, ALU.mult)
            dve.wait_ge(S("activated"), 2)
            for g in range(GROUPS):
                dve.wait_ge(S("spatial_ps"), g + 1)
                cols = slice(g * P, (g + 1) * P)
                a = dve.scalar_tensor_tensor(H[:, :, 512 + g * P:512 + (g + 1) * P], psum[:, 3 + g, 0:T].rearrange("p (b c) -> p b c", b=NB),
                                             b_spat[:, g:g + 1], U[:, :, cols], ALU.add, ALU.mult)
            a.then_inc(S("cat_ready"), 1)
            ht_copies("cat")
            update(0, "even_out_ps", lambda c: (6 + c) % 8, UPD)

            def experts(l):
                u = 2 * l + 1

                def M(name):
                    return S(f"moe{l}_{name}")

                norm(u)
                ht_copies(u)

                dve.wait_ge(S("h_ready"), NB * (u + 1))
                dve.tensor_copy(H_HI, H).then_inc(S("h_top"), 1)

                def wide(v, n):
                    return v.rearrange("p (b o) -> p b o", o=1).broadcast_to([P, NB, n])

                dve.wait_ge(S("logits_turned"), l + 1)
                link(dve.tensor_copy(LG.rearrange("p b n -> p (b n)"), psum[:, 7, 0:NB * 36]))
                link(dve.tensor_reduce(g_max, LG[:, :, 0:4], AX.X, ALU.max))
                link(dve.tensor_tensor(g_tmp, LG[:, :, 0:4], wide(g_max, 4), ALU.is_equal))
                four = iota[:, 0:4].rearrange("p (o n) -> p o n", o=1).broadcast_to([P, NB, 4])
                link(dve.scalar_tensor_tensor(e_mask[:, :, 0:4], four, -8.0, g_tmp, ALU.add, ALU.mult))
                link(dve.tensor_reduce(g_idx, e_mask[:, :, 0:4], AX.X, ALU.min))
                link(dve.tensor_scalar(g_idx, g_idx, 8.0, None, ALU.add))
                link(dve.tensor_tensor(g_tmp, LG[:, :, 0:4], wide(g_max, 4), ALU.subtract))
                e_groups = e_mask.rearrange("p b (g n) -> p b g n", g=MOE_GROUPS)
                for g in range(MOE_GROUPS):
                    link(dve.tensor_scalar(e_groups[:, :, g, :], wide(g_idx, PER_GROUP), float(g), None, ALU.is_equal))
                link(dve.tensor_scalar(e_mask, e_mask, BIG, -BIG, ALU.mult, ALU.add))
                link(dve.tensor_tensor(e_mask, e_mask, LG[:, :, 4:36], ALU.add))
                for b in range(NB):
                    link(dve.max(top_v[:, b, :], e_mask[:, b, :]))
                    link(dve.max_index(top_i[:, b, :].bitcast(U32), top_v[:, b, :], e_mask[:, b, :]))
                dve.tensor_tensor(top_f[:, :, 1:2], top_v[:, :, 1:2], top_v[:, :, 0:1], ALU.subtract).then_inc(S("router_sub"), 1)
                dve.wait_ge(S("router_exp"), l + 1)
                link(dve.tensor_reduce(g_sum, g_tmp, AX.X, ALU.add))
                link(dve.reciprocal(g_prob, g_sum))
                e1 = top_f[:, :, 0]
                link(dve.tensor_scalar(g_sum, e1, 1.0, None, ALU.add))
                link(dve.reciprocal(g_sum, g_sum))
                link(dve.tensor_tensor(gates[:, 0, :], g_sum, g_prob, ALU.mult))
                link(dve.tensor_tensor(gates[:, 1, :], gates[:, 0, :], e1, ALU.mult))
                link(dve.tensor_copy(top_f, top_i[:, :, 0:2].bitcast(U32)))
                all32 = iota32.rearrange("p (o n) -> p o n", o=1).broadcast_to([P, NB, 32])
                for j in range(2):
                    link(dve.tensor_tensor(oh[j], all32, top_f[:, :, j:j + 1].broadcast_to([P, NB, 32]), ALU.is_equal))
                dve.tensor_tensor(oh_sum, oh[0], oh[1], ALU.add).then_inc(S("chosen"), 1)
                link(dve.memset(ht_t[:, :], 0.0))
                dve.wait_ge(S("counts_ps"), l + 1)
                link(dve.tensor_copy(cnt.rearrange("p b n -> p (b n)"), psum[:, 6, 0:96]))
                for j in range(2):
                    link(dve.tensor_tensor(oh[j], oh[j], cnt, ALU.mult))
                    link(dve.tensor_reduce(pos[:, j, :], oh[j], AX.X, ALU.add))
                p6 = pos.rearrange("p j b -> p (j b)")
                link(dve.tensor_scalar(i_a, p6, float(HALF), None, ALU.is_ge))
                for k in range(2, MAX_ROUNDS):
                    link(dve.tensor_scalar(i_b, p6, float(HALF * k), None, ALU.is_ge))
                    link(dve.tensor_tensor(i_a, i_a, i_b, ALU.add))
                link(dve.scalar_tensor_tensor(p6, i_a, float(HALF * (N_EXP - 1)), p6, ALU.mult, ALU.add))
                for j in range(2):
                    link(dve.scalar_tensor_tensor(srel[:, j, :], top_f[:, :, j], float(HALF), pos[:, j, :], ALU.mult, ALU.add))
                link(dve.tensor_reduce(n_max, psum[:, 6, 96:128], AX.X, ALU.max))
                for k in range(1, MAX_ROUNDS):
                    link(dve.tensor_scalar(n_tmp[:, k - 1:k], n_max, float(HALF * k), None, ALU.is_gt))
                link(dve.tensor_reduce(n_rounds, n_tmp, AX.X, ALU.add))
                dve.tensor_copy(rounds.bitcast(U32), n_rounds).then_inc(S("rounds_ready"), 1)

                STEPS = 8

                def places(q, v, first=False, second=False):
                    if not first:
                        dve.wait_ge(M("place_steps"), q * STEPS)
                    if not first and not second:
                        dve.wait_ge(M("xs_ps"), q * 2 - 2)
                        dve.wait_ge(M("weights_ps"), q - 1)
                    for b in range(NB):
                        for j, to in ((0, PW[v]), (1, PTMP)):
                            dve.tensor_scalar(to[:, b, :], iota[:, :], srel[:, j, b:b + 1], gates[:, j, b:b + 1],
                                              ALU.is_equal, ALU.mult).then_inc(M("place_steps"), 1)
                    dve.wait_ge(M("place_steps"), q * STEPS + 6)
                    dve.tensor_tensor(PW[v], PW[v], PTMP, ALU.add).then_inc(M("place_steps"), 1)
                    dve.tensor_scalar(srel, srel, float(-P), None, ALU.add).then_inc(M("place_steps"), 1)
                    dve.wait_ge(M("place_steps"), q * STEPS + 7)
                    dve.tensor_scalar(PP[v], PW[v], 0.0, None, ALU.not_equal).then_inc(M("places_ready"), 1)

                def hidden(q, v, first=False, second=False):
                    dve.wait_ge(M("gated"), q + 1)
                    if not first and not second:
                        dve.wait_ge(M("hidden_ps"), q - 1)
                    dve.tensor_tensor(HID[v], SGM[v], psum[:, 2, 256:512], ALU.mult).then_inc(M("hidden"), 1)
                    dve.wait_ge(M("hidden_ps"), q + 1)
                    if not first and not second:
                        dve.wait_ge(M("down"), q * 2 - 2)
                    dve.tensor_copy(HTS[v].rearrange("p k s -> p (k s)"), psum[:, 3, 0:256]).then_inc(M("hidden_t"), 1)

                def add_back(q, first=False):
                    for c in range(6):
                        b, n = divmod(c, 2)
                        dve.wait_ge(M("back_ps"), q * 6 + c + 1)
                        if not first and c == 0:
                            dve.wait_ge(M("added"), q * 6)
                        acc = ACC[:, b, n * 512:(n + 1) * 512]
                        dve.tensor_tensor(acc, acc, bank((6, 7, 4, 5, 6, 7)[c]), ALU.add).then_inc(M("added"), 1)

                def split(q):
                    dve.wait_ge(M("weights_sb"), q + 1)
                    dve.tensor_scalar(PPT, PWT, 0.0, None, ALU.not_equal).then_inc(M("slots_t"), 1)
                    dve.wait_ge(M("y_sb"), q * 2 + 2)
                    dve.tensor_copy(Y_HI, Y).then_inc(M("y_split"), 1)
                    dve.wait_ge(M("y_split"), q * 2 + 1)
                    dve.tensor_tensor(Y_LO, Y, Y_HI, ALU.subtract).then_inc(M("y_split"), 1)

                def pair(q, v, first=False, second=False):
                    places(q + 1, 1 - v, second=first)
                    hidden(q, v, first, second)
                    if not first:
                        add_back(q - 1, second)
                    split(q)

                places(0, 0, first=True)
                pair(0, 0, first=True)
                pair(1, 1, second=True)
                R = rounds_of(dve, l)
                with dve.Fori(1, R * (PAIRS // 2)) as i:
                    for v in range(2):
                        pair(i * 2 + v, v)
                add_back(R * PAIRS - 1)
                dve.wait_ge(M("added"), R * (PAIRS * 6))
                dve.wait_ge(M("x_sb"), R * (PAIRS * 2) + 2)
                dve.wait_ge(S("gate_in"), 16 * (u + 1))
                for b in range(NB):
                    link(dve.tensor_tensor(UPD_M[b % 2], ACC[:, b, :], GT[:, min(b, 1), :], ALU.mult))
                    dve.tensor_tensor(X[:, b, :], X[:, b, :], UPD_M[b % 2], ALU.add).then_inc(S("x_updated"), 1)

            experts(0)

            norm(2)
            ht_copies(2)
            dve.wait_ge(S("qkv_ready"), 9)
            dve.wait_ge(S("odd_small"), 16 * 5)
            dve.wait_ge(S("sides_turned"), 3)
            dve.tensor_copy(KT[:, :, 1, :], psum[:, 7, 0:256].rearrange("p (g t) -> p g t", g=2)).then_inc(S("k_t_ready"), 1)
            sq = SQ_QK
            for b in range(NB):
                heads = QKV[:, b, 0:1280].rearrange("p (h n) -> p h n", h=10)
                link(dve.tensor_tensor(sq, heads, heads, ALU.mult))
                link(dve.tensor_reduce(q_ms[:, 10 * b:10 * b + 10], sq, AX.X, ALU.add))
            dve.tensor_scalar(q_ms, q_ms, 1.0 / HD, EPS, ALU.mult, ALU.add).then_inc(S("mean_squares"), 1)
            inverse_root("qk", q_ms, q_rs, q_rt)
            for b in range(NB):
                heads = QKV[:, b, 0:1280].rearrange("p (h n) -> p h n", h=10)
                inv = q_rs[:, 10 * b:10 * b + 10].rearrange("p (h o) -> p h o", o=1).broadcast_to([P, 10, HD])
                link(dve.tensor_tensor(heads, heads, inv, ALU.mult))
                dve.tensor_tensor(heads[:, 0:8, :], heads[:, 0:8, :], GQ.rearrange("p (o n) -> p o n", o=1).broadcast_to([P, 8, HD]), ALU.mult)
                a = dve.tensor_tensor(heads[:, 8:10, :], heads[:, 8:10, :], GK.rearrange("p (o n) -> p o n", o=1).broadcast_to([P, 2, HD]), ALU.mult)
                if b == 0:
                    a.then_inc(S("qk_normed"), 1)
                    continue
                link(a)
                x1, x2 = heads[:, :, 0:HD:2], heads[:, :, 1:HD:2]
                cos, sin = (ROPE[:, b - 1, i, :].rearrange("p (o n) -> p o n", o=1).broadcast_to([P, 10, 64]) for i in range(2))
                dve.tensor_tensor(RT1, x1, cos, ALU.mult)
                dve.tensor_tensor(RT2, x2, sin, ALU.mult)
                dve.tensor_tensor(RT3, x1, sin, ALU.mult)
                link(dve.tensor_tensor(RT4, x2, cos, ALU.mult))
                dve.tensor_tensor(x1, RT1, RT2, ALU.subtract)
                dve.tensor_tensor(x2, RT3, RT4, ALU.add).then_inc(S("qk_normed"), 1)
                if b == 1:
                    dve.wait_ge(S("qk_normed"), 2)
            for b in range(NB):
                dve.wait_ge(S("k_turned"), b + 1)
                dst = KT[:, :, 0 if b == 0 else b + 1, :]
                dve.tensor_copy(dst, psum[:, 3 * (b % 2) + 2, 0:256].rearrange("p (g t) -> p g t", g=2)).then_inc(S("k_t_ready"), 1)
            def score_max(i):
                dve.wait_ge(S("att_scores_ps"), i + 1)
                link(dve.tensor_reduce(att_max[:, i, :], psum[:, 0:4, 0:P if i < 2 else 3 * P], AX.X, ALU.max))
                dve.tensor_scalar(att_max[:, i, :], att_max[:, i, :], -HD ** -0.5, None, ALU.mult).then_inc(S("max_ready"), 1)

            score_max(0)
            for i in range(6):
                n = P if i < 2 else 3 * P
                blocks_ = n // P
                dve.wait_ge(S("exps_ready"), i + 1)
                link(dve.reciprocal(att_sum[:, i, :], att_sum[:, i, :]))
                pr = PR[i % 2][:, :, 0:n]
                inv = att_sum[:, i, :].rearrange("p (h o) -> p h o", o=1).broadcast_to([P, 4, n])
                dve.tensor_tensor(pr, pr, inv, ALU.mult).then_inc(S("probs_ready"), 1)
                if i < 5:
                    score_max(i + 1)
                dve.wait_ge(S("probs_turned"), i + 1)
                if i >= 1:
                    dve.wait_ge(S("probs_t_used"), i)
                dve.tensor_copy(PT[:, 0:blocks_, :], psum[:, 4:4 + blocks_, :]).then_inc(S("probs_t_ready"), 1)
            update(2, "odd_out_ps", lambda c: c, UPD_O)
            experts(1)
            norm(4)


_INS = ["x_prompt", "x_sample", "state_gla", "cache_k", "cache_v", "c", "c_ctx", "w_mod", "b_mod", "norm1_g", "norm2_g",
        "w_in_even", "w_gate_up", "b_gate_up", "gla_norm_g", "w_spatial", "b_spatial", "w_out_even", "w_in_odd", "q_norm_g",
        "k_norm_g", "w_out_odd", "w_router_group", "b_router_group", "w_router_expert", "b_router_expert", "w_exp_gate",
        "w_exp_up", "w_exp_down", "final_norm_g"]
_OUTS = {"y_prompt": (1, 128, 1024), "y_sample": (1, 256, 1024), "new_state_gla": (1, 1, 2, 4, 64, 128),
         "new_cache_k": (1, 1, 128, 2, 128), "new_cache_v": (1, 1, 128, 2, 128)}


def kernel(**inputs):
    import concourse.bacc as _bacc
    from concourse.bass_utils import run_bass_kernel_spmd as _run

    nc = _bacc.Bacc("TRN2", target_bir_lowering=False, num_devices=1)
    arrays = {f"in_{n}": np.ascontiguousarray(inputs[n]) for n in _INS}
    arrays.update({f"in_{n}": a for n, a in shape_constants().items()})
    d = {n[3:]: nc.dram_tensor(n, a.shape, mybir.dt.from_np(a.dtype), kind="ExternalInput").ap() for n, a in arrays.items()}
    outs = {n: nc.dram_tensor(f"out_{n}", s, F32, kind="ExternalOutput").ap() for n, s in _OUTS.items()}
    build(nc, d, outs)
    r = _run(nc, [arrays], core_ids=[0])
    return tuple(r.results[0][f"out_{n}"] for n in _OUTS)
```

```python
from contextlib import ExitStack

import numpy as np

import concourse.bass as bass
from concourse import mybir

P = 128
D = 1024
KC = D // P
NB = 3
T = NB * P
EPS = 1e-6
COLS = 512
RING = 6
GLA_HEADS, GLA_DK, GLA_DV, GLA_RANK = 4, 64, 128, 16
GLA_TAU = 16.0
QK_W = GLA_HEADS * GLA_DK
V_W = GLA_HEADS * GLA_DV
GROUPS = 4
ATT_HEADS, KV_HEADS, HD = 8, 2, 128
N_EXP, PER_GROUP, MOE_GROUPS = 32, 8, 4
F_EXP = D // 4
PAIRS = N_EXP // 2
HALF = 64
MAX_ROUNDS = T // HALF
GRID_W = 64
BIG = 1e30

ALU = mybir.AluOpType
ACT = mybir.ActivationFunctionType
AX = mybir.AxisListType
F32 = mybir.dt.float32
U32 = mybir.dt.uint32
U8 = mybir.dt.uint8
F32R = mybir.dt.float32r
LEVELS = [64, 32, 16, 8, 4, 2, 1]


def shape_constants():
    i = np.arange(P)
    masks = np.zeros((P, len(LEVELS), P), np.float32)
    for n, m in enumerate(LEVELS):
        same = (i[:, None] // (2 * m)) == (i[None, :] // (2 * m))
        other = (i[:, None] // m) != (i[None, :] // m)
        masks[:, n, :] = same & other
    pick = np.zeros((P, 2 + 2 * 32), np.float32)
    for j in range(4):
        for s in range(2):
            pick[32 * j + s, s] = 1.0
    for r in range(32):
        pick[[r, 32 + r], 2 + 2 * r:4 + 2 * r] = 1.0
    n_freq = HD // 4
    t = np.arange(2 * P)
    inv = (10000.0 ** (-np.arange(n_freq, dtype=np.float32) / n_freq)).astype(np.float32)
    row = (t // GRID_W).astype(np.float32)[:, None] * inv
    col = (t % GRID_W).astype(np.float32)[:, None] * inv
    ang = np.concatenate([row, col], axis=-1)
    rope = np.stack([np.cos(ang), np.sin(ang)], axis=1).astype(np.float32)
    rope = np.ascontiguousarray(rope.reshape(2, P, 2, HD // 2).transpose(1, 0, 2, 3))
    return {
        "k_ident": np.eye(P, dtype=np.float32),
        "k_before": (i[:, None] < i[None, :]).astype(np.float32),
        "k_iota": np.broadcast_to(i.astype(np.float32), (P, P)).copy(),
        "k_masks": masks,
        "k_pick": pick,
        "k_rope": rope,
    }


MOD_GROUPS = {
    "front": [(0, 0), (0, 1), (0, 2), (0, 3), (0, 8), (0, 9), (1, 2), (1, 3), (1, 8), (1, 9)],
    "even": [(0, 4), (0, 5)],
    "gate": [(0, 6), (0, 7)],
    "norm_1": [(0, 10), (0, 11)],
    "router": [(1, 0), (1, 1)],
    "norm_2": [(1, 4), (1, 5), (1, 6)],
    "attention": [(1, 7)],
    "norm_3": [(1, 10), (1, 11)],
}
MODS = [m for group in MOD_GROUPS.values() for m in group]
FRONT = len(MOD_GROUPS["front"])
MOD_BANKS = {"even": (4, 4), "gate": (7, 7), "norm_1": (4, 5), "router": (4, 5), "norm_2": (2, 3), "attention": (6, 7), "norm_3": (6, 7)}
EVEN_PLAN = ["part", "g0", "sum", "part", "g1", "sum", 0, "g2", 1, "vg0", 2, "vg1", 3, "vg2", 4, "u0", 5, "u1", 6, "u2", 7]


def mods(group):
    start = 0
    for name, chunks in MOD_GROUPS.items():
        if name == group:
            return range(start, start + len(chunks))
        start += len(chunks)


def group_of(i):
    return next(name for name in MOD_GROUPS if i in mods(name))


def weight_chunks():
    def of(group):
        return [("mod", i) for i in mods(group)]

    first = of("front") + [("even_in", 0), ("even_in", 1)]
    even = iter(of("even"))
    for step in EVEN_PLAN:
        if step == "part":
            first.append(next(even))
        elif step in ("g0", "vg0", "u0"):
            first.append(("even_in", {"g0": 2, "vg0": 3, "u0": 4}[step]))
    first += of("gate") + [("even_out", n) for n in range(2)] + of("norm_1") + of("router")
    second = of("norm_2") + [("odd_in", n) for n in range(3)] + of("attention") + [("odd_out", n) for n in range(2)] + of("norm_3")
    return first, second


FIRST, SECOND = weight_chunks()
CHUNKS = FIRST + SECOND
ROOTS = ["norm_0", "ln", "gla", "norm_1", "norm_2", "qk_0", "qk_1", "qk_2", "norm_3", "norm_4"]
TURNS = [0, "cat", 1, 2, 3]
EVEN_COLS = [0, 2 * QK_W, 2 * QK_W + V_W, 2 * QK_W + 2 * V_W + 2 * GLA_RANK + 512, 2 * QK_W + 2 * V_W + 2 * GLA_RANK]
A_COL = 2 * QK_W + 2 * V_W


def slot_of(j):
    return (j - len(FIRST)) % RING


def scaled(i):
    return MODS[i][1] // 2 in (1, 4)


def fills_of(j):
    return sum(slot_of(i) == slot_of(j) for i in range(j + 1))


def last_in(slot, upto):
    return max(j for j in range(upto) if slot_of(j) == slot)


def build(nc, d, outs):
    ctx = ExitStack()
    sems = {}

    def S(name):
        if name not in sems:
            sems[name] = ctx.enter_context(nc.semaphore(name))
        return sems[name]

    address = {}

    def sb(name, cols, dt=F32, parts=P):
        address[name] = (nc.sbuf_base + 31) // 32 * 32
        return ctx.enter_context(nc.sbuf_tensor(name, [parts, cols], dt))

    with ctx:
        ring = sb("ring", RING * 4096)
        x_t = sb("x", NB * D)
        h_t = sb("h", NB * D)
        ht_t = sb("ht", KC * T)
        gs_t = sb("shift_scale", 4 * D)
        gt_t = sb("gate_rows", 2 * D)
        ar = sb("arena", 11264)
        ident = sb("ident", P)
        before = sb("before", P)
        iota = sb("iota", P)
        masks = sb("masks", len(LEVELS) * P, U8)
        ones = sb("ones", P)
        pick = sb("pick", 2 + 2 * 32)
        mod_bias = sb("mod_bias", COLS, F32R, parts=64)
        pick_bias = sb("pick_bias", 2 * 32, F32R, parts=64)
        cond_t = sb("cond_silu", KC * 32)
        small = sb("small", 264)
        psum = ctx.enter_context(nc.psum_tensor("psum", [P, 8, 512], F32))
        mod_rows = nc.dram_tensor("mod_rows", (2, 6, 2, D), F32, kind="Internal").ap()

        X = x_t[:, :].rearrange("p (b n) -> p b n", b=NB)
        H = h_t[:, :].rearrange("p (b n) -> p b n", b=NB)
        HT = ht_t[:, :].rearrange("p (k t) -> p k t", k=KC)
        GS = gs_t[:, :].rearrange("p (a s n) -> p a s n", a=2, s=2)
        GT = gt_t[:, :].rearrange("p (s n) -> p s n", s=2)
        RC = ring[:, :].rearrange("p (r k n) -> p r k n", r=RING, k=KC)
        RG = ring[:, :].rearrange("p (r e k n) -> p r e k n", r=RING, e=2, k=KC)
        RD = ring[:, :].rearrange("p (r e k n) -> p r e k n", r=RING, e=2, k=2)
        RS = ring[:, :].rearrange("p (r e n) -> p r e n", r=RING, e=2)

        def bank(b):
            return psum[:, b, :]

        def rounded(name, base, col, cols):
            t = nc.alloc_sbuf_tensor_at(name, [P, cols], F32R, offset=address[base] + 4 * col)
            return t[:, :]

        class View:

            def __init__(self, base):
                self.at, self.base = 0, base

            def __call__(self, cols, pattern=None, parts=P, **sizes):
                v = self.base[0:parts, self.at:self.at + cols]
                self.at += cols
                return v.rearrange(pattern, **sizes) if pattern else v

        sm = View(small)
        ss, ms, rs, rt = sm(3), sm(3), sm(3), sm(3)
        b_gate = sm(4)
        b_spat = sm(4)
        gla_ms, gla_rs, gla_rt = sm(12), sm(12), sm(12)
        ln_rs, ln_rt, ln_v = sm(12), sm(12), sm(12)
        dec_f, dec_b = sm(2), sm(2)
        att_max, att_sum = sm(24, "p (i h) -> p i h", i=6), sm(24, "p (i h) -> p i h", i=6)
        q_ms, q_rs, q_rt = ([sm(12), sm(12), sm(6)] for _ in range(3))

        cond_silu = cond_t[:, :].rearrange("p (k m) -> p k m", m=32)
        vm = View(ar)
        mod_part = [vm(COLS) for _ in range(2)]
        front_row = [vm(COLS, parts=2) for _ in range(FRONT)]

        ve = View(ar)
        QK = ve(4 * T, "p (c t) -> p c t", c=4)
        BF = ve(2 * T, "p (c t) -> p c t", c=2)
        BB = ve(2 * T, "p (c t) -> p c t", c=2)
        ATT = ve(12 * P, "p (i t) -> p i t", i=12)
        V = ve(NB * 512, "p (b n) -> p b n", b=NB)
        SG = ve(NB * 512, "p (b n) -> p b n", b=NB)
        VG = ve(NB * 512, "p (b n) -> p b n", b=NB)
        U = ve(NB * 512, "p (b n) -> p b n", b=NB)
        WST = ve(GROUPS * P, "p (g t) -> p g t", g=GROUPS)
        bias_raw = U[0:64, 1, :]
        cond = WST.rearrange("p g t -> p (g t)")[:, 0:KC * 2].rearrange("p (k s) -> p k s", s=2)
        WA = VG[:, 0:1, 0:256].rearrange("p o (k n) -> p (o k) n", k=KC)
        WS_RAW = U[:, 0, :].rearrange("p (g s) -> p g s", g=GROUPS)
        EX = [H[:, :, :].rearrange("p b n -> p (b n)")[:, i * 1536:(i + 1) * 1536].rearrange("p (c t) -> p c t", c=4) for i in range(2)]
        MASKS_F32 = SG.rearrange("p b n -> p (b n)")[:, 0:len(LEVELS) * P]
        vz = View(gs_t)
        Z = vz(4 * T, "p (c t) -> p c t", c=4)
        EZ = vz(4 * T, "p (c t) -> p c t", c=4)
        AT = vz(T, parts=32)
        WGU = vz(512, parts=32)
        GLAG = vz(P)
        v2 = View(gs_t)
        E2 = v2(8 * 256, "p (a c t) -> p a c t", a=4, c=2)
        KDT = v2(8 * P, "p (i t) -> p i t", i=8)
        vs = View(gt_t)
        S0 = vs(1024, "p (a h v) -> p a h v", a=2, h=4)
        S1 = vs(1024, "p (a h v) -> p a h v", a=2, h=4)
        O = ATT.rearrange("p i t -> p (i t)").rearrange("p (b n) -> p b n", b=NB)
        OSQ = QK.rearrange("p c t -> p (c t)")
        ST_OUT = BF.rearrange("p c t -> p (c t)")[:, 0:512].rearrange("p (a c v) -> p a c v", a=2, c=2)
        BN = BB.rearrange("p c t -> p (c t)")[:, 0:12 * 8].rearrange("p (i n) -> p i n", i=12)
        UPD = [QK.rearrange("p c t -> p (c t)")[:, i * 512:(i + 1) * 512] for i in range(2)]

        vo = View(ar)
        QKV = vo(NB * 1536, "p (b n) -> p b n", b=NB)
        KT = vo(KV_HEADS * 4 * P, "p (g b t) -> p g b t", g=KV_HEADS, b=4)
        CK = vo(256)
        CV = vo(256)
        ROPE = vo(256, "p (b c n) -> p b c n", b=2, c=2)
        GQ, GK = vo(P), vo(P)
        PR0 = vo(1536)
        SQ_QK = vo(1536)
        ROPE_TMP = [SQ_QK[:, 0:512], SQ_QK[:, 512:1024], PR0[:, 0:512], PR0[:, 512:1024]]
        UPD_O = ROPE_TMP[0:2]
        QT = H[:, :, :].rearrange("p b n -> p (b n)").rearrange("p (h t) -> p h t", h=8)
        vg_ = View(gs_t)
        PR = [PR0.rearrange("p (h n) -> p h n", h=4), vg_(1536, "p (h n) -> p h n", h=4)]
        PT = vg_(1536, "p (k n) -> p k n", k=3)
        OT = HT

        vx = View(ar)
        XT = vx(KC * P, "p (k s) -> p k s", k=KC)
        XS = vx(D)
        Y_LO = rounded("y_low", "arena", vx.at, D)
        Y = vx(D)
        Y_HI = rounded("y_top", "arena", vx.at, D)
        vx(D)
        SGM = [vx(256) for _ in range(2)]
        HID = [vx(256) for _ in range(2)]
        HTS = [vx(256, "p (k s) -> p k s", k=2) for _ in range(2)]
        WR = vx(KC * 36, "p (k n) -> p k n", k=KC)
        BR = vx(8)[0:36, 0:1]
        PW = [vx(NB * P, "p (b s) -> p b s", b=NB) for _ in range(2)]
        PP = [rounded(f"places_{v}", "arena", vx.at + v * NB * P, NB * P).rearrange("p (b s) -> p b s", b=NB) for v in range(2)]
        vx(2 * NB * P)
        PTMP = vx(NB * P, "p (b s) -> p b s", b=NB)
        PWT = vx(NB * P, "p (b t) -> p b t", b=NB)
        PPT = rounded("slots_t", "arena", vx.at, NB * P).rearrange("p (b t) -> p b t", b=NB)
        vx(NB * P)
        w_slot = vx(1)
        LT = vx(T, parts=36)
        LG = vx(NB * 36, "p (b n) -> p b n", b=NB)
        g_max, g_idx, g_sum, g_prob = vx(3), vx(3), vx(3), vx(3)
        g_tmp = vx(12, "p (b n) -> p b n", b=NB)
        e_mask = vx(NB * 32, "p (b n) -> p b n", b=NB)
        top_v = vx(NB * 8, "p (b n) -> p b n", b=NB)
        top_i = vx(NB * 8, "p (b n) -> p b n", b=NB)
        top_f = vx(NB * 2, "p (b n) -> p b n", b=NB)
        gates = vx(6, "p (j b) -> p j b", j=2)
        oh = [vx(NB * 32, "p (b n) -> p b n", b=NB) for _ in range(2)]
        oh_sum = vx(NB * 32, "p (b n) -> p b n", b=NB)
        cnt = vx(NB * 32, "p (b n) -> p b n", b=NB)
        pos = vx(6, "p (j b) -> p j b", j=2)
        i_a, i_b, i_c = vx(6), vx(6), vx(6)
        srel = vx(6, "p (j b) -> p j b", j=2)
        n_max, n_rounds, n_tmp = vx(1), vx(1), vx(5)
        rounds = vx(1)
        H_HI = rounded("h_top", "shift_scale", 0, NB * D).rearrange("p (b n) -> p b n", b=NB)
        H_LO = rounded("h_low", "h", 0, NB * D).rearrange("p (b n) -> p b n", b=NB)
        ACC = ht_t[:, :].rearrange("p (b n) -> p b n", b=NB)
        UPD_M = [XT.rearrange("p k s -> p (k s)"), XS]
        iota32 = iota[:, 0:32]

        def col_src(j):
            name, n = CHUNKS[j]
            if name == "mod":
                l, c = MODS[n]
                return d["w_mod"][l].rearrange("(p k) n -> p k n", k=KC)[:, :, c * COLS:(c + 1) * COLS]
            if name == "even_in":
                c = EVEN_COLS[n]
                return d["w_in_even"][0].rearrange("(p k) n -> p k n", k=KC)[:, :, c:c + COLS]
            if name == "even_out":
                return d["w_out_even"][0].rearrange("(p k) n -> p k n", k=KC)[:, :, n * COLS:(n + 1) * COLS]
            if name == "odd_in":
                return d["w_in_odd"][0].rearrange("(p k) n -> p k n", k=KC)[:, :, n * COLS:(n + 1) * COLS]
            return d["w_out_odd"][0].rearrange("(k p) n -> p k n", k=KC)[:, :, n * COLS:(n + 1) * COLS]

        def rest_buffers(i):
            slot = slot_of(CHUNKS.index(("mod", i)))
            return RC[:, slot, 0, :], RC[0:2, slot, 1, :]

        def rounds_of(eng, l):
            eng.wait_ge(S("rounds_ready"), l + 1)
            return eng.value_load(rounds[0:1, 0:1].bitcast(U32), min_val=0, max_val=MAX_ROUNDS - 1) + 1

        def used_up(eng, j):
            name, n = CHUNKS[j]
            if name == "mod" and n < FRONT:
                eng.wait_ge(S("mod_part_ps"), n + 1)
            elif name == "mod":
                eng.wait_ge(S("rest_stored"), 16 * (n - FRONT + 1))
            elif name == "even_in":
                eng.wait_ge(S(("qk_ps", "v_ps", "g_ps", "vg_ps", "u_ps")[n]), (4, 3, 3, 3, 3)[n])
            elif name == "even_out":
                eng.wait_ge(S("even_out_ps"), NB * (n + 1))
            elif name == "odd_in":
                eng.wait_ge(S("odd_in_ps"), NB * (n + 1))
            else:
                eng.wait_ge(S("odd_out_ps"), NB * (n + 1))

        block = ctx.enter_context(nc.Block())

        @block.sync
        def _(sp):
            def load_chunk(j):
                sp.dma_start(RC[:, slot_of(j)], col_src(j)).then_inc(S(f"chunk_in_{slot_of(j)}"), 16)

            def load_experts(l, a, first_expert, slot):
                w = d[("w_exp_gate", "w_exp_up", "w_exp_down")[a]][l].rearrange("e (p k) n -> p e (k n)", p=P)
                sp.dma_start(RS[:, slot], w[:, bass.ds(first_expert, 2), :]).then_inc(S(f"moe{l}_in_{slot}"), 16)

            with nc.allow_non_contiguous_dma(reason="small vectors by channel"):
                sp.dma_start(cond[:, :, 0:1].rearrange("p k s -> p (k s)"), d["c_ctx"].rearrange("(p k) -> p k", k=KC)).then_inc(S("cond_in"), 16)
                sp.dma_start(cond[:, :, 1:2].rearrange("p k s -> p (k s)"), d["c"][0].rearrange("(p k) -> p k", k=KC)).then_inc(S("cond_in"), 16)
            load_chunk(0)
            sp.dma_start(pick[:, :], d["k_pick"]).then_inc(S("mod_small"), 16)
            for r in (0, 32):
                sp.dma_start(bias_raw[r:r + 24, :], d["b_mod"].rearrange("l (n c) -> (l n) c", c=COLS)).then_inc(S("mod_small"), 16)
                for part in range(2):
                    gains = d[("norm1_g", "norm2_g")[part]].rearrange("l (h c) -> (l h) c", c=COLS)
                    sp.dma_start(bias_raw[r + 24 + 4 * part:r + 28 + 4 * part, :], gains).then_inc(S("mod_small"), 16)
            for j in range(1, len(FIRST)):
                if j == 3:
                    sp.dma_start(X[:, 0, :], d["x_prompt"][0]).then_inc(S("x_loaded"), 16)
                    sp.dma_start(X[:, 1:3, :], d["x_sample"][0].rearrange("(b p) n -> p b n", p=P)).then_inc(S("x_loaded"), 16)
                if j >= RING:
                    used_up(sp, j - RING)
                load_chunk(j)

            def experts(l, before_first):
                for u in range(2):
                    for a in range(3):
                        before_first(3 * u + a)
                        load_experts(l, a, 2 * u, 3 * u + a)
                R = rounds_of(sp, l)
                with sp.Fori(1, R * (PAIRS // 2)) as i:
                    for u in range(2):
                        first_expert = sp.snap(((i * 2 + u) % PAIRS) * 2)
                        multiplied = sp.snap(i * 2 + (u - 1))
                        down_multiplied = sp.snap(i * 4 + (2 * u - 2))
                        sp.wait_ge(S(f"moe{l}_gate_up"), multiplied)
                        sp.sem_inc(S("slots_freed"), 1)
                        load_experts(l, 0, first_expert, 3 * u)
                        load_experts(l, 1, first_expert, 3 * u + 1)
                        sp.wait_ge(S(f"moe{l}_down"), down_multiplied)
                        sp.sem_inc(S("slots_freed"), 1)
                        load_experts(l, 2, first_expert, 3 * u + 2)
                return R

            R = experts(0, lambda slot: used_up(sp, last_in(slot, len(FIRST))))
            sp.wait_ge(S("moe0_gate_up"), R * PAIRS - 1)
            for j in range(2):
                load_chunk(len(FIRST) + j)
            sp.wait_ge(S("moe0_down"), R * (2 * PAIRS) - 2)
            load_chunk(len(FIRST) + 2)
            sp.wait_ge(S("moe0_gate_up"), R * PAIRS)
            for j in range(3, 5):
                load_chunk(len(FIRST) + j)
            sp.wait_ge(S("moe0_down"), R * (2 * PAIRS))
            load_chunk(len(FIRST) + 5)
            for j in range(RING, len(SECOND)):
                used_up(sp, len(FIRST) + j - RING)
                load_chunk(len(FIRST) + j)

            experts(1, lambda slot: used_up(sp, last_in(slot, len(CHUNKS))))

        @block.gpsimd
        def _(pool):
            def load(dst, src, sem="consts"):
                pool.dma_start(dst, src).then_inc(S(sem), 16)

            def load_rows(u, part, dst, sem):
                n = dst.shape[1]
                l = u // 2
                src = mod_rows[l, 3 * (u % 2) + part[0]:3 * (u % 2) + part[1]].rearrange("a s n -> (a s n)")
                pool.dma_start(dst, src.rearrange("(o n) -> o n", o=1).broadcast_to([P, n])).then_inc(S(sem), 16)

            load(ident[:, :], d["k_ident"])
            load(before[:, :], d["k_before"])
            load(iota[:, :], d["k_iota"])
            load(MASKS_F32, d["k_masks"].rearrange("p l t -> p (l t)"), "masks_in")
            def load_router(l):
                with nc.allow_non_contiguous_dma(reason="router weights"):
                    load(WR[:, :, 0:4], d["w_router_group"][l].rearrange("(p k) n -> p k n", k=KC), "router_in")
                    load(WR[:, :, 4:36], d["w_router_expert"][l].rearrange("(p k) n -> p k n", k=KC), "router_in")
                    load(BR[0:4, :], d["b_router_group"][l].rearrange("(n o) -> n o", o=1), "router_in")
                    load(BR[4:36, :], d["b_router_expert"][l].rearrange("(n o) -> n o", o=1), "router_in")

            with nc.allow_non_contiguous_dma(reason="small vectors by channel"):
                load(b_gate, d["b_gate_up"][0].rearrange("a (c p) -> p (a c)", p=P))
                load(b_spat, d["b_spatial"][0].rearrange("g t -> t g"))

            def store_mod(i, row, sem):
                l, n = MODS[i]
                part, half = divmod(n, 2)
                pool.dma_start(mod_rows[l, part, :, half * COLS:(half + 1) * COLS], row).then_inc(S(sem), 16)

            load(WA, d["w_in_even"][0].rearrange("(p k) n -> p k n", k=KC)[:, :, A_COL:A_COL + 2 * GLA_RANK], "even_small")
            load(WS_RAW, d["w_spatial"][0].rearrange("g t s -> t g s"), "even_small")
            pool.memset(S0.rearrange("p a h v -> p (a h v)"), 0.0).then_inc(S("pool_zeros"), 1)
            pool.memset(S1.rearrange("p a h v -> p (a h v)"), 0.0).then_inc(S("pool_zeros"), 1)
            pool.wait_ge(S("pool_zeros"), 2)
            for a in range(2):
                for h in range(GLA_HEADS):
                    r = 64 * (h % 2)
                    load(S0[r:r + 64, a, h, :], d["state_gla"][0, 0, a, h], "state_in")
            for i in range(4, FRONT):
                pool.wait_ge(S("front_row_ready"), i + 1)
                store_mod(i, front_row[i], "front_stored")

            pool.wait_ge(S("h_ready"), NB)
            pool.wait_ge(S("sides_turned"), 1)
            pool.memset(WGU, 0.0).then_inc(S("pool_zeros"), 1)
            pool.wait_ge(S("pool_zeros"), 3)
            for a in range(2):
                load(WGU[a * GLA_RANK:(a + 1) * GLA_RANK, a * QK_W:(a + 1) * QK_W], d["w_gate_up"][0, a], "even_small")
            load(GLAG, d["gla_norm_g"][0].rearrange("(o n) -> o n", o=1).broadcast_to([P, P]), "even_small")

            def store_rest(group):
                for i in mods(group):
                    pool.wait_ge(S("rest_row_ready"), i - FRONT + 1)
                    store_mod(i, rest_buffers(i)[1], "rest_stored")
                    pool.wait_ge(S("rest_stored"), 16 * (i - FRONT + 1))

            store_rest("even")
            pool.wait_ge(S("states_ready"), 1)
            for a in range(2):
                for hh in range(2):
                    dst = outs["new_state_gla"][0, 0, a, hh::2].rearrange("c d v -> d c v")
                    pool.dma_start(dst, ST_OUT[64 * hh:64 * hh + 64, a]).then_inc(S("stored"), 16)
            pool.wait_ge(S("gla_out"), 3)
            load_rows(0, (2, 3), gt_t[:, :], "gate_in")
            load_router(0)
            pool.wait_ge(S("gla_gain_ready"), 1)
            store_rest("gate")
            load_rows(1, (0, 2), gs_t[:, :], "rows_in")

            def experts(l):
                u = 2 * l + 1
                store_rest(f"norm_{u}")
                pool.wait_ge(S("turned"), 6 * (TURNS.index(u) + 1))
                pool.wait_ge(S("h_top"), l + 1)
                pool.tensor_tensor(H_LO, H, H_HI, ALU.subtract).then_inc(S("h_split"), 1)
                if l == 0:
                    store_rest("router")
                pool.wait_ge(S("x_updated"), NB * u)
                load_rows(u, (2, 3), gt_t[:, :], "gate_in")
                R = rounds_of(pool, l)
                pool.wait_ge(S(f"moe{l}_xs_ps"), R * (PAIRS * 2) + 2)
                pool.sem_inc(S("rows_free"), 1)

            experts(0)
            load_rows(2, (0, 2), gs_t[:, :], "rows_in")
            store_rest("norm_2")
            pool.wait_ge(S("x_updated"), NB * 2)
            load(CK, d["cache_k"][0, 0].rearrange("t g n -> t (g n)"), "odd_small")
            load(CV, d["cache_v"][0, 0].rearrange("t g n -> t (g n)"), "odd_small")
            load(ROPE, d["k_rope"], "odd_small")
            load(GQ, d["q_norm_g"][0].rearrange("(o n) -> o n", o=1).broadcast_to([P, P]), "odd_small")
            load(GK, d["k_norm_g"][0].rearrange("(o n) -> o n", o=1).broadcast_to([P, P]), "odd_small")
            store_rest("attention")
            load_rows(2, (2, 3), gt_t[:, :], "gate_in")
            pool.wait_ge(S("qk_normed"), 3)
            pool.dma_start(outs["new_cache_k"][0, 0].rearrange("t g n -> t (g n)"), QKV[:, 0, 1024:1280]).then_inc(S("stored"), 16)
            pool.dma_start(outs["new_cache_v"][0, 0].rearrange("t g n -> t (g n)"), QKV[:, 0, 1280:1536]).then_inc(S("stored"), 16)
            pool.wait_ge(S("probs_t_used"), 6)
            load_rows(3, (0, 2), gs_t[:, :], "rows_in")
            load_router(1)
            pool.wait_ge(S("stored"), 16 * 6)
            experts(1)
            load(GS[:, 0, 0, :], d["final_norm_g"].rearrange("(o n) -> o n", o=1).broadcast_to([P, D]), "rows_in")
            for b in range(NB):
                pool.wait_ge(S("h_ready"), NB * 4 + b + 1)
                dst = outs["y_prompt"][0] if b == 0 else outs["y_sample"][0, (b - 1) * P:b * P]
                pool.dma_start(dst, H[:, b, :]).then_inc(S("stored"), 16)
            pool.wait_ge(S("stored"), 16 * 9)

        @block.tensor
        def _(pe):
            def chunk(name, n):
                j = CHUNKS.index((name, n))
                pe.wait_ge(S(f"chunk_in_{slot_of(j)}"), 16 * fills_of(j))
                return RC[:, slot_of(j)]

            def turn(b, ready, count):
                pe.wait_ge(S(ready), count)
                for half in range(2):
                    for kk in range(4):
                        t = pe.transpose(psum[:, 2 * b + half, kk * P:(kk + 1) * P], H[:, b, 4 * half + kk:D:KC], ident[:, :])
                    t.then_inc(S("turned"), 1)

            def transposed(u, b=NB - 1):
                for half in ("top", "low"):
                    pe.wait_ge(S(f"ht_{half}"), NB * TURNS.index(u) + b + 1)

            def project(to, b, w):
                for k in range(KC):
                    mm = pe.matmul(bank(to), HT[:, k, b * P:(b + 1) * P], w[:, k, :], start=(k == 0), stop=(k == KC - 1))
                return mm

            def turn_and_project(u, ready, counts, w, sem):
                turn(0, ready, counts[0])
                turn(1, ready, counts[1])
                for b in range(NB):
                    transposed(u, b)
                    project((6 + b) % 8, b, w).then_inc(S(sem), 1)
                    if b == 0:
                        turn(2, ready, counts[2])

            def mod_products(i):
                w = chunk("mod", i)
                if i < FRONT:
                    to = i % 2
                    if i >= 2:
                        pe.wait_ge(S("mod_part_sb"), i - 1)
                else:
                    to, sum_bank = MOD_BANKS[group_of(i)]
                    pe.wait_ge(S("mod_part_sb"), i)
                    if to == sum_bank and i > FRONT:
                        pe.wait_ge(S("rest_row_ready"), i - FRONT)
                for r in range(2):
                    for j in range(4):
                        k = 4 * r + j
                        mm = pe.matmul(psum[32 * j:32 * j + 32, to, :], cond_silu[:, k, :], w[:, k, :], start=(r == 0), stop=(r == 1))
                mm.then_inc(S("mod_part_ps"), 1)

            def mod_sum(i):
                l, n = MODS[i]
                row = 12 * l + n
                gain = 24 + 4 * (n // 6) + 2 * l + n % 2
                pe.wait_ge(S("mod_part_sb"), i + 1)
                if i < FRONT:
                    to, part = 2 + i % 2, mod_part[i % 2]
                    if i >= 2:
                        pe.wait_ge(S("front_row_ready"), i - 1)
                    if scaled(i):
                        pe.matmul(psum[0:2, 4 + i % 2, :], pick_bias[:, 2 * gain:2 * gain + 2], mod_bias[:, :], start=True, stop=True)
                else:
                    to, part = MOD_BANKS[group_of(i)][1], rest_buffers(i)[0]
                    if i > FRONT:
                        pe.wait_ge(S("rest_row_ready"), i - FRONT)
                pe.matmul(psum[0:2, to, :], pick[:, 0:2], part, start=True, stop=False)
                pe.matmul(psum[0:2, to, :], pick_bias[:, 2 * row:2 * row + 2], mod_bias[:, :], start=False, stop=True).then_inc(S("mod_sum_ps"), 1)

            def mod_group(group):
                for i in mods(group):
                    mod_products(i)
                    mod_sum(i)
                pe.wait_ge(S("rest_row_ready"), mods(group)[-1] - FRONT + 1)

            def spread(i):
                pe.wait_ge(S("front_row_ready"), i + 1)
                pe.wait_ge(S("consts"), 16 * 5)
                for s in range(2):
                    if i >= 1:
                        pe.wait_ge(S("spread_sb"), 2 * (i - 1) + s + 1)
                    pe.matmul(bank(6 + s), ident[0:2, s:s + 1].broadcast_to([2, P]), front_row[i], start=True, stop=True).then_inc(S("spread_ps"), 1)

            pe.wait_ge(S("cond_ready"), 1)
            for i in range(FRONT):
                mod_products(i)
                if i == 1:
                    pe.wait_ge(S("bias_ready"), 2)
                if i >= 1:
                    mod_sum(i - 1)
                if 2 <= i < 6:
                    spread(i - 2)
            mod_sum(FRONT - 1)

            pe.wait_ge(S("even_small"), 32)
            for g in range(GROUPS):
                t = pe.transpose(psum[:, 7, g * P:(g + 1) * P], WS_RAW[:, g, :], ident[:, :])
            t.then_inc(S("sides_turned"), 1)
            pe.wait_ge(S("front_row_ready"), FRONT)
            for b in range(NB):
                turn(b, "h_ready", b + 1)
            transposed(0)
            w = chunk("even_in", 0)
            for c in range(4):
                for k in range(KC):
                    mm = pe.matmul(psum[:, c, 0:T], w[:, k, c * P:(c + 1) * P], HT[:, k, :], start=(k == 0), stop=(k == KC - 1))
                mm.then_inc(S("qk_ps"), 1)
            for k in range(KC):
                mm = pe.matmul(psum[0:32, 4, 0:T], WA[:, k, :], HT[:, k, :], start=(k == 0), stop=(k == KC - 1))
            mm.then_inc(S("decay_in_ps"), 1)
            pe.wait_ge(S("spatial_ready"), 1)
            w = chunk("even_in", 1)
            project(5, 0, w).then_inc(S("v_ps"), 1)
            pe.wait_ge(S("decay_in_ready"), 1)
            pe.wait_ge(S("even_small"), 16 * 5)
            pe.wait_ge(S("qk_ready"), 4)
            for j in range(4):
                pe.matmul(psum[:, j, 0:T], WGU[:, j * P:(j + 1) * P], AT[:, :], start=True, stop=True).then_inc(S("decay_ps"), 1)
            for b in (1, 2):
                project(5 + b, b, w).then_inc(S("v_ps"), 1)

            def scores(n):
                src = QK if n == 0 else EX[(n - 1) % 2]
                if n == 0:
                    pe.wait_ge(S("z_ready"), 4)
                else:
                    pe.wait_ge(S("decayed_ready"), n)
                    pe.wait_ge(S("att_merged"), 2 * n)
                for r in range(2):
                    rows = slice(64 * r, 64 * r + 64)
                    for i in range(6):
                        b, c = divmod(i, 2)
                        mm = pe.matmul(psum[:, 2 * r + i // 4, (i % 4) * P:(i % 4 + 1) * P], src[rows, 2 + c, b * P:(b + 1) * P],
                                       src[rows, c, b * P:(b + 1) * P], start=True, stop=True)
                mm.then_inc(S("scores_ps"), 1)

            mod = FRONT
            for step in EVEN_PLAN:
                if step == "part":
                    mod_products(mod)
                    continue
                if step == "sum":
                    mod_sum(mod)
                    mod += 1
                    continue
                if isinstance(step, int):
                    scores(step)
                    continue
                name, b = step[:-1], int(step[-1])
                before_it = {"g": "v", "vg": "g", "u": "vg"}[name]
                if b == 0:
                    w = chunk("even_in", {"g": 2, "vg": 3, "u": 4}[name])
                pe.wait_ge(S(f"{before_it}_ready"), b + 1)
                project(5 + b, b, w).then_inc(S(f"{name}_ps"), 1)

            pe.wait_ge(S("u_ready"), 3)
            pe.wait_ge(S("rest_row_ready"), len(mods("even")))
            pe.wait_ge(S("to_end_ready"), 1)
            for a in range(2):
                for jc in range(4):
                    t = pe.transpose(psum[:, 4 + a, jc * P:(jc + 1) * P], E2[:, 2 + a, jc % 2, (jc // 2) * P:(jc // 2 + 1) * P], ident[:, :])
            t.then_inc(S("sides_turned"), 1)
            pe.wait_ge(S("kdt_ready"), 1)
            for a in range(2):
                for j in range(2):
                    blk = j if a == 0 else 2 * j
                    for h in range(GLA_HEADS):
                        c, r = divmod(h, 2)
                        mm = pe.matmul(psum[64 * r:64 * r + 64, 6 + a, (2 * j + c) * P:(2 * j + c + 1) * P],
                                       KDT[:, 4 * a + 2 * j + c, 64 * r:64 * r + 64], V[:, blk, h * P:(h + 1) * P], start=True, stop=True)
            mm.then_inc(S("state_ps"), 1)
            pe.wait_ge(S("att_merged"), 16)
            pe.wait_ge(S("states_ready"), 2)
            for b in range(NB):
                for h in range(GLA_HEADS):
                    c, r = divmod(h, 2)
                    to = psum[:, b, h * P:(h + 1) * P]
                    mm = pe.matmul(to, ATT[:, 6 * r + 2 * b + c, :], V[:, b, h * P:(h + 1) * P], start=True, stop=(b == 0))
                    if b > 0:
                        fwd = (S0 if b == 1 else S1)[:, 0, h, :]
                        bwd = (S1 if b == 1 else S0)[:, 1, h, :]
                        pe.matmul(to, E2[:, 0, c, (b - 1) * P:b * P], fwd, start=False, stop=False)
                        mm = pe.matmul(to, E2[:, 1, c, (b - 1) * P:b * P], bwd, start=False, stop=True)
                mm.then_inc(S("gla_out"), 1)
            pe.wait_ge(S("vg_normed"), 1)
            for g in range(GROUPS):
                pe.matmul(psum[:, 3 + g, 0:T], WST[:, g, :], VG[:, :, g * P:(g + 1) * P], start=True, stop=True).then_inc(S("spatial_ps"), 1)
            mod_group("gate")
            turn_and_project("cat", "cat_ready", (1, 1, 1), chunk("even_out", 0), "even_out_ps")
            w = chunk("even_out", 1)
            for b in range(NB):
                project((6 + 3 + b) % 8, b, w).then_inc(S("even_out_ps"), 1)

            def experts(l):
                u = 2 * l + 1

                def M(name):
                    return S(f"moe{l}_{name}")

                mod_group(f"norm_{u}")
                for b in range(NB):
                    turn(b, "h_ready", NB * u + b + 1)
                transposed(u)
                pe.wait_ge(S("router_in"), 16 * 4 * (l + 1))
                for k in range(KC):
                    mm = pe.matmul(psum[0:36, 6, 0:T], WR[:, k, :], HT[:, k, :], start=(k == 0), stop=(k == KC - 1))
                mm.then_inc(S("logits_ps"), 1)
                pe.wait_ge(S("logits_t"), l + 1)
                for b in range(NB):
                    t = pe.transpose(psum[:, 7, b * 36:(b + 1) * 36], LT[:, b * P:(b + 1) * P], ident[0:36, 0:36])
                t.then_inc(S("logits_turned"), 1)
                if l == 0:
                    mod_group("router")
                pe.wait_ge(S("chosen"), l + 1)
                for b in range(NB):
                    for a in range(b + 1):
                        pe.matmul(psum[:, 6, b * 32:(b + 1) * 32], (before if a == b else ones)[:, :], oh_sum[:, a, :],
                                  start=(a == 0), stop=(a == b)) if (a, b) != (NB - 1, NB - 1) else pe.matmul(
                            psum[:, 6, b * 32:(b + 1) * 32], before[:, :], oh_sum[:, a, :], start=False, stop=True).then_inc(S("counts_ps"), 1)
                for a in range(NB):
                    mm = pe.matmul(psum[:, 7, 0:32], ones[:, :], oh_sum[:, a, :], start=(a == 0), stop=(a == NB - 1))
                mm.then_inc(S("counts_ps"), 1)

                def gather(q, v, first=False):
                    pe.wait_ge(M("places_ready"), q + 1)
                    if not first:
                        pe.wait_ge(M("x_sb"), q * 2)
                    for half in range(2):
                        cols = slice(half * 512, (half + 1) * 512)
                        for b in range(NB):
                            pe.matmul(bank(half), PP[v][:, b, :], H_HI[:, b, cols], start=(b == 0), stop=False)
                            mm = pe.matmul(bank(half), PP[v][:, b, :], H_LO[:, b, cols], start=False, stop=(b == NB - 1))
                        mm.then_inc(M("xs_ps"), 1)

                def turn_rows(q):
                    pe.wait_ge(M("xs_sb"), q * 2 + 2)
                    for half in range(2):
                        for kk in range(4):
                            t = pe.transpose(psum[:, half, kk * P:(kk + 1) * P], XS[:, 4 * half + kk:D:KC], ident[:, :])
                        t.then_inc(M("x_ps"), 1)

                def weights_back(q, v, first=False):
                    if not first:
                        pe.wait_ge(M("added"), q * 6)
                    for b in range(NB):
                        t = pe.transpose(psum[:, 7, b * P:(b + 1) * P], PW[v][:, b, :], ident[:, :])
                    t.then_inc(M("weights_ps"), 1)

                def combine(q, first=False):
                    pe.wait_ge(M("y_split"), q * 2 + 2)
                    pe.wait_ge(M("slots_t"), q + 1)
                    for c in range(6):
                        b, n = divmod(c, 2)
                        to = bank((6, 7, 4, 5, 6, 7)[c])
                        if c >= 4:
                            pe.wait_ge(M("added"), q * 6 + c - 3)
                        cols = slice(n * 512, (n + 1) * 512)
                        pe.matmul(to, PPT[:, b, :], Y_HI[:, cols], start=True, stop=False)
                        pe.matmul(to, PPT[:, b, :], Y_LO[:, cols], start=False, stop=True).then_inc(M("back_ps"), 1)

                def pair(q, v, first=False):
                    for a in range(2):
                        pe.wait_ge(M(f"in_{3 * v + a}"), landed(q, v))
                    pe.wait_ge(M("x_sb"), q * 2 + 2)
                    if not first:
                        pe.wait_ge(M("hidden"), q)
                    for k in range(KC):
                        for e in range(2):
                            mm = pe.matmul(psum[64 * e:64 * e + 64, 2, :], XT[:, k, 64 * e:64 * e + 64], RG[:, 3 * v:3 * v + 2, e, k, :],
                                           start=(k == 0), stop=(k == KC - 1))
                    mm.then_inc(M("gate_up"), 1)
                    gather(q + 1, 1 - v)
                    pe.wait_ge(M("hidden"), q + 1)
                    if not first:
                        pe.wait_ge(M("hidden_t"), q)
                    for k in range(2):
                        t = pe.transpose(psum[:, 3, k * P:(k + 1) * P], HID[v][:, k:256:2], ident[:, :])
                    t.then_inc(M("hidden_ps"), 1)
                    if not first:
                        combine(q - 1)
                    turn_rows(q + 1)
                    pe.wait_ge(M("hidden_t"), q + 1)
                    pe.wait_ge(M(f"in_{3 * v + 2}"), landed(q, v))
                    if not first:
                        pe.wait_ge(M("added"), q * 6 - 2)
                    for n in range(2):
                        for k in range(2):
                            for e in range(2):
                                mm = pe.matmul(psum[64 * e:64 * e + 64, 4 + n, :], HTS[v][:, k, 64 * e:64 * e + 64],
                                               RD[:, 3 * v + 2, e, k, n * 512:(n + 1) * 512], start=(k == 0), stop=(k == 1))
                        mm.then_inc(M("down"), 1)
                    weights_back(q, v, first)

                def landed(q, v):
                    return (q - v) * 8 + 16

                pe.wait_ge(S("h_split"), l + 1)
                gather(0, 0, first=True)
                turn_rows(0)
                pair(0, 0, first=True)
                pair(1, 1)
                R = rounds_of(pe, l)
                with pe.Fori(1, R * (PAIRS // 2)) as i:
                    for v in range(2):
                        pair(i * 2 + v, v)
                combine(R * PAIRS - 1)

            experts(0)

            mod_group("norm_2")
            turn_and_project(2, "h_ready", [NB * 2 + b + 1 for b in range(NB)], chunk("odd_in", 0), "odd_in_ps")
            for n in (1, 2):
                w = chunk("odd_in", n)
                for b in range(NB):
                    if 3 * n + b == 8:
                        pe.wait_ge(S("qkv_ready"), 1)
                    project((6 + 3 * n + b) % 8, b, w).then_inc(S("odd_in_ps"), 1)
            pe.wait_ge(S("odd_small"), 16 * 5)
            pe.wait_ge(S("qkv_ready"), 9)
            for g in range(KV_HEADS):
                t = pe.transpose(psum[:, 7, g * P:(g + 1) * P], CK[:, g * P:(g + 1) * P], ident[:, :])
            t.then_inc(S("sides_turned"), 1)
            pe.wait_ge(S("k_t_ready"), 1)
            mod_group("attention")

            def turn_heads(to, b, cols, heads):
                for h in range(heads):
                    t = pe.transpose(to[:, h * P:(h + 1) * P], QKV[:, b, cols + h * P:cols + (h + 1) * P], ident[:, :])
                return t

            for half in range(2):
                pe.wait_ge(S("qk_normed"), 1 + half)
                for b in range(NB):
                    turn_heads(bank(3 * half + b), b, 512 * half, 4).then_inc(S("q_turned"), 1)
            pe.wait_ge(S("qk_normed"), 3)
            for b in range(NB):
                t = turn_heads(psum[:, 6 + b // 2, (b % 2) * 256:(b % 2) * 256 + 256], b, D, KV_HEADS)
                if b >= 1:
                    t.then_inc(S("k_turned"), 1)

            def att_scores(i):
                b, g = divmod(i, 2)
                pe.wait_ge(S("exps_ready"), i)
                if i == 0:
                    pe.wait_ge(S("q_t_ready"), 6)
                    pe.wait_ge(S("k_t_ready"), 3)
                keys = KT[:, g, 0:1, :] if b == 0 else KT[:, g, 1:4, :]
                for hh in range(4):
                    mm = pe.matmul(psum[:, hh, 0:keys.shape[1] * P], QT[:, 4 * g + hh, b * P:(b + 1) * P], keys, start=True, stop=True)
                mm.then_inc(S("att_scores_ps"), 1)

            def turn_probs(i):
                pe.wait_ge(S("probs_ready"), i + 1)
                if i >= 1:
                    pe.wait_ge(S("probs_t_ready"), i)
                for kb in range(1 if i < 2 else 3):
                    for hh in range(4):
                        t = pe.transpose(psum[:, 4 + kb, hh * P:(hh + 1) * P], PR[i % 2][:, hh, kb * P:(kb + 1) * P], ident[:, :])
                t.then_inc(S("probs_turned"), 1)

            def att_values(i):
                b, g = divmod(i, 2)
                blocks = 1 if b == 0 else 3
                pe.wait_ge(S("probs_t_ready"), i + 1)
                if i >= 1:
                    pe.wait_ge(S("att_out_ready"), i)
                for kb in range(blocks):
                    if b == 0:
                        vals = QKV[:, 0, 1280 + g * P:1280 + (g + 1) * P]
                    else:
                        vals = CV[:, g * P:(g + 1) * P] if kb == 0 else QKV[:, kb, 1280 + g * P:1280 + (g + 1) * P]
                    mm = pe.matmul(bank(7), vals, PT[:, kb, :], start=(kb == 0), stop=(kb == blocks - 1))
                mm.then_inc(S("probs_t_used"), 1)

            att_scores(0)
            for i in range(6):
                if i < 5:
                    att_scores(i + 1)
                if i >= 1:
                    att_values(i - 1)
                turn_probs(i)
            att_values(5)
            pe.wait_ge(S("att_out_ready"), 6)
            for n in range(2):
                w = chunk("odd_out", n)
                for b in range(NB):
                    project(3 * n + b, b, w).then_inc(S("odd_out_ps"), 1)

            experts(1)

        def att_out(act, i):
            b, g = divmod(i, 2)
            act.wait_ge(S("probs_t_used"), i + 1)
            act.copy(OT[:, 4 * g:4 * g + 4, b * P:(b + 1) * P], bank(7).rearrange("p (h t) -> p h t", h=4)).then_inc(S("att_out_ready"), 1)

        @block.scalar
        def _(act):
            def norm(u):
                norm_squares(u)
                inverse_root(f"norm_{u}", ms, rs)

            def norm_squares(u):
                if u == 0:
                    act.wait_ge(S("x_loaded"), 32)
                for b in range(NB):
                    if u > 0:
                        act.wait_ge(S("x_updated"), NB * (u - 1) + b + 1)
                    a = act.activation(H[:, b, :], X[:, b, :], ACT.Square, accum_out=ss[:, b:b + 1])
                a.then_inc(S("squares"), 1)

            def inverse_root(tag, v, y):
                n = ROOTS.index(tag) + 1
                act.wait_ge(S("mean_squares"), n)
                act.activation(y, v, ACT.Ln).then_inc(S("root_log"), 1)
                act.wait_ge(S("root_log"), n)
                act.activation(y, y, ACT.Exp, scale=-0.5).then_inc(S("root_guess"), 1)

            def mod_part_copy(i):
                act.wait_ge(S("mod_part_ps"), i + 1)
                act.copy(rest_buffers(i)[0], bank(MOD_BANKS[group_of(i)][0])).then_inc(S("mod_part_sb"), 1)

            def mod_row_copy(i):
                act.wait_ge(S("mod_sum_ps"), i + 1)
                act.copy(rest_buffers(i)[1], psum[0:2, MOD_BANKS[group_of(i)][1], :]).then_inc(S("rest_row_ready"), 1)

            def mod_copies(chunks):
                for i in chunks:
                    mod_part_copy(i)
                    mod_row_copy(i)

            def ht_copies(u):
                for b in range(NB):
                    act.wait_ge(S("turned"), 6 * TURNS.index(u) + 2 * b + 1)
                    act.copy(HT[:, 0:4, b * P:(b + 1) * P], bank(2 * b).rearrange("p (k t) -> p k t", k=4)).then_inc(S("ht_top"), 1)

            act.wait_ge(S("cond_in"), 32)
            act.wait_ge(S("cond_zero"), 1)
            act.activation(cond_silu[:, :, 0:2], cond, ACT.Silu).then_inc(S("cond_ready"), 1)
            for i in range(FRONT):
                act.wait_ge(S("mod_part_ps"), i + 1)
                if i >= 2:
                    act.wait_ge(S("mod_sum_ps"), i - 1)
                act.copy(mod_part[i % 2], bank(i % 2)).then_inc(S("mod_part_sb"), 1)
                if 2 <= i < 6:
                    part, half = divmod(i - 2, 2)
                    for s in range(2):
                        act.wait_ge(S("spread_ps"), 2 * (i - 2) + s + 1)
                        act.copy(GS[:, part, s, half * COLS:(half + 1) * COLS], bank(6 + s)).then_inc(S("spread_sb"), 1)
                if i == 6:
                    norm_squares(0)
                if i == 8:
                    inverse_root("norm_0", ms, rs)

            ht_copies(0)
            act.wait_ge(S("front_stored"), 16 * (FRONT - 4))
            for c in range(2):
                act.wait_ge(S("qk_ps"), c + 1)
                act.mul(QK[:, c, :], psum[:, c, 0:T], GLA_DK ** -0.5).then_inc(S("qk_ready"), 1)
            act.wait_ge(S("decay_in_ps"), 1)
            act.copy(AT, psum[0:32, 4, 0:T]).then_inc(S("decay_in_ready"), 1)

            def evacuate(name, dst, b):
                act.wait_ge(S(f"{name}_ps"), b + 1)
                act.copy(dst[:, b, :], bank(5 + b)).then_inc(S(f"{name}_ready"), 1)

            evacuate("v", V, 0)
            act.wait_ge(S("z_abs"), 1)
            act.activation(EZ, EZ, ACT.Exp, scale=-1.0).then_inc(S("z_logs"), 1)
            act.wait_ge(S("z_logs"), 1)
            act.activation(EZ, EZ, ACT.Ln, bias=1.0).then_inc(S("z_logs"), 1)
            evacuate("v", V, 1)
            evacuate("v", V, 2)
            act.wait_ge(S("masks_ready"), 1)

            def level_exp(n):
                act.wait_ge(S("decays_ready"), n)
                act.activation(EX[(n - 1) % 2], EX[(n - 1) % 2], ACT.Exp, scale=1.0 / GLA_TAU).then_inc(S("decays_exp"), 1)

            def in_plan(steps, mod):
                for step in steps:
                    if step == "part":
                        mod_part_copy(mod)
                    elif step == "sum":
                        mod_row_copy(mod)
                        mod += 1
                    elif isinstance(step, int):
                        if step < 7:
                            level_exp(step + 1)
                        if step == 6:
                            act.wait_ge(S("vg_ready"), 3)
                            act.activation(VG, VG, ACT.Gelu_apprx_tanh).then_inc(S("activated"), 1)
                    else:
                        evacuate(step[:-1], {"g": SG, "vg": VG, "u": U}[step[:-1]], int(step[-1]))
                return mod

            before_levels = EVEN_PLAN.index(0)
            mod = in_plan(EVEN_PLAN[:before_levels], FRONT)
            act.wait_ge(S("sums_ready"), 1)
            act.activation(E2[:, 0], BF[:, :, P:T], ACT.Exp, scale=1.0 / GLA_TAU)
            act.activation(E2[:, 1], BB[:, :, P:T], ACT.Exp, scale=1.0 / GLA_TAU)
            act.activation(E2[:, 2:4], E2[:, 2:4], ACT.Exp, scale=1.0 / GLA_TAU)
            act.activation(dec_f.rearrange("p (c o) -> p c o", o=1), BF[:, :, 2 * P - 1:2 * P], ACT.Exp, scale=1.0 / GLA_TAU)
            act.activation(dec_b.rearrange("p (c o) -> p c o", o=1), BB[:, :, 2 * P:2 * P + 1], ACT.Exp, scale=1.0 / GLA_TAU).then_inc(S("to_end_exp"), 1)
            in_plan(EVEN_PLAN[before_levels:], mod)
            act.wait_ge(S("sides_turned"), 2)
            act.copy(KDT.rearrange("p i t -> p (i t)"), psum[:, 4:6, :].rearrange("p b n -> p (b n)")).then_inc(S("kdt_ready"), 1)
            act.wait_ge(S("u_ready"), 3)
            act.activation(U, U, ACT.Gelu_apprx_tanh).then_inc(S("activated"), 1)
            act.wait_ge(S("g_ready"), 3)
            act.activation(SG, SG, ACT.Silu).then_inc(S("activated"), 1)
            inverse_root("ln", ln_v, ln_rs)
            act.wait_ge(S("gla_out"), 3)
            act.copy(O.rearrange("p b n -> p (b n)"), psum[:, 0:3, :].rearrange("p b n -> p (b n)")).then_inc(S("o_ready"), 1)
            inverse_root("gla", gla_ms, gla_rs)
            mod_copies(mods("gate"))
            ht_copies("cat")

            def experts(l):
                u = 2 * l + 1

                def M(name):
                    return S(f"moe{l}_{name}")

                norm(u)
                mod_copies(mods(f"norm_{u}"))
                ht_copies(u)
                act.wait_ge(S("logits_ps"), l + 1)
                act.wait_ge(S("router_in"), 16 * 4 * (l + 1))
                act.activation(LT, psum[0:36, 6, 0:T], ACT.Identity, bias=BR).then_inc(S("logits_t"), 1)
                if l == 0:
                    mod_copies(mods("router")[:1])
                act.wait_ge(S("router_sub"), l + 1)
                act.activation(g_tmp, g_tmp, ACT.Exp)
                act.activation(top_f[:, :, 0:1], top_f[:, :, 1:2], ACT.Exp).then_inc(S("router_exp"), 1)
                if l == 0:
                    mod_copies(mods("router")[1:])

                def rows_copies(q, first=False):
                    for half in range(2):
                        act.wait_ge(M("xs_ps"), q * 2 + half + 1)
                        if not first and half == 0:
                            act.wait_ge(M("x_ps"), q * 2)
                        act.copy(XS[:, half * 512:(half + 1) * 512], bank(half)).then_inc(M("xs_sb"), 1)

                def x_copies(q, first=False):
                    for half in range(2):
                        act.wait_ge(M("x_ps"), q * 2 + half + 1)
                        if not first and half == 0:
                            act.wait_ge(M("gate_up"), q)
                        act.copy(XT[:, 4 * half:4 * half + 4, :], bank(half).rearrange("p (k s) -> p k s", k=4)).then_inc(M("x_sb"), 1)

                def weights_copy(q, first=False):
                    act.wait_ge(M("weights_ps"), q + 1)
                    if not first:
                        act.wait_ge(M("slots_t"), q)
                    act.activation(PWT, psum[:, 7, 0:T].rearrange("p (b t) -> p b t", b=NB), ACT.Copy, accum_out=w_slot).then_inc(M("weights_sb"), 1)

                def pair(q, v, first=False, second=False):
                    act.wait_ge(M("gate_up"), q + 1)
                    if not first and not second:
                        act.wait_ge(M("hidden"), q - 1)
                    act.activation(SGM[v], psum[:, 2, 0:256], ACT.Silu).then_inc(M("gated"), 1)
                    rows_copies(q + 1)
                    x_copies(q + 1)
                    weights_copy(q, first)
                    act.wait_ge(M("weights_sb"), q + 1)
                    for n in range(2):
                        act.wait_ge(M("down"), q * 2 + n + 1)
                        if not first and n == 0:
                            act.wait_ge(M("back_ps"), q * 6)
                        act.activation(Y[:, n * 512:(n + 1) * 512], bank(4 + n), ACT.Copy, scale=w_slot).then_inc(M("y_sb"), 1)

                rows_copies(0, first=True)
                x_copies(0, first=True)
                pair(0, 0, first=True)
                pair(1, 1, second=True)
                R = rounds_of(act, l)
                with act.Fori(1, R * (PAIRS // 2)) as i:
                    for v in range(2):
                        pair(i * 2 + v, v)

            experts(0)

            mod_copies(mods("norm_2")[:2])
            norm(2)
            mod_copies(mods("norm_2")[2:])
            ht_copies(2)
            for i in range(9):
                n, b = divmod(i, 3)
                act.wait_ge(S("odd_in_ps"), i + 1)
                act.copy(QKV[:, b, n * 512:(n + 1) * 512], bank((6 + i) % 8)).then_inc(S("qkv_ready"), 1)
                if i in (2, 5):
                    inverse_root(f"qk_{n}", q_ms[n], q_rs[n])
            act.wait_ge(S("sides_turned"), 3)
            act.copy(KT[:, :, 1, :], psum[:, 7, 0:256].rearrange("p (g t) -> p g t", g=2)).then_inc(S("k_t_ready"), 1)
            inverse_root("qk_2", q_ms[2], q_rs[2])
            mod_copies(mods("attention"))
            for i in range(6):
                half, b = divmod(i, 3)
                act.wait_ge(S("q_turned"), i + 1)
                act.copy(QT[:, 4 * half:4 * half + 4, b * P:(b + 1) * P],
                         bank(i).rearrange("p (h t) -> p h t", h=4)).then_inc(S("q_t_ready"), 1)
            act.wait_ge(S("k_turned"), 1)
            act.copy(KT[:, :, 0:3:2, :], bank(6).rearrange("p (b g t) -> p g b t", b=2, g=2)).then_inc(S("k_t_ready"), 1)
            act.wait_ge(S("k_turned"), 2)
            act.copy(KT[:, :, 3, :], psum[:, 7, 0:256].rearrange("p (g t) -> p g t", g=2)).then_inc(S("k_t_ready"), 1)
            for i in range(6):
                n = P if i < 2 else 3 * P
                act.wait_ge(S("max_ready"), i + 1)
                if i >= 2:
                    act.wait_ge(S("probs_turned"), i - 1)
                for hh in range(4):
                    a = act.activation(PR[i % 2][:, hh, 0:n], psum[:, hh, 0:n], ACT.Exp, bias=att_max[:, i, hh:hh + 1],
                                       scale=HD ** -0.5, accum_out=att_sum[:, i, hh:hh + 1])
                a.then_inc(S("exps_ready"), 1)
                if i >= 2:
                    att_out(act, i - 2)
            att_out(act, 4)
            att_out(act, 5)
            experts(1)
            norm(4)

        @block.vector
        def _(dve):
            links = [0]

            def link(ins):
                links[0] += 1
                ins.then_inc(S("dve_links"), 1)
                dve.wait_ge(S("dve_links"), links[0])

            def inverse_root(tag, v, y, t):
                dve.wait_ge(S("root_guess"), ROOTS.index(tag) + 1)
                link(dve.tensor_tensor(t, y, y, ALU.mult))
                link(dve.tensor_tensor(t, t, v, ALU.mult))
                link(dve.tensor_scalar(t, t, -0.5, 1.5, ALU.mult, ALU.add))
                link(dve.tensor_tensor(y, y, t, ALU.mult))

            def norm(u):
                norm_means(u)
                norm_apply(u)

            def norm_means(u):
                dve.wait_ge(S("squares"), u + 1)
                if u > 0:
                    dve.wait_ge(S("x_updated"), NB * u)
                dve.tensor_scalar(ms, ss, 1.0 / D, EPS, ALU.mult, ALU.add).then_inc(S("mean_squares"), 1)

            def norm_apply(u):
                inverse_root(f"norm_{u}", ms, rs, rt)
                if u == 0:
                    dve.wait_ge(S("spread_sb"), 8)
                else:
                    dve.wait_ge(S("rows_in"), 16 * u)
                for b in range(NB):
                    s = min(b, 1)
                    gain = GS[:, 1, s, :] if u < 4 else GS[:, 0, 0, :]
                    a = dve.scalar_tensor_tensor(H[:, b, :], X[:, b, :], rs[:, b:b + 1], gain, ALU.mult, ALU.mult)
                    if u == 4:
                        a.then_inc(S("h_ready"), 1)
                        continue
                    link(a)
                    dve.tensor_tensor(H[:, b, :], H[:, b, :], GS[:, 0, s, :], ALU.add).then_inc(S("h_ready"), 1)

            def ht_copies(u):
                for b in range(NB):
                    dve.wait_ge(S("turned"), 6 * TURNS.index(u) + 2 * b + 2)
                    dve.tensor_copy(HT[:, 4:8, b * P:(b + 1) * P], bank(2 * b + 1).rearrange("p (k t) -> p k t", k=4)).then_inc(S("ht_low"), 1)

            def update(u, ps, bank_of, buf):
                dve.wait_ge(S("gate_in"), 16 * (u + 1))
                for c in range(6):
                    n, b = divmod(c, 3)
                    cols = slice(n * 512, (n + 1) * 512)
                    dve.wait_ge(S(ps), c + 1)
                    link(dve.tensor_tensor(buf[c % 2], bank(bank_of(c)), GT[:, min(b, 1), cols], ALU.mult))
                    a = dve.tensor_tensor(X[:, b, cols], X[:, b, cols], buf[c % 2], ALU.add)
                    if n == 1:
                        a.then_inc(S("x_updated"), 1)

            dve.memset(ones[:, :], 1.0)
            dve.memset(cond_silu, 0.0).then_inc(S("cond_zero"), 1)
            dve.wait_ge(S("mod_small"), 16 * 7)
            dve.tensor_copy(pick_bias[:, :], pick[0:64, 2:2 + 2 * 32])
            dve.tensor_copy(mod_bias[:, :], bias_raw).then_inc(S("bias_ready"), 1)
            dve.wait_ge(S("bias_ready"), 1)
            dve.tensor_tensor(mod_bias[32:64, :], bias_raw[32:64, :], mod_bias[32:64, :], ALU.subtract).then_inc(S("bias_ready"), 1)
            for i in range(FRONT):
                if i == 7:
                    norm_means(0)
                if i == 9:
                    norm_apply(0)
                dve.wait_ge(S("mod_sum_ps"), i + 1)
                sums = psum[0:2, 2 + i % 2, :]
                if scaled(i):
                    link(dve.tensor_copy(front_row[i], psum[0:2, 4 + i % 2, :]))
                    a = dve.scalar_tensor_tensor(front_row[i], sums, 1.0, front_row[i], ALU.add, ALU.mult)
                else:
                    a = dve.tensor_copy(front_row[i], sums)
                a.then_inc(S("front_row_ready"), 1)
            dve.wait_ge(S("masks_in"), 16)
            dve.tensor_copy(masks[:, :], MASKS_F32).then_inc(S("masks_ready"), 1)

            dve.wait_ge(S("sides_turned"), 1)
            dve.tensor_copy(WST.rearrange("p g t -> p (g t)"), bank(7)).then_inc(S("spatial_ready"), 1)
            ht_copies(0)
            dve.wait_ge(S("front_stored"), 16 * (FRONT - 4))
            for c in (2, 3):
                dve.wait_ge(S("qk_ps"), c + 1)
                dve.tensor_copy(QK[:, c, :], psum[:, c, 0:T]).then_inc(S("qk_ready"), 1)
            for j in range(4):
                dve.wait_ge(S("decay_ps"), j + 1)
                dve.tensor_scalar(Z[:, j, :], psum[:, j, 0:T], b_gate[:, j:j + 1], None, ALU.add).then_inc(S("z_ready"), 1)
            dve.wait_ge(S("z_ready"), 4)
            dve.scalar_tensor_tensor(EZ, Z, -1.0, Z, ALU.mult, ALU.max).then_inc(S("z_abs"), 1)
            dve.wait_ge(S("z_logs"), 2)
            link(dve.scalar_tensor_tensor(Z, Z, 0.0, EZ, ALU.min, ALU.subtract))
            for c in range(2):
                for b in range(NB):
                    blk = slice(b * P, (b + 1) * P)
                    dve.tensor_tensor_scan(BF[:, c, blk], ones[:, :], Z[:, c, blk], 0.0, ALU.mult, ALU.add)
                    a = dve.tensor_tensor_scan(BB[:, c, blk][:, ::-1], ones[:, :], Z[:, 2 + c, blk][:, ::-1], 0.0, ALU.mult, ALU.add)
            link(a)

            def blocks(v):
                return v.rearrange("p c (b t) -> p c b t", t=P)

            to_f = blocks(E2[:, 2])
            to_b = blocks(E2[:, 3])
            dve.tensor_tensor(to_f, blocks(BF)[:, :, 0:2, P - 1:P].broadcast_to([P, 2, 2, P]), blocks(BF)[:, :, 0:2, :], ALU.subtract)
            dve.tensor_tensor(to_b, blocks(BB)[:, :, 0:3:2, 0:1].broadcast_to([P, 2, 2, P]), blocks(BB)[:, :, 0:3:2, :], ALU.subtract).then_inc(S("sums_ready"), 1)

            def level_decays(n):
                m = LEVELS[n - 1]
                if n >= 3:
                    dve.wait_ge(S("scores_ps"), n - 1)

                def halves(v):
                    return v.rearrange("p c (a h m) -> p c a h m", h=2, m=m)

                ex, f, g = halves(EX[(n - 1) % 2]), halves(BF), halves(BB)
                shape = [P, 2, T // (2 * m), m]
                border_f = f[:, :, :, 0, m - 1:m].broadcast_to(shape)
                border_b = g[:, :, :, 1, 0:1].broadcast_to(shape)
                dve.tensor_tensor(ex[:, 0:2, :, 1, :], f[:, :, :, 1, :], border_f, ALU.subtract)
                dve.tensor_tensor(ex[:, 0:2, :, 0, :], g[:, :, :, 0, :], border_b, ALU.subtract)
                dve.tensor_tensor(ex[:, 2:4, :, 0, :], border_f, f[:, :, :, 0, :], ALU.subtract)
                dve.tensor_tensor(ex[:, 2:4, :, 1, :], border_b, g[:, :, :, 1, :], ALU.subtract).then_inc(S("decays_ready"), 1)

            def scores_of(r):
                return psum[:, 2 * r:2 * r + 2, :].rearrange("p b n -> p (b n)")[:, 0:6 * P].rearrange("p (i t) -> p i t", i=6)

            def merge(n):
                dve.wait_ge(S("scores_ps"), n + 1)
                if n >= 1:
                    dve.wait_ge(S("att_merged"), 2 * n)
                for r in range(2):
                    att = ATT[:, 6 * r:6 * r + 6, :]
                    if n == 0:
                        eye = ident[:, :].rearrange("p (o t) -> p o t", o=1).broadcast_to([P, 6, P])
                        a = dve.scalar_tensor_tensor(att, scores_of(r), 2.0, eye, ALU.mult, ALU.mult)
                    else:
                        mask = masks[:, (n - 1) * P:n * P].rearrange("p (o t) -> p o t", o=1).broadcast_to([P, 6, P])
                        a = dve.copy_predicated(att, mask, scores_of(r))
                    a.then_inc(S("att_merged"), 1)

            level_decays(1)
            dve.wait_ge(S("to_end_exp"), 1)
            for a_ in range(2):
                dve.tensor_tensor(E2[:, a_], E2[:, a_], QK[:, 0:2, P:T], ALU.mult)
            dve.tensor_tensor(to_f, to_f, blocks(QK[:, 2:4, :])[:, :, 0:2, :], ALU.mult)
            dve.tensor_tensor(to_b, to_b, blocks(QK[:, 2:4, :])[:, :, 0:3:2, :], ALU.mult).then_inc(S("to_end_ready"), 1)
            for n in range(1, 8):
                dve.wait_ge(S("decays_exp"), n)
                dve.tensor_tensor(EX[(n - 1) % 2], EX[(n - 1) % 2], QK, ALU.mult).then_inc(S("decayed_ready"), 1)
                merge(n - 1)
                if n < 7:
                    level_decays(n + 1)
            dve.wait_ge(S("activated"), 1)
            for i in range(12):
                b, g = divmod(i, 4)
                a = dve.bn_stats(BN[:, i, 0:6], VG[:, b, g * P:(g + 1) * P])
            link(a)
            for i in range(12):
                a = dve.bn_aggr(BN[:, i, 6:8], BN[:, i, 0:6])
            link(a)
            dve.tensor_scalar(ln_v.rearrange("p (i o) -> p i o", o=1), BN[:, :, 7:8], EPS, None, ALU.add).then_inc(S("mean_squares"), 1)
            merge(7)

            dve.wait_ge(S("state_ps"), 1)
            dve.wait_ge(S("decays_exp"), 7)
            for a_ in range(2):
                a = dve.tensor_copy(ST_OUT[:, a_].rearrange("p c v -> p (c v)"), psum[:, 6 + a_, 0:256])
            a.then_inc(S("states_ready"), 1)
            dve.wait_ge(S("state_in"), 16 * 8)
            dve.wait_ge(S("pool_zeros"), 2)
            for a_ in range(2):
                for h in range(GLA_HEADS):
                    c, r = divmod(h, 2)
                    rows = slice(64 * r, 64 * r + 64)
                    dec = (dec_f, dec_b)[a_]
                    a = dve.scalar_tensor_tensor(S1[rows, a_, h, :], S0[rows, a_, h, :], dec[rows, c:c + 1],
                                                 psum[rows, 6 + a_, (2 + c) * P:(3 + c) * P], ALU.mult, ALU.add)
            a.then_inc(S("states_ready"), 1)

            inverse_root("ln", ln_v, ln_rs, ln_rt)
            for i in range(12):
                b, g = divmod(i, 4)
                v = VG[:, b, g * P:(g + 1) * P]
                a = dve.tensor_scalar(v, v, BN[:, i, 6:7], ln_rs[:, i:i + 1], ALU.subtract, ALU.mult)
            a.then_inc(S("vg_normed"), 1)
            dve.wait_ge(S("activated"), 3)
            sg_all = SG.rearrange("p b (h v) -> p (b h) v", v=P)
            a = dve.tensor_tensor(sg_all, sg_all, GLAG.rearrange("p (o v) -> p o v", o=1).broadcast_to([P, 12, P]), ALU.mult)
            a.then_inc(S("gla_gain_ready"), 1)
            dve.wait_ge(S("o_ready"), 1)
            o_all = O.rearrange("p b n -> p (b n)")
            link(dve.tensor_tensor(OSQ, o_all, o_all, ALU.mult))
            link(dve.tensor_reduce(gla_ms, OSQ.rearrange("p (i v) -> p i v", v=P), AX.X, ALU.add))
            dve.tensor_scalar(gla_ms, gla_ms, 1.0 / GLA_DV, EPS, ALU.mult, ALU.add).then_inc(S("mean_squares"), 1)
            inverse_root("gla", gla_ms, gla_rs, gla_rt)
            o_heads = O.rearrange("p b (h v) -> p (b h) v", v=P)
            link(dve.tensor_tensor(o_heads, o_heads, gla_rs.rearrange("p (i o) -> p i o", o=1).broadcast_to([P, 12, P]), ALU.mult))
            dve.wait_ge(S("gla_gain_ready"), 1)
            dve.tensor_tensor(H[:, :, 0:512], O, SG, ALU.mult)
            dve.wait_ge(S("activated"), 2)
            for g in range(GROUPS):
                dve.wait_ge(S("spatial_ps"), g + 1)
                cols = slice(g * P, (g + 1) * P)
                a = dve.scalar_tensor_tensor(H[:, :, 512 + g * P:512 + (g + 1) * P], psum[:, 3 + g, 0:T].rearrange("p (b c) -> p b c", b=NB),
                                             b_spat[:, g:g + 1], U[:, :, cols], ALU.add, ALU.mult)
            a.then_inc(S("cat_ready"), 1)
            ht_copies("cat")
            update(0, "even_out_ps", lambda c: (6 + c) % 8, UPD)

            def experts(l):
                u = 2 * l + 1

                def M(name):
                    return S(f"moe{l}_{name}")

                norm(u)
                ht_copies(u)

                dve.wait_ge(S("h_ready"), NB * (u + 1))
                dve.tensor_copy(H_HI, H).then_inc(S("h_top"), 1)

                def wide(v, n):
                    return v.rearrange("p (b o) -> p b o", o=1).broadcast_to([P, NB, n])

                dve.wait_ge(S("logits_turned"), l + 1)
                link(dve.tensor_copy(LG.rearrange("p b n -> p (b n)"), psum[:, 7, 0:NB * 36]))
                link(dve.tensor_reduce(g_max, LG[:, :, 0:4], AX.X, ALU.max))
                link(dve.tensor_tensor(g_tmp, LG[:, :, 0:4], wide(g_max, 4), ALU.is_equal))
                four = iota[:, 0:4].rearrange("p (o n) -> p o n", o=1).broadcast_to([P, NB, 4])
                link(dve.scalar_tensor_tensor(e_mask[:, :, 0:4], four, -8.0, g_tmp, ALU.add, ALU.mult))
                link(dve.tensor_reduce(g_idx, e_mask[:, :, 0:4], AX.X, ALU.min))
                link(dve.tensor_scalar(g_idx, g_idx, 8.0, None, ALU.add))
                link(dve.tensor_tensor(g_tmp, LG[:, :, 0:4], wide(g_max, 4), ALU.subtract))
                e_groups = e_mask.rearrange("p b (g n) -> p b g n", g=MOE_GROUPS)
                for g in range(MOE_GROUPS):
                    link(dve.tensor_scalar(e_groups[:, :, g, :], wide(g_idx, PER_GROUP), float(g), None, ALU.is_equal))
                link(dve.tensor_scalar(e_mask, e_mask, BIG, -BIG, ALU.mult, ALU.add))
                link(dve.tensor_tensor(e_mask, e_mask, LG[:, :, 4:36], ALU.add))
                for b in range(NB):
                    link(dve.max(top_v[:, b, :], e_mask[:, b, :]))
                    link(dve.max_index(top_i[:, b, :].bitcast(U32), top_v[:, b, :], e_mask[:, b, :]))
                dve.tensor_tensor(top_f[:, :, 1:2], top_v[:, :, 1:2], top_v[:, :, 0:1], ALU.subtract).then_inc(S("router_sub"), 1)
                dve.wait_ge(S("router_exp"), l + 1)
                link(dve.tensor_reduce(g_sum, g_tmp, AX.X, ALU.add))
                link(dve.reciprocal(g_prob, g_sum))
                e1 = top_f[:, :, 0]
                link(dve.tensor_scalar(g_sum, e1, 1.0, None, ALU.add))
                link(dve.reciprocal(g_sum, g_sum))
                link(dve.tensor_tensor(gates[:, 0, :], g_sum, g_prob, ALU.mult))
                link(dve.tensor_tensor(gates[:, 1, :], gates[:, 0, :], e1, ALU.mult))
                link(dve.tensor_copy(top_f, top_i[:, :, 0:2].bitcast(U32)))
                all32 = iota32.rearrange("p (o n) -> p o n", o=1).broadcast_to([P, NB, 32])
                for j in range(2):
                    link(dve.tensor_tensor(oh[j], all32, top_f[:, :, j:j + 1].broadcast_to([P, NB, 32]), ALU.is_equal))
                dve.tensor_tensor(oh_sum, oh[0], oh[1], ALU.add).then_inc(S("chosen"), 1)
                link(dve.memset(ht_t[:, :], 0.0))
                dve.wait_ge(S("counts_ps"), 2 * l + 1)
                link(dve.tensor_copy(cnt.rearrange("p b n -> p (b n)"), psum[:, 6, 0:96]))
                for j in range(2):
                    link(dve.tensor_tensor(oh[j], oh[j], cnt, ALU.mult))
                    link(dve.tensor_reduce(pos[:, j, :], oh[j], AX.X, ALU.add))
                p6 = pos.rearrange("p j b -> p (j b)")
                link(dve.tensor_scalar(i_a, p6, float(HALF), None, ALU.is_ge))
                for k in range(2, MAX_ROUNDS):
                    link(dve.tensor_scalar(i_b, p6, float(HALF * k), None, ALU.is_ge))
                    link(dve.tensor_tensor(i_a, i_a, i_b, ALU.add))
                link(dve.scalar_tensor_tensor(p6, i_a, float(HALF * (N_EXP - 1)), p6, ALU.mult, ALU.add))
                for j in range(2):
                    link(dve.scalar_tensor_tensor(srel[:, j, :], top_f[:, :, j], float(HALF), pos[:, j, :], ALU.mult, ALU.add))
                STEPS = 8

                def places(q, v, first=False, second=False):
                    if not first:
                        dve.wait_ge(M("place_steps"), q * STEPS)
                    if not first and not second:
                        dve.wait_ge(M("xs_ps"), q * 2 - 2)
                        dve.wait_ge(M("weights_ps"), q - 1)
                    for b in range(NB):
                        for j, to in ((0, PW[v]), (1, PTMP)):
                            dve.tensor_scalar(to[:, b, :], iota[:, :], srel[:, j, b:b + 1], gates[:, j, b:b + 1],
                                              ALU.is_equal, ALU.mult).then_inc(M("place_steps"), 1)
                    dve.wait_ge(M("place_steps"), q * STEPS + 6)
                    dve.tensor_tensor(PW[v], PW[v], PTMP, ALU.add).then_inc(M("place_steps"), 1)
                    dve.tensor_scalar(srel, srel, float(-P), None, ALU.add).then_inc(M("place_steps"), 1)
                    dve.wait_ge(M("place_steps"), q * STEPS + 7)
                    dve.tensor_scalar(PP[v], PW[v], 0.0, None, ALU.not_equal).then_inc(M("places_ready"), 1)

                def hidden(q, v, first=False, second=False):
                    dve.wait_ge(M("gated"), q + 1)
                    if not first and not second:
                        dve.wait_ge(M("hidden_ps"), q - 1)
                    dve.tensor_tensor(HID[v], SGM[v], psum[:, 2, 256:512], ALU.mult).then_inc(M("hidden"), 1)
                    dve.wait_ge(M("hidden_ps"), q + 1)
                    if not first and not second:
                        dve.wait_ge(M("down"), q * 2 - 2)
                    dve.tensor_copy(HTS[v].rearrange("p k s -> p (k s)"), psum[:, 3, 0:256]).then_inc(M("hidden_t"), 1)

                def add_back(q, first=False):
                    for c in range(6):
                        b, n = divmod(c, 2)
                        dve.wait_ge(M("back_ps"), q * 6 + c + 1)
                        if not first and c == 0:
                            dve.wait_ge(M("added"), q * 6)
                        acc = ACC[:, b, n * 512:(n + 1) * 512]
                        dve.tensor_tensor(acc, acc, bank((6, 7, 4, 5, 6, 7)[c]), ALU.add).then_inc(M("added"), 1)

                def split(q):
                    dve.wait_ge(M("weights_sb"), q + 1)
                    dve.tensor_scalar(PPT, PWT, 0.0, None, ALU.not_equal).then_inc(M("slots_t"), 1)
                    dve.wait_ge(M("y_sb"), q * 2 + 2)
                    dve.tensor_copy(Y_HI, Y).then_inc(M("y_split"), 1)
                    dve.wait_ge(M("y_split"), q * 2 + 1)
                    dve.tensor_tensor(Y_LO, Y, Y_HI, ALU.subtract).then_inc(M("y_split"), 1)

                def pair(q, v, first=False, second=False):
                    places(q + 1, 1 - v, second=first)
                    hidden(q, v, first, second)
                    if not first:
                        add_back(q - 1, second)
                    split(q)

                places(0, 0, first=True)
                dve.wait_ge(S("counts_ps"), 2 * l + 2)
                link(dve.tensor_reduce(n_max, psum[:, 7, 0:32], AX.X, ALU.max))
                for k in range(1, MAX_ROUNDS):
                    link(dve.tensor_scalar(n_tmp[:, k - 1:k], n_max, float(HALF * k), None, ALU.is_gt))
                link(dve.tensor_reduce(n_rounds, n_tmp, AX.X, ALU.add))
                dve.tensor_copy(rounds.bitcast(U32), n_rounds).then_inc(S("rounds_ready"), 1)
                pair(0, 0, first=True)
                pair(1, 1, second=True)
                R = rounds_of(dve, l)
                with dve.Fori(1, R * (PAIRS // 2)) as i:
                    for v in range(2):
                        pair(i * 2 + v, v)
                add_back(R * PAIRS - 1)
                dve.wait_ge(M("added"), R * (PAIRS * 6))
                dve.wait_ge(M("x_sb"), R * (PAIRS * 2) + 2)
                dve.wait_ge(S("gate_in"), 16 * (u + 1))
                for b in range(NB):
                    link(dve.tensor_tensor(UPD_M[b % 2], ACC[:, b, :], GT[:, min(b, 1), :], ALU.mult))
                    dve.tensor_tensor(X[:, b, :], X[:, b, :], UPD_M[b % 2], ALU.add).then_inc(S("x_updated"), 1)

            experts(0)

            norm(2)
            ht_copies(2)
            dve.wait_ge(S("odd_small"), 16 * 5)
            for n in range(3):
                heads_ = KV_HEADS if n == 2 else 4
                dve.wait_ge(S("qkv_ready"), NB * (n + 1))
                if n > 0:
                    dve.wait_ge(S("qk_normed"), n)

                def by_head(v, b=NB):
                    return v.rearrange("p (b h n) -> p b h n", b=b, h=heads_)

                heads = QKV[:, :, n * 512:n * 512 + heads_ * HD].rearrange("p b (h n) -> p b h n", h=heads_)
                sq = by_head(SQ_QK[:, 0:NB * heads_ * HD])
                link(dve.tensor_tensor(sq, heads, heads, ALU.mult))
                link(dve.tensor_reduce(q_ms[n], SQ_QK[:, 0:NB * heads_ * HD].rearrange("p (i n) -> p i n", n=HD), AX.X, ALU.add))
                dve.tensor_scalar(q_ms[n], q_ms[n], 1.0 / HD, EPS, ALU.mult, ALU.add).then_inc(S("mean_squares"), 1)
                inverse_root(f"qk_{n}", q_ms[n], q_rs[n], q_rt[n])
                shape = [P, NB, heads_, HD]
                gain = (GK if n == 2 else GQ).rearrange("p (b h n) -> p b h n", b=1, h=1).broadcast_to(shape)
                link(dve.tensor_tensor(heads, heads, by_head(q_rs[n]).broadcast_to(shape), ALU.mult))
                link(dve.tensor_tensor(heads, heads, gain, ALU.mult))
                x1, x2 = heads[:, 1:3, :, 0:HD:2], heads[:, 1:3, :, 1:HD:2]
                cos, sin = (ROPE[:, :, i, :].rearrange("p b (h n) -> p b h n", h=1).broadcast_to([P, 2, heads_, HD // 2]) for i in range(2))
                t1, t2, t3, t4 = (by_head(t[:, 0:heads_ * HD], 2) for t in ROPE_TMP)
                dve.tensor_tensor(t1, x1, cos, ALU.mult)
                dve.tensor_tensor(t2, x2, sin, ALU.mult)
                dve.tensor_tensor(t3, x1, sin, ALU.mult)
                link(dve.tensor_tensor(t4, x2, cos, ALU.mult))
                dve.tensor_tensor(x1, t1, t2, ALU.subtract)
                dve.tensor_tensor(x2, t3, t4, ALU.add).then_inc(S("qk_normed"), 1)

            def score_max(i):
                dve.wait_ge(S("att_scores_ps"), i + 1)
                link(dve.tensor_reduce(att_max[:, i, :], psum[:, 0:4, 0:P if i < 2 else 3 * P], AX.X, ALU.max))
                dve.tensor_scalar(att_max[:, i, :], att_max[:, i, :], -HD ** -0.5, None, ALU.mult).then_inc(S("max_ready"), 1)

            score_max(0)
            for i in range(6):
                n = P if i < 2 else 3 * P
                blocks_ = n // P
                dve.wait_ge(S("exps_ready"), i + 1)
                link(dve.reciprocal(att_sum[:, i, :], att_sum[:, i, :]))
                pr = PR[i % 2][:, :, 0:n]
                inv = att_sum[:, i, :].rearrange("p (h o) -> p h o", o=1).broadcast_to([P, 4, n])
                dve.tensor_tensor(pr, pr, inv, ALU.mult).then_inc(S("probs_ready"), 1)
                if i < 5:
                    score_max(i + 1)
                dve.wait_ge(S("probs_turned"), i + 1)
                if i >= 1:
                    dve.wait_ge(S("probs_t_used"), i)
                dve.tensor_copy(PT[:, 0:blocks_, :], psum[:, 4:4 + blocks_, :]).then_inc(S("probs_t_ready"), 1)
            update(2, "odd_out_ps", lambda c: c, UPD_O)
            experts(1)
            norm(4)


_INS = ["x_prompt", "x_sample", "state_gla", "cache_k", "cache_v", "c", "c_ctx", "w_mod", "b_mod", "norm1_g", "norm2_g",
        "w_in_even", "w_gate_up", "b_gate_up", "gla_norm_g", "w_spatial", "b_spatial", "w_out_even", "w_in_odd", "q_norm_g",
        "k_norm_g", "w_out_odd", "w_router_group", "b_router_group", "w_router_expert", "b_router_expert", "w_exp_gate",
        "w_exp_up", "w_exp_down", "final_norm_g"]
_OUTS = {"y_prompt": (1, 128, 1024), "y_sample": (1, 256, 1024), "new_state_gla": (1, 1, 2, 4, 64, 128),
         "new_cache_k": (1, 1, 128, 2, 128), "new_cache_v": (1, 1, 128, 2, 128)}


def kernel(**inputs):
    import concourse.bacc as _bacc
    from concourse.bass_utils import run_bass_kernel_spmd as _run

    nc = _bacc.Bacc("TRN2", target_bir_lowering=False, num_devices=1)
    arrays = {f"in_{n}": np.ascontiguousarray(inputs[n]) for n in _INS}
    arrays.update({f"in_{n}": a for n, a in shape_constants().items()})
    d = {n[3:]: nc.dram_tensor(n, a.shape, mybir.dt.from_np(a.dtype), kind="ExternalInput").ap() for n, a in arrays.items()}
    outs = {n: nc.dram_tensor(f"out_{n}", s, F32, kind="ExternalOutput").ap() for n, s in _OUTS.items()}
    build(nc, d, outs)
    r = _run(nc, [arrays], core_ids=[0])
    return tuple(r.results[0][f"out_{n}"] for n in _OUTS)
```

```python
from contextlib import ExitStack

import numpy as np

import concourse.bass as bass
from concourse import mybir

P = 128
D = 1024
KC = D // P
NB = 3
T = NB * P
EPS = 1e-6
COLS = 512
RING = 6
GLA_HEADS, GLA_DK, GLA_DV, GLA_RANK = 4, 64, 128, 16
GLA_TAU = 16.0
QK_W = GLA_HEADS * GLA_DK
V_W = GLA_HEADS * GLA_DV
GROUPS = 4
ATT_HEADS, KV_HEADS, HD = 8, 2, 128
N_EXP, PER_GROUP, MOE_GROUPS = 32, 8, 4
F_EXP = D // 4
PAIRS = N_EXP // 2
HALF = 64
MAX_ROUNDS = T // HALF
GRID_W = 64
BIG = 1e30

ALU = mybir.AluOpType
ACT = mybir.ActivationFunctionType
AX = mybir.AxisListType
F32 = mybir.dt.float32
U32 = mybir.dt.uint32
U8 = mybir.dt.uint8
F32R = mybir.dt.float32r
LEVELS = [64, 32, 16, 8, 4, 2, 1]


def shape_constants():
    i = np.arange(P)
    masks = np.zeros((P, len(LEVELS), P), np.float32)
    for n, m in enumerate(LEVELS):
        same = (i[:, None] // (2 * m)) == (i[None, :] // (2 * m))
        other = (i[:, None] // m) != (i[None, :] // m)
        masks[:, n, :] = same & other
    pick = np.zeros((P, 4 + 2 * 32), np.float32)
    for j in range(4):
        for m in range(4):
            pick[32 * j + m, m] = 1.0
    for r in range(32):
        pick[[r, 32 + r], 4 + 2 * r:6 + 2 * r] = 1.0
    n_freq = HD // 4
    t = np.arange(2 * P)
    inv = (10000.0 ** (-np.arange(n_freq, dtype=np.float32) / n_freq)).astype(np.float32)
    row = (t // GRID_W).astype(np.float32)[:, None] * inv
    col = (t % GRID_W).astype(np.float32)[:, None] * inv
    ang = np.concatenate([row, col], axis=-1)
    rope = np.stack([np.cos(ang), np.sin(ang)], axis=1).astype(np.float32)
    rope = np.ascontiguousarray(rope.reshape(2, P, 2, HD // 2).transpose(1, 0, 2, 3))
    return {
        "k_ident": np.eye(P, dtype=np.float32),
        "k_before": (i[:, None] < i[None, :]).astype(np.float32),
        "k_iota": np.broadcast_to(i.astype(np.float32), (P, P)).copy(),
        "k_masks": masks,
        "k_pick": pick,
        "k_rope": rope,
    }


MOD_GROUPS = {
    "front": [(0, 0), (0, 1), (0, 4)],
    "even": [(0, 2)],
    "gate": [(0, 3)],
    "norm_1": [(0, 5)],
    "router": [(1, 0)],
    "places": [(1, 1)],
    "norm_2": [(1, 2), (1, 4)],
    "attention": [(1, 3)],
    "norm_3": [(1, 5)],
}
MODS = [m for group in MOD_GROUPS.values() for m in group]
FRONT = len(MOD_GROUPS["front"])
FRONT_BANKS = [(2, 4), (3, 5), (6, 7)]
MOD_BANKS = {"even": (4, 4), "gate": (7, 7), "norm_1": (4, 5), "router": (4, 5), "places": (4, 5), "norm_2": (2, 3), "attention": (2, 3), "norm_3": (6, 7)}
EVEN_PLAN = ["part", "g0", "sum", "g1", 0, "g2", 1, "vg0", 2, "vg1", 3, "vg2", 4, "u0", 5, "u1", 6, "u2", 7]


def mods(group):
    start = 0
    for name, chunks in MOD_GROUPS.items():
        if name == group:
            return range(start, start + len(chunks))
        start += len(chunks)


def group_of(i):
    return next(name for name in MOD_GROUPS if i in mods(name))


def weight_chunks():
    def of(group):
        return [("mod", 2 * i + half) for i in mods(group) for half in range(2)]

    first = of("front") + [("even_in", 0), ("even_in", 1)]
    even = iter(of("even"))
    for step in EVEN_PLAN:
        if step == "part":
            first += [next(even), next(even)]
        elif step in ("g0", "vg0", "u0"):
            first.append(("even_in", {"g0": 2, "vg0": 3, "u0": 4}[step]))
    first += of("gate") + [("even_out", n) for n in range(2)] + of("norm_1") + of("router") + of("places")
    second = of("norm_2") + [("odd_in", n) for n in range(3)] + of("attention") + [("odd_out", n) for n in range(2)] + of("norm_3")
    return first, second


FIRST, SECOND = weight_chunks()
CHUNKS = FIRST + SECOND
ROOTS = ["norm_0", "ln", "gla", "norm_1", "norm_2", "qk_0", "qk_1", "qk_2", "norm_3", "norm_4"]
TURNS = [0, "cat", 1, 2, 3]
EVEN_COLS = [0, 2 * QK_W, 2 * QK_W + V_W, 2 * QK_W + 2 * V_W + 2 * GLA_RANK + 512, 2 * QK_W + 2 * V_W + 2 * GLA_RANK]
A_COL = 2 * QK_W + 2 * V_W


def slot_of(j):
    return (j - len(FIRST)) % RING


def scaled(i):
    return MODS[i][1] in (1, 4)


def fills_of(j):
    return sum(slot_of(i) == slot_of(j) for i in range(j + 1))


def last_in(slot, upto):
    return max(j for j in range(upto) if slot_of(j) == slot)


def build(nc, d, outs):
    ctx = ExitStack()
    sems = {}

    def S(name):
        if name not in sems:
            sems[name] = ctx.enter_context(nc.semaphore(name))
        return sems[name]

    address = {}

    def sb(name, cols, dt=F32, parts=P):
        address[name] = (nc.sbuf_base + 31) // 32 * 32
        return ctx.enter_context(nc.sbuf_tensor(name, [parts, cols], dt))

    with ctx:
        ring = sb("ring", RING * 4096)
        x_t = sb("x", NB * D)
        h_t = sb("h", NB * D)
        ht_t = sb("ht", KC * T)
        gs_t = sb("shift_scale", 4 * D)
        gt_t = sb("gate_rows", 2 * D)
        ar = sb("arena", 11264)
        ident = sb("ident", P)
        before = sb("before", P)
        iota = sb("iota", P)
        masks = sb("masks", len(LEVELS) * P, U8)
        ones = sb("ones", P)
        pick = sb("pick", 4 + 2 * 32)
        mod_bias = sb("mod_bias", COLS, F32R, parts=64)
        pick_bias = sb("pick_bias", 2 * 32, F32R, parts=64)
        cond_t = sb("cond_silu", KC * 34)
        small = sb("small", 264)
        psum = ctx.enter_context(nc.psum_tensor("psum", [P, 8, 512], F32))
        mod_rows = nc.dram_tensor("mod_rows", (2, 6, 2, D), F32, kind="Internal").ap()

        X = x_t[:, :].rearrange("p (b n) -> p b n", b=NB)
        H = h_t[:, :].rearrange("p (b n) -> p b n", b=NB)
        HT = ht_t[:, :].rearrange("p (k t) -> p k t", k=KC)
        GS = gs_t[:, :].rearrange("p (a s n) -> p a s n", a=2, s=2)
        GT = gt_t[:, :].rearrange("p (s n) -> p s n", s=2)
        RC = ring[:, :].rearrange("p (r k n) -> p r k n", r=RING, k=KC)
        RG = ring[:, :].rearrange("p (r e k n) -> p r e k n", r=RING, e=2, k=KC)
        RD = ring[:, :].rearrange("p (r e k n) -> p r e k n", r=RING, e=2, k=2)
        RS = ring[:, :].rearrange("p (r e n) -> p r e n", r=RING, e=2)

        def bank(b):
            return psum[:, b, :]

        def rounded(name, base, col, cols):
            t = nc.alloc_sbuf_tensor_at(name, [P, cols], F32R, offset=address[base] + 4 * col)
            return t[:, :]

        class View:

            def __init__(self, base):
                self.at, self.base = 0, base

            def __call__(self, cols, pattern=None, parts=P, **sizes):
                v = self.base[0:parts, self.at:self.at + cols]
                self.at += cols
                return v.rearrange(pattern, **sizes) if pattern else v

        sm = View(small)
        ss, ms, rs, rt = sm(3), sm(3), sm(3), sm(3)
        b_gate = sm(4)
        b_spat = sm(4)
        gla_ms, gla_rs, gla_rt = sm(12), sm(12), sm(12)
        ln_rs, ln_rt, ln_v = sm(12), sm(12), sm(12)
        dec_f, dec_b = sm(2), sm(2)
        att_max, att_sum = sm(24, "p (i h) -> p i h", i=6), sm(24, "p (i h) -> p i h", i=6)
        q_ms, q_rs, q_rt = ([sm(12), sm(12), sm(6)] for _ in range(3))

        cond_silu = cond_t[:, :].rearrange("p (k m) -> p k m", m=34)
        vm = View(ar)
        mod_part = [vm(COLS) for _ in range(2)]
        front_row = [vm(COLS, parts=4) for _ in range(FRONT)]

        ve = View(ar)
        QK = ve(4 * T, "p (c t) -> p c t", c=4)
        BF = ve(2 * T, "p (c t) -> p c t", c=2)
        BB = ve(2 * T, "p (c t) -> p c t", c=2)
        ATT = ve(12 * P, "p (i t) -> p i t", i=12)
        V = ve(NB * 512, "p (b n) -> p b n", b=NB)
        SG = ve(NB * 512, "p (b n) -> p b n", b=NB)
        VG = ve(NB * 512, "p (b n) -> p b n", b=NB)
        U = ve(NB * 512, "p (b n) -> p b n", b=NB)
        WST = ve(GROUPS * P, "p (g t) -> p g t", g=GROUPS)
        bias_raw = U[0:64, 1, :]
        cond = WST.rearrange("p g t -> p (g t)")[:, 0:KC * 2].rearrange("p (k s) -> p k s", s=2)
        WA = VG[:, 0:1, 0:256].rearrange("p o (k n) -> p (o k) n", k=KC)
        WS_RAW = U[:, 0, :].rearrange("p (g s) -> p g s", g=GROUPS)
        EX = [H[:, :, :].rearrange("p b n -> p (b n)")[:, i * 1536:(i + 1) * 1536].rearrange("p (c t) -> p c t", c=4) for i in range(2)]
        MASKS_F32 = SG.rearrange("p b n -> p (b n)")[:, 0:len(LEVELS) * P]
        vz = View(gs_t)
        Z = vz(4 * T, "p (c t) -> p c t", c=4)
        EZ = vz(4 * T, "p (c t) -> p c t", c=4)
        AT = vz(T, parts=32)
        WGU = vz(512, parts=32)
        GLAG = vz(P)
        v2 = View(gs_t)
        E2 = v2(8 * 256, "p (a c t) -> p a c t", a=4, c=2)
        KDT = v2(8 * P, "p (i t) -> p i t", i=8)
        vs = View(gt_t)
        S0 = vs(1024, "p (a h v) -> p a h v", a=2, h=4)
        S1 = vs(1024, "p (a h v) -> p a h v", a=2, h=4)
        O = ATT.rearrange("p i t -> p (i t)").rearrange("p (b n) -> p b n", b=NB)
        OSQ = QK.rearrange("p c t -> p (c t)")
        ST_OUT = BF.rearrange("p c t -> p (c t)")[:, 0:512].rearrange("p (a c v) -> p a c v", a=2, c=2)
        BN = BB.rearrange("p c t -> p (c t)")[:, 0:12 * 8].rearrange("p (i n) -> p i n", i=12)
        UPD = [QK.rearrange("p c t -> p (c t)")[:, i * 512:(i + 1) * 512] for i in range(2)]

        vo = View(ar)
        QKV = vo(NB * 1536, "p (b n) -> p b n", b=NB)
        KT = vo(KV_HEADS * 4 * P, "p (g b t) -> p g b t", g=KV_HEADS, b=4)
        CK = vo(256)
        CV = vo(256)
        ROPE = vo(256, "p (b c n) -> p b c n", b=2, c=2)
        GQ, GK = vo(P), vo(P)
        PR0 = vo(1536)
        SQ_QK = vo(1536)
        ROPE_TMP = [SQ_QK[:, 0:512], SQ_QK[:, 512:1024], PR0[:, 0:512], PR0[:, 512:1024]]
        UPD_O = ROPE_TMP[0:2]
        QT = H[:, :, :].rearrange("p b n -> p (b n)").rearrange("p (h t) -> p h t", h=8)
        vg_ = View(gs_t)
        PR = [PR0.rearrange("p (h n) -> p h n", h=4), vg_(1536, "p (h n) -> p h n", h=4)]
        PT = vg_(1536, "p (k n) -> p k n", k=3)
        OT = HT

        vx = View(ar)
        XT = vx(KC * P, "p (k s) -> p k s", k=KC)
        XS = vx(D)
        Y_LO = rounded("y_low", "arena", vx.at, D)
        Y = vx(D)
        Y_HI = rounded("y_top", "arena", vx.at, D)
        vx(D)
        SGM = [vx(256) for _ in range(2)]
        HID = [vx(256) for _ in range(2)]
        HTS = [vx(256, "p (k s) -> p k s", k=2) for _ in range(2)]
        WR = vx(KC * 36, "p (k n) -> p k n", k=KC)
        BR = vx(8)[0:36, 0:1]
        PW = [vx(NB * P, "p (b s) -> p b s", b=NB) for _ in range(2)]
        PP = [rounded(f"places_{v}", "arena", vx.at + v * NB * P, NB * P).rearrange("p (b s) -> p b s", b=NB) for v in range(2)]
        vx(2 * NB * P)
        PTMP = vx(NB * P, "p (b s) -> p b s", b=NB)
        PWT = vx(NB * P, "p (b t) -> p b t", b=NB)
        PPT = rounded("slots_t", "arena", vx.at, NB * P).rearrange("p (b t) -> p b t", b=NB)
        vx(NB * P)
        w_slot = vx(1)
        LT = vx(T, parts=36)
        LG = vx(NB * 36, "p (b n) -> p b n", b=NB)
        g_max, g_idx, g_sum, g_prob = vx(3), vx(3), vx(3), vx(3)
        g_tmp = vx(12, "p (b n) -> p b n", b=NB)
        e_mask = vx(NB * 32, "p (b n) -> p b n", b=NB)
        top_v = vx(NB * 8, "p (b n) -> p b n", b=NB)
        top_i = vx(NB * 8, "p (b n) -> p b n", b=NB)
        top_f = vx(NB * 2, "p (b n) -> p b n", b=NB)
        gates = vx(6, "p (j b) -> p j b", j=2)
        oh = [vx(NB * 32, "p (b n) -> p b n", b=NB) for _ in range(2)]
        oh_sum = vx(NB * 32, "p (b n) -> p b n", b=NB)
        cnt = vx(NB * 32, "p (b n) -> p b n", b=NB)
        pos = vx(6, "p (j b) -> p j b", j=2)
        i_a = vx(6)
        passed = vx(6 * (MAX_ROUNDS - 1), "p (i k) -> p i k", i=6)
        srel = vx(6, "p (j b) -> p j b", j=2)
        n_max, n_rounds, n_tmp = vx(1), vx(1), vx(5)
        rounds = vx(1)
        H_HI = rounded("h_top", "shift_scale", 0, NB * D).rearrange("p (b n) -> p b n", b=NB)
        H_LO = rounded("h_low", "h", 0, NB * D).rearrange("p (b n) -> p b n", b=NB)
        ACC = ht_t[:, :].rearrange("p (b n) -> p b n", b=NB)
        UPD_M = [XT.rearrange("p k s -> p (k s)"), XS]
        iota32 = iota[:, 0:32]

        def col_src(j):
            name, n = CHUNKS[j]
            if name == "mod":
                l, part = MODS[n // 2]
                c = 2 * part + n % 2
                return d["w_mod"][l].rearrange("(p k) n -> p k n", k=KC)[:, :, c * COLS:(c + 1) * COLS]
            if name == "even_in":
                c = EVEN_COLS[n]
                return d["w_in_even"][0].rearrange("(p k) n -> p k n", k=KC)[:, :, c:c + COLS]
            if name == "even_out":
                return d["w_out_even"][0].rearrange("(p k) n -> p k n", k=KC)[:, :, n * COLS:(n + 1) * COLS]
            if name == "odd_in":
                return d["w_in_odd"][0].rearrange("(p k) n -> p k n", k=KC)[:, :, n * COLS:(n + 1) * COLS]
            return d["w_out_odd"][0].rearrange("(k p) n -> p k n", k=KC)[:, :, n * COLS:(n + 1) * COLS]

        def rest_buffers(i):
            slot = slot_of(CHUNKS.index(("mod", 2 * i + 1)))
            return RC[:, slot, 0, :], RC[0:4, slot, 1, :], RC[0:4, slot, 2, :]

        def rounds_of(eng, l):
            eng.wait_ge(S("rounds_ready"), l + 1)
            return eng.value_load(rounds[0:1, 0:1].bitcast(U32), min_val=0, max_val=MAX_ROUNDS - 1) + 1

        def used_up(eng, j):
            name, n = CHUNKS[j]
            if name == "mod" and (n < 2 * FRONT or n % 2 == 0):
                eng.wait_ge(S("mod_part_ps"), n + 1)
            elif name == "mod":
                eng.wait_ge(S("rest_stored"), 32 * (n // 2 - FRONT + 1))
            elif name == "even_in":
                eng.wait_ge(S(("qk_ps", "v_ps", "g_ps", "vg_ps", "u_ps")[n]), (4, 3, 3, 3, 3)[n])
            elif name == "even_out":
                eng.wait_ge(S("even_out_ps"), NB * (n + 1))
            elif name == "odd_in":
                eng.wait_ge(S("odd_in_ps"), (3, 6, 12)[n])
            else:
                eng.wait_ge(S("odd_out_ps"), NB * (n + 1))

        block = ctx.enter_context(nc.Block())

        @block.sync
        def _(sp):
            def load_chunk(j):
                sp.dma_start(RC[:, slot_of(j)], col_src(j)).then_inc(S(f"chunk_in_{slot_of(j)}"), 16)

            def load_experts(l, a, first_expert, slot):
                w = d[("w_exp_gate", "w_exp_up", "w_exp_down")[a]][l].rearrange("e (p k) n -> p e (k n)", p=P)
                sp.dma_start(RS[:, slot], w[:, bass.ds(first_expert, 2), :]).then_inc(S(f"moe{l}_in_{slot}"), 16)

            with nc.allow_non_contiguous_dma(reason="small vectors by channel"):
                sp.dma_start(cond[:, :, 0:1].rearrange("p k s -> p (k s)"), d["c_ctx"].rearrange("(p k) -> p k", k=KC)).then_inc(S("cond_in"), 16)
                sp.dma_start(cond[:, :, 1:2].rearrange("p k s -> p (k s)"), d["c"][0].rearrange("(p k) -> p k", k=KC)).then_inc(S("cond_in"), 16)
            load_chunk(0)
            sp.dma_start(pick[:, :], d["k_pick"]).then_inc(S("mod_small"), 16)
            for r in (0, 32):
                sp.dma_start(bias_raw[r:r + 24, :], d["b_mod"].rearrange("l (n c) -> (l n) c", c=COLS)).then_inc(S("mod_small"), 16)
                for part in range(2):
                    gains = d[("norm1_g", "norm2_g")[part]].rearrange("l (h c) -> (l h) c", c=COLS)
                    sp.dma_start(bias_raw[r + 24 + 4 * part:r + 28 + 4 * part, :], gains).then_inc(S("mod_small"), 16)
            for j in range(1, len(FIRST)):
                if j == 4:
                    sp.dma_start(X[:, 0, :], d["x_prompt"][0]).then_inc(S("x_loaded"), 16)
                    sp.dma_start(X[:, 1:3, :], d["x_sample"][0].rearrange("(b p) n -> p b n", p=P)).then_inc(S("x_loaded"), 16)
                if j >= RING:
                    used_up(sp, j - RING)
                load_chunk(j)

            def experts(l, before_first):
                for u in range(2):
                    for a in range(3):
                        before_first(3 * u + a)
                        load_experts(l, a, 2 * u, 3 * u + a)
                R = rounds_of(sp, l)
                with sp.Fori(1, R * (PAIRS // 2)) as i:
                    for u in range(2):
                        first_expert = sp.snap(((i * 2 + u) % PAIRS) * 2)
                        multiplied = sp.snap(i * 2 + (u - 1))
                        down_multiplied = sp.snap(i * 4 + (2 * u - 2))
                        sp.wait_ge(S(f"moe{l}_gate_up"), multiplied)
                        sp.sem_inc(S("slots_freed"), 1)
                        load_experts(l, 0, first_expert, 3 * u)
                        load_experts(l, 1, first_expert, 3 * u + 1)
                        sp.wait_ge(S(f"moe{l}_down"), down_multiplied)
                        sp.sem_inc(S("slots_freed"), 1)
                        load_experts(l, 2, first_expert, 3 * u + 2)
                return R

            R = experts(0, lambda slot: used_up(sp, last_in(slot, len(FIRST))))
            sp.wait_ge(S("moe0_gate_up"), R * PAIRS - 1)
            for j in range(2):
                load_chunk(len(FIRST) + j)
            sp.wait_ge(S("moe0_down"), R * (2 * PAIRS) - 2)
            load_chunk(len(FIRST) + 2)
            sp.wait_ge(S("moe0_gate_up"), R * PAIRS)
            for j in range(3, 5):
                load_chunk(len(FIRST) + j)
            sp.wait_ge(S("moe0_down"), R * (2 * PAIRS))
            load_chunk(len(FIRST) + 5)
            for j in range(RING, len(SECOND)):
                used_up(sp, len(FIRST) + j - RING)
                load_chunk(len(FIRST) + j)

            experts(1, lambda slot: used_up(sp, last_in(slot, len(CHUNKS))))

        @block.gpsimd
        def _(pool):
            def load(dst, src, sem="consts"):
                pool.dma_start(dst, src).then_inc(S(sem), 16)

            def load_rows(u, part, dst, sem):
                n = dst.shape[1]
                l = u // 2
                src = mod_rows[l, 3 * (u % 2) + part[0]:3 * (u % 2) + part[1]].rearrange("a s n -> (a s n)")
                pool.dma_start(dst, src.rearrange("(o n) -> o n", o=1).broadcast_to([P, n])).then_inc(S(sem), 16)

            load(ident[:, :], d["k_ident"])
            load(before[:, :], d["k_before"])
            load(iota[:, :], d["k_iota"])
            load(MASKS_F32, d["k_masks"].rearrange("p l t -> p (l t)"), "even_first")
            def load_router(l):
                with nc.allow_non_contiguous_dma(reason="router weights"):
                    load(WR[:, :, 0:4], d["w_router_group"][l].rearrange("(p k) n -> p k n", k=KC), "router_in")
                    load(WR[:, :, 4:36], d["w_router_expert"][l].rearrange("(p k) n -> p k n", k=KC), "router_in")
                    load(BR[0:4, :], d["b_router_group"][l].rearrange("(n o) -> n o", o=1), "router_in")
                    load(BR[4:36, :], d["b_router_expert"][l].rearrange("(n o) -> n o", o=1), "router_in")

            with nc.allow_non_contiguous_dma(reason="small vectors by channel"):
                load(b_gate, d["b_gate_up"][0].rearrange("a (c p) -> p (a c)", p=P))
                load(b_spat, d["b_spatial"][0].rearrange("g t -> t g"))

            def store_mod(i, rows, sem):
                l, part = MODS[i]
                for half in range(2):
                    pool.dma_start(mod_rows[l, part, :, half * COLS:(half + 1) * COLS], rows[2 * half:2 * half + 2, :]).then_inc(S(sem), 16)

            load(WA, d["w_in_even"][0].rearrange("(p k) n -> p k n", k=KC)[:, :, A_COL:A_COL + 2 * GLA_RANK], "even_first")
            load(WS_RAW, d["w_spatial"][0].rearrange("g t s -> t g s"), "even_first")
            pool.memset(S0.rearrange("p a h v -> p (a h v)"), 0.0).then_inc(S("pool_steps"), 1)
            pool.memset(S1.rearrange("p a h v -> p (a h v)"), 0.0).then_inc(S("pool_steps"), 1)
            pool.wait_ge(S("pool_steps"), 2)
            for a in range(2):
                for h in range(GLA_HEADS):
                    r = 64 * (h % 2)
                    load(S0[r:r + 64, a, h, :], d["state_gla"][0, 0, a, h], "state_in")
            for i in range(2, FRONT):
                pool.wait_ge(S("front_row_ready"), i + 1)
                store_mod(i, front_row[i], "front_stored")

            pool.wait_ge(S("h_ready"), NB)
            pool.memset(WGU, 0.0).then_inc(S("pool_steps"), 1)
            pool.wait_ge(S("pool_steps"), 3)
            for a in range(2):
                load(WGU[a * GLA_RANK:(a + 1) * GLA_RANK, a * QK_W:(a + 1) * QK_W], d["w_gate_up"][0, a], "even_small")
            load(GLAG, d["gla_norm_g"][0].rearrange("(o n) -> o n", o=1).broadcast_to([P, P]), "even_small")

            def store_rest(group):
                for i in mods(group):
                    pool.wait_ge(S("rest_row_ready"), i - FRONT + 1)
                    _, rows, gains = rest_buffers(i)
                    if scaled(i):
                        pool.tensor_tensor(rows, rows, gains, ALU.mult).then_inc(S("pool_steps"), 1)
                        pool.wait_ge(S("pool_steps"), 3 + sum(scaled(k) for k in range(FRONT, i + 1)))
                    store_mod(i, rows, "rest_stored")
                    pool.wait_ge(S("rest_stored"), 32 * (i - FRONT + 1))

            store_rest("even")
            pool.wait_ge(S("states_ready"), 1)
            for a in range(2):
                for hh in range(2):
                    dst = outs["new_state_gla"][0, 0, a, hh::2].rearrange("c d v -> d c v")
                    pool.dma_start(dst, ST_OUT[64 * hh:64 * hh + 64, a]).then_inc(S("stored"), 16)
            pool.wait_ge(S("gla_out"), 3)
            load_rows(0, (2, 3), gt_t[:, :], "gate_in")
            load_router(0)
            pool.wait_ge(S("gla_gain_ready"), 1)
            store_rest("gate")
            load_rows(1, (0, 2), gs_t[:, :], "rows_in")

            def experts(l):
                u = 2 * l + 1
                store_rest(f"norm_{u}")
                pool.wait_ge(S("turned"), 6 * (TURNS.index(u) + 1))
                pool.wait_ge(S("h_top"), l + 1)
                pool.tensor_tensor(H_LO, H, H_HI, ALU.subtract).then_inc(S("h_split"), 1)
                if l == 0:
                    store_rest("router")
                    store_rest("places")
                pool.wait_ge(S("x_updated"), NB * u)
                load_rows(u, (2, 3), gt_t[:, :], "gate_in")
                R = rounds_of(pool, l)
                pool.wait_ge(S(f"moe{l}_xs_ps"), R * (PAIRS * 2) + 2)
                pool.sem_inc(S("rows_free"), 1)

            experts(0)
            load_rows(2, (0, 2), gs_t[:, :], "rows_in")
            store_rest("norm_2")
            pool.wait_ge(S("x_updated"), NB * 2)
            load(CK, d["cache_k"][0, 0].rearrange("t g n -> t (g n)"), "odd_small")
            load(CV, d["cache_v"][0, 0].rearrange("t g n -> t (g n)"), "odd_small")
            load(ROPE, d["k_rope"], "odd_small")
            load(GQ, d["q_norm_g"][0].rearrange("(o n) -> o n", o=1).broadcast_to([P, P]), "odd_small")
            load(GK, d["k_norm_g"][0].rearrange("(o n) -> o n", o=1).broadcast_to([P, P]), "odd_small")
            store_rest("attention")
            load_rows(2, (2, 3), gt_t[:, :], "gate_in")
            pool.wait_ge(S("qk_normed"), 3)
            pool.wait_ge(S("qkv_ready"), 12)
            pool.dma_start(outs["new_cache_k"][0, 0].rearrange("t g n -> t (g n)"), QKV[:, 0, 1024:1280]).then_inc(S("stored"), 16)
            pool.dma_start(outs["new_cache_v"][0, 0].rearrange("t g n -> t (g n)"), QKV[:, 0, 1280:1536]).then_inc(S("stored"), 16)
            pool.wait_ge(S("probs_t_used"), 6)
            load_rows(3, (0, 2), gs_t[:, :], "rows_in")
            load_router(1)
            pool.wait_ge(S("stored"), 16 * 6)
            experts(1)
            load(GS[:, 0, 0, :], d["final_norm_g"].rearrange("(o n) -> o n", o=1).broadcast_to([P, D]), "rows_in")
            for b in range(NB):
                pool.wait_ge(S("h_ready"), NB * 4 + b + 1)
                dst = outs["y_prompt"][0] if b == 0 else outs["y_sample"][0, (b - 1) * P:b * P]
                pool.dma_start(dst, H[:, b, :]).then_inc(S("stored"), 16)
            pool.wait_ge(S("stored"), 16 * 9)

        @block.tensor
        def _(pe):
            def chunk(name, n):
                j = CHUNKS.index((name, n))
                pe.wait_ge(S(f"chunk_in_{slot_of(j)}"), 16 * fills_of(j))
                return RC[:, slot_of(j)]

            def turn(b, ready, count):
                pe.wait_ge(S(ready), count)
                for half in range(2):
                    for kk in range(4):
                        t = pe.transpose(psum[:, 2 * b + half, kk * P:(kk + 1) * P], H[:, b, 4 * half + kk:D:KC], ident[:, :])
                    t.then_inc(S("turned"), 1)

            def transposed(u, b=NB - 1):
                for half in ("top", "low"):
                    pe.wait_ge(S(f"ht_{half}"), NB * TURNS.index(u) + b + 1)

            def project(to, b, w, cols=COLS):
                for k in range(KC):
                    mm = pe.matmul(psum[:, to, 0:cols], HT[:, k, b * P:(b + 1) * P], w[:, k, :], start=(k == 0), stop=(k == KC - 1))
                return mm

            def turn_and_project(u, ready, counts, w, sem):
                turn(0, ready, counts[0])
                turn(1, ready, counts[1])
                for b in range(NB):
                    transposed(u, b)
                    project((6 + b) % 8, b, w).then_inc(S(sem), 1)
                    if b == 0:
                        turn(2, ready, counts[2])

            def mod_products(i):
                if i < FRONT:
                    to = i % 2
                    if i >= 2:
                        pe.wait_ge(S("mod_part_sb"), i - 1)
                else:
                    to, sum_bank = MOD_BANKS[group_of(i)]
                    pe.wait_ge(S("mod_part_sb"), i)
                    if (to == sum_bank or scaled(i - 1)) and i > FRONT:
                        pe.wait_ge(S("rest_row_ready"), i - FRONT)
                for half in range(2):
                    w = chunk("mod", 2 * i + half)
                    for r in range(2):
                        for j in range(4):
                            k = 4 * r + j
                            mm = pe.matmul(psum[32 * j:32 * j + 32, to, :], cond_silu[:, k, 2 - 2 * half:34 - 2 * half], w[:, k, :],
                                           start=(half == 0 and r == 0), stop=(half == 1 and r == 1))
                    mm.then_inc(S("mod_part_ps"), 1)

            def mod_sum(i):
                l, part = MODS[i]
                bias = 12 * l + 2 * part
                gain = 24 + 4 * (part // 3) + 2 * l
                pe.wait_ge(S("mod_part_sb"), i + 1)
                if i < FRONT:
                    (to, gain_bank), parts = FRONT_BANKS[i], mod_part[i % 2]
                else:
                    gain_bank, to = MOD_BANKS[group_of(i)]
                    parts = rest_buffers(i)[0]
                    if i > FRONT:
                        pe.wait_ge(S("rest_row_ready"), i - FRONT)
                if scaled(i):
                    pe.matmul(psum[0:4, gain_bank, :], pick_bias[:, 2 * gain:2 * gain + 4], mod_bias[:, :], start=True, stop=True)
                pe.matmul(psum[0:4, to, :], pick[:, 0:4], parts, start=True, stop=False)
                pe.matmul(psum[0:4, to, :], pick_bias[:, 2 * bias:2 * bias + 4], mod_bias[:, :], start=False, stop=True).then_inc(S("mod_sum_ps"), 1)

            def mod_group(group):
                for i in mods(group):
                    mod_products(i)
                    mod_sum(i)
                pe.wait_ge(S("rest_row_ready"), mods(group)[-1] - FRONT + 1)

            def spread(i):
                pe.wait_ge(S("front_row_ready"), i + 1)
                pe.wait_ge(S("consts"), 16 * 5)
                for r in range(4):
                    c = 4 * i + r
                    if c >= 2:
                        pe.wait_ge(S("spread_sb"), c - 1)
                    pe.matmul(bank(6 + c % 2), ident[0:4, r:r + 1].broadcast_to([4, P]), front_row[i], start=True, stop=True).then_inc(S("spread_ps"), 1)

            pe.wait_ge(S("cond_ready"), 1)
            mod_products(0)
            mod_products(1)
            pe.wait_ge(S("bias_ready"), 2)
            mod_sum(0)
            mod_sum(1)
            spread(0)
            spread(1)
            mod_products(2)
            pe.wait_ge(S("spread_sb"), 8)
            mod_sum(2)

            pe.wait_ge(S("mod_part_sb"), FRONT)
            for b in range(NB):
                turn(b, "h_ready", b + 1)
            transposed(0)
            w = chunk("even_in", 0)
            for c in range(4):
                for k in range(KC):
                    mm = pe.matmul(psum[:, c, 0:T], w[:, k, c * P:(c + 1) * P], HT[:, k, :], start=(k == 0), stop=(k == KC - 1))
                mm.then_inc(S("qk_ps"), 1)
            pe.wait_ge(S("even_first"), 16 * 3)
            for k in range(KC):
                mm = pe.matmul(psum[0:32, 4, 0:T], WA[:, k, :], HT[:, k, :], start=(k == 0), stop=(k == KC - 1))
            mm.then_inc(S("decay_in_ps"), 1)
            pe.wait_ge(S("even_first"), 16 * 3)
            pe.wait_ge(S("front_row_ready"), FRONT)
            for g in range(GROUPS):
                t = pe.transpose(psum[:, 7, g * P:(g + 1) * P], WS_RAW[:, g, :], ident[:, :])
            t.then_inc(S("sides_turned"), 1)
            w = chunk("even_in", 1)
            project(5, 0, w).then_inc(S("v_ps"), 1)
            pe.wait_ge(S("decay_in_ready"), 1)
            pe.wait_ge(S("even_small"), 16 * 3)
            pe.wait_ge(S("qk_ready"), 4)
            for j in range(4):
                pe.matmul(psum[:, j, 0:T], WGU[:, j * P:(j + 1) * P], AT[:, :], start=True, stop=True).then_inc(S("decay_ps"), 1)
            pe.wait_ge(S("spatial_ready"), 1)
            for b in (1, 2):
                project(5 + b, b, w).then_inc(S("v_ps"), 1)

            def scores(n):
                src = QK if n == 0 else EX[(n - 1) % 2]
                if n == 0:
                    pe.wait_ge(S("z_ready"), 4)
                else:
                    pe.wait_ge(S("decayed_ready"), n)
                    pe.wait_ge(S("att_merged"), 2 * n)
                for r in range(2):
                    rows = slice(64 * r, 64 * r + 64)
                    for i in range(6):
                        b, c = divmod(i, 2)
                        mm = pe.matmul(psum[:, 2 * r + i // 4, (i % 4) * P:(i % 4 + 1) * P], src[rows, 2 + c, b * P:(b + 1) * P],
                                       src[rows, c, b * P:(b + 1) * P], start=True, stop=True)
                mm.then_inc(S("scores_ps"), 1)

            mod = FRONT
            for step in EVEN_PLAN:
                if step == "part":
                    mod_products(mod)
                    continue
                if step == "sum":
                    mod_sum(mod)
                    mod += 1
                    continue
                if isinstance(step, int):
                    scores(step)
                    continue
                name, b = step[:-1], int(step[-1])
                before_it = {"g": "v", "vg": "g", "u": "vg"}[name]
                if b == 0:
                    w = chunk("even_in", {"g": 2, "vg": 3, "u": 4}[name])
                pe.wait_ge(S(f"{before_it}_ready"), b + 1)
                project(5 + b, b, w).then_inc(S(f"{name}_ps"), 1)

            pe.wait_ge(S("u_ready"), 3)
            pe.wait_ge(S("rest_row_ready"), len(mods("even")))
            pe.wait_ge(S("to_end_ready"), 1)
            for a in range(2):
                for jc in range(4):
                    t = pe.transpose(psum[:, 4 + a, jc * P:(jc + 1) * P], E2[:, 2 + a, jc % 2, (jc // 2) * P:(jc // 2 + 1) * P], ident[:, :])
            t.then_inc(S("sides_turned"), 1)
            pe.wait_ge(S("kdt_ready"), 1)
            for a in range(2):
                for j in range(2):
                    blk = j if a == 0 else 2 * j
                    for h in range(GLA_HEADS):
                        c, r = divmod(h, 2)
                        mm = pe.matmul(psum[64 * r:64 * r + 64, 6 + a, (2 * j + c) * P:(2 * j + c + 1) * P],
                                       KDT[:, 4 * a + 2 * j + c, 64 * r:64 * r + 64], V[:, blk, h * P:(h + 1) * P], start=True, stop=True)
            mm.then_inc(S("state_ps"), 1)
            pe.wait_ge(S("att_merged"), 16)
            pe.wait_ge(S("states_ready"), 2)
            for b in range(NB):
                for h in range(GLA_HEADS):
                    c, r = divmod(h, 2)
                    to = psum[:, b, h * P:(h + 1) * P]
                    mm = pe.matmul(to, ATT[:, 6 * r + 2 * b + c, :], V[:, b, h * P:(h + 1) * P], start=True, stop=(b == 0))
                    if b > 0:
                        fwd = (S0 if b == 1 else S1)[:, 0, h, :]
                        bwd = (S1 if b == 1 else S0)[:, 1, h, :]
                        pe.matmul(to, E2[:, 0, c, (b - 1) * P:b * P], fwd, start=False, stop=False)
                        mm = pe.matmul(to, E2[:, 1, c, (b - 1) * P:b * P], bwd, start=False, stop=True)
                mm.then_inc(S("gla_out"), 1)
            pe.wait_ge(S("vg_normed"), 1)
            for g in range(GROUPS):
                pe.matmul(psum[:, 3 + g, 0:T], WST[:, g, :], VG[:, :, g * P:(g + 1) * P], start=True, stop=True).then_inc(S("spatial_ps"), 1)
            mod_group("gate")
            turn_and_project("cat", "cat_ready", (1, 1, 1), chunk("even_out", 0), "even_out_ps")
            w = chunk("even_out", 1)
            for b in range(NB):
                project(1 + b, b, w).then_inc(S("even_out_ps"), 1)

            def experts(l):
                u = 2 * l + 1

                def M(name):
                    return S(f"moe{l}_{name}")

                mod_group(f"norm_{u}")
                turn(0, "h_ready", NB * u + 1)
                turn(1, "h_ready", NB * u + 2)
                pe.wait_ge(S("router_in"), 16 * 4 * (l + 1))
                for b in range(NB):
                    transposed(u, b)
                    for k in range(KC):
                        mm = pe.matmul(psum[0:36, 6, b * P:(b + 1) * P], WR[:, k, :], HT[:, k, b * P:(b + 1) * P], start=(k == 0), stop=(k == KC - 1))
                    if b == 0:
                        turn(2, "h_ready", NB * u + 3)
                mm.then_inc(S("logits_ps"), 1)
                pe.wait_ge(S("logits_t"), l + 1)
                for b in range(NB):
                    t = pe.transpose(psum[:, 7, b * 36:(b + 1) * 36], LT[:, b * P:(b + 1) * P], ident[0:36, 0:36])
                t.then_inc(S("logits_turned"), 1)
                if l == 0:
                    mod_group("router")
                pe.wait_ge(S("chosen"), l + 1)
                for b in range(NB):
                    for a in range(b):
                        pe.matmul(psum[:, 6, b * 32:(b + 1) * 32], ones[:, :], oh_sum[:, a, :], start=(a == 0), stop=False)
                    mm = pe.matmul(psum[:, 6, b * 32:(b + 1) * 32], before[:, :], oh_sum[:, b, :], start=(b == 0), stop=True)
                mm.then_inc(S("counts_ps"), 1)
                for a in range(NB):
                    mm = pe.matmul(psum[:, 7, 0:32], ones[:, :], oh_sum[:, a, :], start=(a == 0), stop=(a == NB - 1))
                mm.then_inc(S("counts_ps"), 1)
                if l == 0:
                    mod_products(mods("places")[0])
                    mod_sum(mods("places")[0])

                def gather(q, v, first=False):
                    pe.wait_ge(M("places_ready"), q + 1)
                    if not first:
                        pe.wait_ge(M("x_sb"), q * 2)
                    for half in range(2):
                        cols = slice(half * 512, (half + 1) * 512)
                        for b in range(NB):
                            pe.matmul(bank(half), PP[v][:, b, :], H_HI[:, b, cols], start=(b == 0), stop=False)
                            mm = pe.matmul(bank(half), PP[v][:, b, :], H_LO[:, b, cols], start=False, stop=(b == NB - 1))
                        mm.then_inc(M("xs_ps"), 1)

                def turn_rows(q):
                    pe.wait_ge(M("xs_sb"), q * 2 + 2)
                    for half in range(2):
                        for kk in range(4):
                            t = pe.transpose(psum[:, half, kk * P:(kk + 1) * P], XS[:, 4 * half + kk:D:KC], ident[:, :])
                        t.then_inc(M("x_ps"), 1)

                def weights_back(q, v, first=False):
                    if not first:
                        pe.wait_ge(M("added"), q * 6)
                    for b in range(NB):
                        t = pe.transpose(psum[:, 7, b * P:(b + 1) * P], PW[v][:, b, :], ident[:, :])
                    t.then_inc(M("weights_ps"), 1)

                def combine(q, first=False):
                    pe.wait_ge(M("y_split"), q * 2 + 2)
                    pe.wait_ge(M("slots_t"), q + 1)
                    for c in range(6):
                        b, n = divmod(c, 2)
                        to = bank((6, 7, 4, 5, 6, 7)[c])
                        if c >= 4:
                            pe.wait_ge(M("added"), q * 6 + c - 3)
                        cols = slice(n * 512, (n + 1) * 512)
                        pe.matmul(to, PPT[:, b, :], Y_HI[:, cols], start=True, stop=False)
                        pe.matmul(to, PPT[:, b, :], Y_LO[:, cols], start=False, stop=True).then_inc(M("back_ps"), 1)

                def pair(q, v, first=False):
                    for a in range(2):
                        pe.wait_ge(M(f"in_{3 * v + a}"), landed(q, v))
                    pe.wait_ge(M("x_sb"), q * 2 + 2)
                    if not first:
                        pe.wait_ge(M("hidden"), q)
                    for k in range(KC):
                        for e in range(2):
                            mm = pe.matmul(psum[64 * e:64 * e + 64, 2, :], XT[:, k, 64 * e:64 * e + 64], RG[:, 3 * v:3 * v + 2, e, k, :],
                                           start=(k == 0), stop=(k == KC - 1))
                    mm.then_inc(M("gate_up"), 1)
                    gather(q + 1, 1 - v)
                    pe.wait_ge(M("hidden"), q + 1)
                    if not first:
                        pe.wait_ge(M("hidden_t"), q)
                    for k in range(2):
                        t = pe.transpose(psum[:, 3, k * P:(k + 1) * P], HID[v][:, k:256:2], ident[:, :])
                    t.then_inc(M("hidden_ps"), 1)
                    if not first:
                        combine(q - 1)
                    turn_rows(q + 1)
                    pe.wait_ge(M("hidden_t"), q + 1)
                    pe.wait_ge(M(f"in_{3 * v + 2}"), landed(q, v))
                    if first and l == 0:
                        pe.wait_ge(S("rest_row_ready"), mods("places")[0] - FRONT + 1)
                    if not first:
                        pe.wait_ge(M("added"), q * 6 - 2)
                    for n in range(2):
                        for k in range(2):
                            for e in range(2):
                                mm = pe.matmul(psum[64 * e:64 * e + 64, 4 + n, :], HTS[v][:, k, 64 * e:64 * e + 64],
                                               RD[:, 3 * v + 2, e, k, n * 512:(n + 1) * 512], start=(k == 0), stop=(k == 1))
                        mm.then_inc(M("down"), 1)
                    weights_back(q, v, first)

                def landed(q, v):
                    return (q - v) * 8 + 16

                pe.wait_ge(S("h_split"), l + 1)
                gather(0, 0, first=True)
                turn_rows(0)
                pair(0, 0, first=True)
                pair(1, 1)
                R = rounds_of(pe, l)
                with pe.Fori(1, R * (PAIRS // 2)) as i:
                    for v in range(2):
                        pair(i * 2 + v, v)
                combine(R * PAIRS - 1)

            experts(0)

            mod_group("norm_2")
            turn_and_project(2, "h_ready", [NB * 2 + b + 1 for b in range(NB)], chunk("odd_in", 0), "odd_in_ps")
            w = chunk("odd_in", 1)
            for b in range(NB):
                project(1 + b, b, w).then_inc(S("odd_in_ps"), 1)
            w = chunk("odd_in", 2)
            for i in range(6):
                part, b = divmod(i, 3)
                if i == 2:
                    pe.wait_ge(S("qkv_ready"), 1)
                if part == 1:
                    pe.wait_ge(S("qkv_ready"), 2 + b)
                cols = slice(256 * part, 256 * part + 256)
                project((4 + i) % 8, b, w[:, :, cols], 256).then_inc(S("odd_in_ps"), 1)
                if i == 2:
                    pe.wait_ge(S("qkv_ready"), 6)
                    mod_products(mods("attention")[0])
                if i == 3:
                    mod_sum(mods("attention")[0])
            pe.wait_ge(S("odd_small"), 16 * 5)
            pe.wait_ge(S("qkv_ready"), 12)
            for g in range(KV_HEADS):
                t = pe.transpose(psum[:, 7, g * P:(g + 1) * P], CK[:, g * P:(g + 1) * P], ident[:, :])
            t.then_inc(S("sides_turned"), 1)

            def turn_heads(to, b, cols, heads):
                for h in range(heads):
                    t = pe.transpose(to[:, h * P:(h + 1) * P], QKV[:, b, cols + h * P:cols + (h + 1) * P], ident[:, :])
                return t

            for half in range(2):
                pe.wait_ge(S("qk_normed"), 1 + half)
                if half == 0:
                    pe.wait_ge(S("rest_row_ready"), mods("attention")[0] - FRONT + 1)
                for b in range(NB):
                    turn_heads(bank(3 * half + b), b, 512 * half, 4).then_inc(S("q_turned"), 1)
            pe.wait_ge(S("k_t_ready"), 1)
            pe.wait_ge(S("qk_normed"), 3)
            for b in range(NB):
                t = turn_heads(psum[:, 6 + b // 2, (b % 2) * 256:(b % 2) * 256 + 256], b, D, KV_HEADS)
                if b >= 1:
                    t.then_inc(S("k_turned"), 1)

            def att_scores(i):
                b, g = divmod(i, 2)
                pe.wait_ge(S("exps_ready"), i)
                if i == 0:
                    pe.wait_ge(S("q_t_ready"), 6)
                    pe.wait_ge(S("k_t_ready"), 3)
                keys = KT[:, g, 0:1, :] if b == 0 else KT[:, g, 1:4, :]
                for hh in range(4):
                    mm = pe.matmul(psum[:, hh, 0:keys.shape[1] * P], QT[:, 4 * g + hh, b * P:(b + 1) * P], keys, start=True, stop=True)
                    if hh % 2 == 1:
                        mm.then_inc(S("att_scores_ps"), 1)

            def turn_probs(i):
                pe.wait_ge(S("probs_ready"), i + 1)
                if i >= 1:
                    pe.wait_ge(S("probs_t_ready"), i)
                for kb in range(1 if i < 2 else 3):
                    for hh in range(4):
                        t = pe.transpose(psum[:, 4 + kb, hh * P:(hh + 1) * P], PR[i % 2][:, hh, kb * P:(kb + 1) * P], ident[:, :])
                t.then_inc(S("probs_turned"), 1)

            def att_values(i):
                b, g = divmod(i, 2)
                blocks = 1 if b == 0 else 3
                pe.wait_ge(S("probs_t_ready"), i + 1)
                if i >= 1:
                    pe.wait_ge(S("att_out_ready"), i)
                for kb in range(blocks):
                    if b == 0:
                        vals = QKV[:, 0, 1280 + g * P:1280 + (g + 1) * P]
                    else:
                        vals = CV[:, g * P:(g + 1) * P] if kb == 0 else QKV[:, kb, 1280 + g * P:1280 + (g + 1) * P]
                    mm = pe.matmul(bank(7), vals, PT[:, kb, :], start=(kb == 0), stop=(kb == blocks - 1))
                mm.then_inc(S("probs_t_used"), 1)

            att_scores(0)
            for i in range(6):
                if i < 5:
                    att_scores(i + 1)
                if i >= 1:
                    att_values(i - 1)
                turn_probs(i)
            att_values(5)
            pe.wait_ge(S("att_out_ready"), 6)
            for n in range(2):
                w = chunk("odd_out", n)
                for b in range(NB):
                    project(3 * n + b, b, w).then_inc(S("odd_out_ps"), 1)

            experts(1)

        def att_out(act, i):
            b, g = divmod(i, 2)
            act.wait_ge(S("probs_t_used"), i + 1)
            act.copy(OT[:, 4 * g:4 * g + 4, b * P:(b + 1) * P], bank(7).rearrange("p (h t) -> p h t", h=4)).then_inc(S("att_out_ready"), 1)

        @block.scalar
        def _(act):
            def norm(u):
                norm_squares(u)
                inverse_root(f"norm_{u}", ms, rs)

            def norm_squares(u):
                if u == 0:
                    act.wait_ge(S("x_loaded"), 32)
                for b in range(NB):
                    if u > 0:
                        act.wait_ge(S("x_updated"), NB * (u - 1) + b + 1)
                    a = act.activation(H[:, b, :], X[:, b, :], ACT.Square, accum_out=ss[:, b:b + 1])
                a.then_inc(S("squares"), 1)

            def inverse_root(tag, v, y):
                n = ROOTS.index(tag) + 1
                act.wait_ge(S("mean_squares"), n)
                act.activation(y, v, ACT.Sqrt).then_inc(S("roots"), 1)

            def mod_part_copy(i):
                act.wait_ge(S("mod_part_ps"), 2 * i + 2)
                act.copy(rest_buffers(i)[0], bank(MOD_BANKS[group_of(i)][0])).then_inc(S("mod_part_sb"), 1)

            def mod_row_copy(i):
                part_bank, sum_bank = MOD_BANKS[group_of(i)]
                _, rows, gains = rest_buffers(i)
                act.wait_ge(S("mod_sum_ps"), i + 1)
                if scaled(i):
                    act.copy(gains, psum[0:4, part_bank, :])
                    act.activation(rows, psum[0:4, sum_bank, :], ACT.Identity, bias=1.0).then_inc(S("rest_row_ready"), 1)
                else:
                    act.copy(rows, psum[0:4, sum_bank, :]).then_inc(S("rest_row_ready"), 1)

            def mod_copies(chunks):
                for i in chunks:
                    mod_part_copy(i)
                    mod_row_copy(i)

            def ht_copies(u, both=True):
                for b in range(NB):
                    for half in range(2 if both else 1):
                        act.wait_ge(S("turned"), 6 * TURNS.index(u) + 2 * b + half + 1)
                        act.copy(HT[:, 4 * half:4 * half + 4, b * P:(b + 1) * P],
                                 bank(2 * b + half).rearrange("p (k t) -> p k t", k=4)).then_inc(S(("ht_top", "ht_low")[half]), 1)

            act.wait_ge(S("cond_in"), 32)
            act.wait_ge(S("cond_zero"), 1)
            act.activation(cond_silu[:, :, 2:4], cond, ACT.Silu).then_inc(S("cond_ready"), 1)
            def spread_copies():
                for c in range(8):
                    part, half, stream = c // 4, c // 2 % 2, c % 2
                    act.wait_ge(S("spread_ps"), c + 1)
                    act.copy(GS[:, part, stream, half * COLS:(half + 1) * COLS], bank(6 + c % 2)).then_inc(S("spread_sb"), 1)

            for i in range(FRONT):
                act.wait_ge(S("mod_part_ps"), 2 * i + 2)
                if i >= 2:
                    act.wait_ge(S("mod_sum_ps"), i - 1)
                act.copy(mod_part[i % 2], bank(i % 2)).then_inc(S("mod_part_sb"), 1)
                if i == 1:
                    norm_squares(0)
                    inverse_root("norm_0", ms, rs)
                    spread_copies()
            ht_copies(0)
            act.wait_ge(S("front_stored"), 32 * (FRONT - 2))
            for c in range(2):
                act.wait_ge(S("qk_ps"), c + 1)
                act.mul(QK[:, c, :], psum[:, c, 0:T], GLA_DK ** -0.5).then_inc(S("qk_ready"), 1)
            act.wait_ge(S("decay_in_ps"), 1)
            act.copy(AT, psum[0:32, 4, 0:T]).then_inc(S("decay_in_ready"), 1)

            def evacuate(name, dst, b):
                act.wait_ge(S(f"{name}_ps"), b + 1)
                act.copy(dst[:, b, :], bank(5 + b)).then_inc(S(f"{name}_ready"), 1)

            evacuate("v", V, 0)
            act.wait_ge(S("z_abs"), 1)
            act.activation(EZ, EZ, ACT.Exp, scale=-1.0).then_inc(S("z_logs"), 1)
            act.wait_ge(S("z_logs"), 1)
            act.activation(EZ, EZ, ACT.Ln, bias=1.0).then_inc(S("z_logs"), 1)
            evacuate("v", V, 1)
            evacuate("v", V, 2)
            act.wait_ge(S("masks_ready"), 1)

            def level_exp(n):
                act.wait_ge(S("decays_ready"), n)
                act.activation(EX[(n - 1) % 2], EX[(n - 1) % 2], ACT.Exp, scale=1.0 / GLA_TAU).then_inc(S("decays_exp"), 1)

            def in_plan(steps, mod):
                for step in steps:
                    if step == "part":
                        mod_part_copy(mod)
                    elif step == "sum":
                        mod_row_copy(mod)
                        mod += 1
                    elif isinstance(step, int):
                        if step < 7:
                            level_exp(step + 1)
                        if step == 6:
                            act.wait_ge(S("vg_ready"), 3)
                            act.activation(VG, VG, ACT.Gelu_apprx_tanh).then_inc(S("activated"), 1)
                    else:
                        evacuate(step[:-1], {"g": SG, "vg": VG, "u": U}[step[:-1]], int(step[-1]))
                return mod

            before_levels = EVEN_PLAN.index(0)
            mod = in_plan(EVEN_PLAN[:before_levels], FRONT)
            act.wait_ge(S("sums_ready"), 1)
            act.activation(E2[:, 0], BF[:, :, P:T], ACT.Exp, scale=1.0 / GLA_TAU)
            act.activation(E2[:, 1], BB[:, :, P:T], ACT.Exp, scale=1.0 / GLA_TAU)
            act.activation(E2[:, 2:4], E2[:, 2:4], ACT.Exp, scale=1.0 / GLA_TAU)
            act.activation(dec_f.rearrange("p (c o) -> p c o", o=1), BF[:, :, 2 * P - 1:2 * P], ACT.Exp, scale=1.0 / GLA_TAU)
            act.activation(dec_b.rearrange("p (c o) -> p c o", o=1), BB[:, :, 2 * P:2 * P + 1], ACT.Exp, scale=1.0 / GLA_TAU).then_inc(S("to_end_exp"), 1)
            in_plan(EVEN_PLAN[before_levels:], mod)
            act.wait_ge(S("sides_turned"), 2)
            act.copy(KDT.rearrange("p i t -> p (i t)"), psum[:, 4:6, :].rearrange("p b n -> p (b n)")).then_inc(S("kdt_ready"), 1)
            act.wait_ge(S("u_ready"), 3)
            act.activation(U, U, ACT.Gelu_apprx_tanh).then_inc(S("activated"), 1)
            act.wait_ge(S("g_ready"), 3)
            act.activation(SG, SG, ACT.Silu).then_inc(S("activated"), 1)
            inverse_root("ln", ln_v, ln_rs)
            act.wait_ge(S("gla_out"), 3)
            act.copy(O.rearrange("p b n -> p (b n)"), psum[:, 0:3, :].rearrange("p b n -> p (b n)")).then_inc(S("o_ready"), 1)
            inverse_root("gla", gla_ms, gla_rs)
            mod_copies(mods("gate"))
            ht_copies("cat", both=False)

            def experts(l):
                u = 2 * l + 1

                def M(name):
                    return S(f"moe{l}_{name}")

                norm(u)
                mod_copies(mods(f"norm_{u}"))
                ht_copies(u)
                act.wait_ge(S("logits_ps"), l + 1)
                act.wait_ge(S("router_in"), 16 * 4 * (l + 1))
                act.activation(LT, psum[0:36, 6, 0:T], ACT.Identity, bias=BR).then_inc(S("logits_t"), 1)
                act.wait_ge(S("router_sub"), l + 1)
                act.activation(g_tmp, g_tmp, ACT.Exp)
                act.activation(top_f[:, :, 0:1], top_f[:, :, 1:2], ACT.Exp).then_inc(S("router_exp"), 1)
                if l == 0:
                    mod_copies(mods("router"))
                    mod_copies(mods("places"))

                def rows_copies(q, first=False):
                    for half in range(2):
                        act.wait_ge(M("xs_ps"), q * 2 + half + 1)
                        if not first and half == 0:
                            act.wait_ge(M("x_ps"), q * 2)
                        act.copy(XS[:, half * 512:(half + 1) * 512], bank(half)).then_inc(M("xs_sb"), 1)

                def x_copies(q, first=False):
                    for half in range(2):
                        act.wait_ge(M("x_ps"), q * 2 + half + 1)
                        if not first and half == 0:
                            act.wait_ge(M("gate_up"), q)
                        act.copy(XT[:, 4 * half:4 * half + 4, :], bank(half).rearrange("p (k s) -> p k s", k=4)).then_inc(M("x_sb"), 1)

                def weights_copy(q, first=False):
                    act.wait_ge(M("weights_ps"), q + 1)
                    if not first:
                        act.wait_ge(M("slots_t"), q)
                    act.activation(PWT, psum[:, 7, 0:T].rearrange("p (b t) -> p b t", b=NB), ACT.Copy, accum_out=w_slot).then_inc(M("weights_sb"), 1)

                def pair(q, v, first=False, second=False):
                    act.wait_ge(M("gate_up"), q + 1)
                    if not first and not second:
                        act.wait_ge(M("hidden"), q - 1)
                    act.activation(SGM[v], psum[:, 2, 0:256], ACT.Silu).then_inc(M("gated"), 1)
                    rows_copies(q + 1)
                    x_copies(q + 1)
                    weights_copy(q, first)
                    act.wait_ge(M("weights_sb"), q + 1)
                    for n in range(2):
                        act.wait_ge(M("down"), q * 2 + n + 1)
                        if not first and n == 0:
                            act.wait_ge(M("back_ps"), q * 6)
                        act.activation(Y[:, n * 512:(n + 1) * 512], bank(4 + n), ACT.Copy, scale=w_slot).then_inc(M("y_sb"), 1)

                rows_copies(0, first=True)
                x_copies(0, first=True)
                pair(0, 0, first=True)
                pair(1, 1, second=True)
                R = rounds_of(act, l)
                with act.Fori(1, R * (PAIRS // 2)) as i:
                    for v in range(2):
                        pair(i * 2 + v, v)

            experts(0)

            mod_copies(mods("norm_2")[:1])
            norm(2)
            mod_copies(mods("norm_2")[1:])
            ht_copies(2)
            for i in range(12):
                act.wait_ge(S("odd_in_ps"), i + 1)
                if i < 6:
                    n, b = divmod(i, 3)
                    act.copy(QKV[:, b, n * 512:(n + 1) * 512], bank((6 + i) % 8)).then_inc(S("qkv_ready"), 1)
                    if b == 2:
                        inverse_root(f"qk_{n}", q_ms[n], q_rs[n])
                    continue
                part, b = divmod(i - 6, 3)
                act.copy(QKV[:, b, D + 256 * part:D + 256 * part + 256], psum[:, (4 + i - 6) % 8, 0:256]).then_inc(S("qkv_ready"), 1)
                if i == 8:
                    mod_part_copy(mods("attention")[0])
                if i == 9:
                    inverse_root("qk_2", q_ms[2], q_rs[2])
                    mod_row_copy(mods("attention")[0])
            act.wait_ge(S("sides_turned"), 3)
            act.copy(KT[:, :, 1, :], psum[:, 7, 0:256].rearrange("p (g t) -> p g t", g=2)).then_inc(S("k_t_ready"), 1)
            for i in range(6):
                half, b = divmod(i, 3)
                act.wait_ge(S("q_turned"), i + 1)
                act.copy(QT[:, 4 * half:4 * half + 4, b * P:(b + 1) * P],
                         bank(i).rearrange("p (h t) -> p h t", h=4)).then_inc(S("q_t_ready"), 1)
            act.wait_ge(S("k_turned"), 1)
            act.copy(KT[:, :, 0:3:2, :], bank(6).rearrange("p (b g t) -> p g b t", b=2, g=2)).then_inc(S("k_t_ready"), 1)
            act.wait_ge(S("k_turned"), 2)
            act.copy(KT[:, :, 3, :], psum[:, 7, 0:256].rearrange("p (g t) -> p g t", g=2)).then_inc(S("k_t_ready"), 1)
            for i in range(6):
                n = P if i < 2 else 3 * P
                if i >= 2:
                    act.wait_ge(S("probs_turned"), i - 1)
                for hh in range(4):
                    if hh % 2 == 0:
                        act.wait_ge(S("max_ready"), 2 * i + hh // 2 + 1)
                    a = act.activation(PR[i % 2][:, hh, 0:n], psum[:, hh, 0:n], ACT.Exp, bias=att_max[:, i, hh:hh + 1],
                                       scale=HD ** -0.5, accum_out=att_sum[:, i, hh:hh + 1])
                a.then_inc(S("exps_ready"), 1)
                if i >= 2:
                    att_out(act, i - 2)
            att_out(act, 4)
            att_out(act, 5)
            experts(1)
            norm(4)

        @block.vector
        def _(dve):
            links = [0]

            def link(ins):
                links[0] += 1
                ins.then_inc(S("dve_links"), 1)
                dve.wait_ge(S("dve_links"), links[0])

            def inverse_root(tag, v, y, t):
                dve.wait_ge(S("roots"), ROOTS.index(tag) + 1)
                link(dve.reciprocal(y, y))
                link(dve.scalar_tensor_tensor(t, y, -0.5, y, ALU.mult, ALU.mult))
                link(dve.tensor_tensor(t, t, v, ALU.mult))
                link(dve.scalar_tensor_tensor(y, t, 1.5, y, ALU.add, ALU.mult))

            def norm(u):
                norm_means(u)
                norm_apply(u)

            def norm_means(u):
                dve.wait_ge(S("squares"), u + 1)
                if u > 0:
                    dve.wait_ge(S("x_updated"), NB * u)
                dve.tensor_scalar(ms, ss, 1.0 / D, EPS, ALU.mult, ALU.add).then_inc(S("mean_squares"), 1)

            def norm_apply(u):
                inverse_root(f"norm_{u}", ms, rs, rt)
                if u == 0:
                    dve.wait_ge(S("spread_sb"), 8)
                else:
                    dve.wait_ge(S("rows_in"), 16 * u)
                for b in range(NB):
                    s = min(b, 1)
                    gain = GS[:, 1, s, :] if u < 4 else GS[:, 0, 0, :]
                    a = dve.scalar_tensor_tensor(H[:, b, :], X[:, b, :], rs[:, b:b + 1], gain, ALU.mult, ALU.mult)
                    if u == 4:
                        a.then_inc(S("h_ready"), 1)
                        continue
                    link(a)
                    dve.tensor_tensor(H[:, b, :], H[:, b, :], GS[:, 0, s, :], ALU.add).then_inc(S("h_ready"), 1)

            def ht_copies(u):
                for b in range(NB):
                    dve.wait_ge(S("turned"), 6 * TURNS.index(u) + 2 * b + 2)
                    dve.tensor_copy(HT[:, 4:8, b * P:(b + 1) * P], bank(2 * b + 1).rearrange("p (k t) -> p k t", k=4)).then_inc(S("ht_low"), 1)

            def update(u, ps, bank_of, buf):
                dve.wait_ge(S("gate_in"), 16 * (u + 1))
                for c in range(6):
                    n, b = divmod(c, 3)
                    cols = slice(n * 512, (n + 1) * 512)
                    dve.wait_ge(S(ps), c + 1)
                    link(dve.tensor_tensor(buf[c % 2], bank(bank_of(c)), GT[:, min(b, 1), cols], ALU.mult))
                    a = dve.tensor_tensor(X[:, b, cols], X[:, b, cols], buf[c % 2], ALU.add)
                    if n == 1:
                        a.then_inc(S("x_updated"), 1)

            dve.memset(ones[:, :], 1.0)
            dve.memset(cond_silu, 0.0).then_inc(S("cond_zero"), 1)
            dve.wait_ge(S("mod_small"), 16 * 7)
            dve.tensor_copy(pick_bias[:, :], pick[0:64, 4:4 + 2 * 32])
            dve.tensor_copy(mod_bias[:, :], bias_raw).then_inc(S("bias_ready"), 1)
            dve.wait_ge(S("bias_ready"), 1)
            dve.tensor_tensor(mod_bias[32:64, :], bias_raw[32:64, :], mod_bias[32:64, :], ALU.subtract).then_inc(S("bias_ready"), 1)
            for i in range(FRONT):
                if i == 2:
                    norm_means(0)
                    norm_apply(0)
                dve.wait_ge(S("mod_sum_ps"), i + 1)
                sums, gains = (psum[0:4, to, :] for to in FRONT_BANKS[i])
                if scaled(i):
                    link(dve.tensor_copy(front_row[i], gains))
                    a = dve.scalar_tensor_tensor(front_row[i], sums, 1.0, front_row[i], ALU.add, ALU.mult)
                else:
                    a = dve.tensor_copy(front_row[i], sums)
                a.then_inc(S("front_row_ready"), 1)
            dve.wait_ge(S("even_first"), 16 * 3)
            dve.tensor_copy(masks[:, :], MASKS_F32).then_inc(S("masks_ready"), 1)

            dve.wait_ge(S("front_stored"), 32 * (FRONT - 2))
            for c in (2, 3):
                dve.wait_ge(S("qk_ps"), c + 1)
                dve.tensor_copy(QK[:, c, :], psum[:, c, 0:T]).then_inc(S("qk_ready"), 1)
            dve.wait_ge(S("sides_turned"), 1)
            dve.tensor_copy(WST.rearrange("p g t -> p (g t)"), bank(7)).then_inc(S("spatial_ready"), 1)
            for j in range(4):
                dve.wait_ge(S("decay_ps"), j + 1)
                dve.tensor_scalar(Z[:, j, :], psum[:, j, 0:T], b_gate[:, j:j + 1], None, ALU.add).then_inc(S("z_ready"), 1)
            dve.wait_ge(S("z_ready"), 4)
            dve.scalar_tensor_tensor(EZ, Z, -1.0, Z, ALU.mult, ALU.max).then_inc(S("z_abs"), 1)
            dve.wait_ge(S("z_logs"), 2)
            link(dve.scalar_tensor_tensor(Z, Z, 0.0, EZ, ALU.min, ALU.subtract))
            for c in range(2):
                for b in range(NB):
                    blk = slice(b * P, (b + 1) * P)
                    dve.tensor_tensor_scan(BF[:, c, blk], ones[:, :], Z[:, c, blk], 0.0, ALU.mult, ALU.add)
                    a = dve.tensor_tensor_scan(BB[:, c, blk][:, ::-1], ones[:, :], Z[:, 2 + c, blk][:, ::-1], 0.0, ALU.mult, ALU.add)
            link(a)

            def blocks(v):
                return v.rearrange("p c (b t) -> p c b t", t=P)

            to_f = blocks(E2[:, 2])
            to_b = blocks(E2[:, 3])
            dve.tensor_tensor(to_f, blocks(BF)[:, :, 0:2, P - 1:P].broadcast_to([P, 2, 2, P]), blocks(BF)[:, :, 0:2, :], ALU.subtract)
            dve.tensor_tensor(to_b, blocks(BB)[:, :, 0:3:2, 0:1].broadcast_to([P, 2, 2, P]), blocks(BB)[:, :, 0:3:2, :], ALU.subtract).then_inc(S("sums_ready"), 1)

            def level_decays(n):
                m = LEVELS[n - 1]
                if n >= 3:
                    dve.wait_ge(S("scores_ps"), n - 1)

                def halves(v):
                    return v.rearrange("p c (a h m) -> p c a h m", h=2, m=m)

                ex, f, g = halves(EX[(n - 1) % 2]), halves(BF), halves(BB)
                shape = [P, 2, T // (2 * m), m]
                border_f = f[:, :, :, 0, m - 1:m].broadcast_to(shape)
                border_b = g[:, :, :, 1, 0:1].broadcast_to(shape)
                dve.tensor_tensor(ex[:, 0:2, :, 1, :], f[:, :, :, 1, :], border_f, ALU.subtract)
                dve.tensor_tensor(ex[:, 0:2, :, 0, :], g[:, :, :, 0, :], border_b, ALU.subtract)
                dve.tensor_tensor(ex[:, 2:4, :, 0, :], border_f, f[:, :, :, 0, :], ALU.subtract)
                dve.tensor_tensor(ex[:, 2:4, :, 1, :], border_b, g[:, :, :, 1, :], ALU.subtract).then_inc(S("decays_ready"), 1)

            def scores_of(r):
                return psum[:, 2 * r:2 * r + 2, :].rearrange("p b n -> p (b n)")[:, 0:6 * P].rearrange("p (i t) -> p i t", i=6)

            def merge(n):
                dve.wait_ge(S("scores_ps"), n + 1)
                if n >= 1:
                    dve.wait_ge(S("att_merged"), 2 * n)
                for r in range(2):
                    att = ATT[:, 6 * r:6 * r + 6, :]
                    if n == 0:
                        eye = ident[:, :].rearrange("p (o t) -> p o t", o=1).broadcast_to([P, 6, P])
                        a = dve.scalar_tensor_tensor(att, scores_of(r), 2.0, eye, ALU.mult, ALU.mult)
                    else:
                        mask = masks[:, (n - 1) * P:n * P].rearrange("p (o t) -> p o t", o=1).broadcast_to([P, 6, P])
                        a = dve.copy_predicated(att, mask, scores_of(r))
                    a.then_inc(S("att_merged"), 1)

            level_decays(1)
            dve.wait_ge(S("to_end_exp"), 1)
            for a_ in range(2):
                dve.tensor_tensor(E2[:, a_], E2[:, a_], QK[:, 0:2, P:T], ALU.mult)
            dve.tensor_tensor(to_f, to_f, blocks(QK[:, 2:4, :])[:, :, 0:2, :], ALU.mult)
            dve.tensor_tensor(to_b, to_b, blocks(QK[:, 2:4, :])[:, :, 0:3:2, :], ALU.mult).then_inc(S("to_end_ready"), 1)
            for n in range(1, 8):
                dve.wait_ge(S("decays_exp"), n)
                dve.tensor_tensor(EX[(n - 1) % 2], EX[(n - 1) % 2], QK, ALU.mult).then_inc(S("decayed_ready"), 1)
                merge(n - 1)
                if n < 7:
                    level_decays(n + 1)
            dve.wait_ge(S("activated"), 1)
            for i in range(12):
                b, g = divmod(i, 4)
                a = dve.bn_stats(BN[:, i, 0:6], VG[:, b, g * P:(g + 1) * P])
            link(a)
            for i in range(12):
                a = dve.bn_aggr(BN[:, i, 6:8], BN[:, i, 0:6])
            link(a)
            dve.tensor_scalar(ln_v.rearrange("p (i o) -> p i o", o=1), BN[:, :, 7:8], EPS, None, ALU.add).then_inc(S("mean_squares"), 1)
            merge(7)

            dve.wait_ge(S("state_ps"), 1)
            dve.wait_ge(S("decays_exp"), 7)
            for a_ in range(2):
                a = dve.tensor_copy(ST_OUT[:, a_].rearrange("p c v -> p (c v)"), psum[:, 6 + a_, 0:256])
            a.then_inc(S("states_ready"), 1)
            dve.wait_ge(S("state_in"), 16 * 8)
            dve.wait_ge(S("pool_steps"), 2)
            for a_ in range(2):
                for h in range(GLA_HEADS):
                    c, r = divmod(h, 2)
                    rows = slice(64 * r, 64 * r + 64)
                    dec = (dec_f, dec_b)[a_]
                    a = dve.scalar_tensor_tensor(S1[rows, a_, h, :], S0[rows, a_, h, :], dec[rows, c:c + 1],
                                                 psum[rows, 6 + a_, (2 + c) * P:(3 + c) * P], ALU.mult, ALU.add)
            a.then_inc(S("states_ready"), 1)

            inverse_root("ln", ln_v, ln_rs, ln_rt)
            for i in range(12):
                b, g = divmod(i, 4)
                v = VG[:, b, g * P:(g + 1) * P]
                a = dve.tensor_scalar(v, v, BN[:, i, 6:7], ln_rs[:, i:i + 1], ALU.subtract, ALU.mult)
            a.then_inc(S("vg_normed"), 1)
            dve.wait_ge(S("activated"), 3)
            sg_all = SG.rearrange("p b (h v) -> p (b h) v", v=P)
            a = dve.tensor_tensor(sg_all, sg_all, GLAG.rearrange("p (o v) -> p o v", o=1).broadcast_to([P, 12, P]), ALU.mult)
            a.then_inc(S("gla_gain_ready"), 1)
            dve.wait_ge(S("o_ready"), 1)
            o_all = O.rearrange("p b n -> p (b n)")
            link(dve.tensor_tensor(OSQ, o_all, o_all, ALU.mult))
            link(dve.tensor_reduce(gla_ms, OSQ.rearrange("p (i v) -> p i v", v=P), AX.X, ALU.add))
            dve.tensor_scalar(gla_ms, gla_ms, 1.0 / GLA_DV, EPS, ALU.mult, ALU.add).then_inc(S("mean_squares"), 1)
            inverse_root("gla", gla_ms, gla_rs, gla_rt)
            o_heads = O.rearrange("p b (h v) -> p (b h) v", v=P)
            link(dve.tensor_tensor(o_heads, o_heads, gla_rs.rearrange("p (i o) -> p i o", o=1).broadcast_to([P, 12, P]), ALU.mult))
            dve.wait_ge(S("gla_gain_ready"), 1)
            dve.tensor_tensor(H[:, :, 0:512], O, SG, ALU.mult)
            dve.wait_ge(S("activated"), 2)
            for g in range(GROUPS):
                dve.wait_ge(S("spatial_ps"), g + 1)
                cols = slice(g * P, (g + 1) * P)
                a = dve.scalar_tensor_tensor(H[:, :, 512 + g * P:512 + (g + 1) * P], psum[:, 3 + g, 0:T].rearrange("p (b c) -> p b c", b=NB),
                                             b_spat[:, g:g + 1], U[:, :, cols], ALU.add, ALU.mult)
            a.then_inc(S("cat_ready"), 1)
            ht_copies("cat")
            update(0, "even_out_ps", lambda c: (6 + c) % 8, UPD)

            def experts(l):
                u = 2 * l + 1

                def M(name):
                    return S(f"moe{l}_{name}")

                norm(u)

                dve.wait_ge(S("h_ready"), NB * (u + 1))
                dve.tensor_copy(H_HI, H).then_inc(S("h_top"), 1)

                def wide(v, n):
                    return v.rearrange("p (b o) -> p b o", o=1).broadcast_to([P, NB, n])

                dve.wait_ge(S("logits_turned"), l + 1)
                link(dve.tensor_copy(LG.rearrange("p b n -> p (b n)"), psum[:, 7, 0:NB * 36]))
                link(dve.tensor_reduce(g_max, LG[:, :, 0:4], AX.X, ALU.max))
                link(dve.tensor_tensor(g_tmp, LG[:, :, 0:4], wide(g_max, 4), ALU.is_equal))
                four = iota[:, 0:4].rearrange("p (o n) -> p o n", o=1).broadcast_to([P, NB, 4])
                link(dve.scalar_tensor_tensor(e_mask[:, :, 0:4], four, -8.0, g_tmp, ALU.add, ALU.mult))
                link(dve.tensor_reduce(g_idx, e_mask[:, :, 0:4], AX.X, ALU.min))
                link(dve.tensor_scalar(g_idx, g_idx, 8.0, None, ALU.add))
                link(dve.tensor_tensor(g_tmp, LG[:, :, 0:4], wide(g_max, 4), ALU.subtract))
                e_groups = e_mask.rearrange("p b (g n) -> p b g n", g=MOE_GROUPS)
                shape = [P, NB, MOE_GROUPS, PER_GROUP]
                of_token = g_idx.rearrange("p (b g n) -> p b g n", g=1, n=1).broadcast_to(shape)
                of_group = iota[:, 0:MOE_GROUPS].rearrange("p (b g n) -> p b g n", b=1, n=1).broadcast_to(shape)
                link(dve.tensor_tensor(e_groups, of_token, of_group, ALU.is_equal))
                link(dve.tensor_scalar(e_mask, e_mask, BIG, -BIG, ALU.mult, ALU.add))
                link(dve.tensor_tensor(e_mask, e_mask, LG[:, :, 4:36], ALU.add))
                for b in range(NB):
                    a = dve.max(top_v[:, b, :], e_mask[:, b, :])
                link(a)
                for b in range(NB):
                    a = dve.max_index(top_i[:, b, :].bitcast(U32), top_v[:, b, :], e_mask[:, b, :])
                link(a)
                dve.tensor_tensor(top_f[:, :, 1:2], top_v[:, :, 1:2], top_v[:, :, 0:1], ALU.subtract).then_inc(S("router_sub"), 1)
                dve.wait_ge(S("router_exp"), l + 1)
                link(dve.tensor_reduce(g_sum, g_tmp, AX.X, ALU.add))
                link(dve.reciprocal(g_prob, g_sum))
                e1 = top_f[:, :, 0]
                link(dve.tensor_scalar(g_sum, e1, 1.0, None, ALU.add))
                link(dve.reciprocal(g_sum, g_sum))
                link(dve.tensor_tensor(gates[:, 0, :], g_sum, g_prob, ALU.mult))
                link(dve.tensor_tensor(gates[:, 1, :], gates[:, 0, :], e1, ALU.mult))
                link(dve.tensor_copy(top_f, top_i[:, :, 0:2].bitcast(U32)))
                all32 = iota32.rearrange("p (o n) -> p o n", o=1).broadcast_to([P, NB, 32])
                for j in range(2):
                    link(dve.tensor_tensor(oh[j], all32, top_f[:, :, j:j + 1].broadcast_to([P, NB, 32]), ALU.is_equal))
                dve.tensor_tensor(oh_sum, oh[0], oh[1], ALU.add).then_inc(S("chosen"), 1)
                link(dve.memset(ht_t[:, :], 0.0))
                dve.wait_ge(S("counts_ps"), 2 * l + 1)
                link(dve.tensor_copy(cnt.rearrange("p b n -> p (b n)"), psum[:, 6, 0:96]))
                for j in range(2):
                    link(dve.tensor_tensor(oh[j], oh[j], cnt, ALU.mult))
                    link(dve.tensor_reduce(pos[:, j, :], oh[j], AX.X, ALU.add))
                p6 = pos.rearrange("p j b -> p (j b)")
                shape = [P, 6, MAX_ROUNDS - 1]
                after_round = iota[:, 1:MAX_ROUNDS].rearrange("p (i k) -> p i k", i=1).broadcast_to(shape)
                link(dve.scalar_tensor_tensor(passed, p6.rearrange("p (i k) -> p i k", k=1).broadcast_to(shape), 1.0 / HALF, after_round, ALU.mult, ALU.is_ge))
                link(dve.tensor_reduce(i_a, passed, AX.X, ALU.add))
                link(dve.scalar_tensor_tensor(p6, i_a, float(HALF * (N_EXP - 1)), p6, ALU.mult, ALU.add))
                for j in range(2):
                    link(dve.scalar_tensor_tensor(srel[:, j, :], top_f[:, :, j], float(HALF), pos[:, j, :], ALU.mult, ALU.add))
                STEPS = 8

                def places(q, v, first=False, second=False):
                    if not first:
                        dve.wait_ge(M("place_steps"), q * STEPS)
                    if not first and not second:
                        dve.wait_ge(M("xs_ps"), q * 2 - 2)
                        dve.wait_ge(M("weights_ps"), q - 1)
                    for b in range(NB):
                        for j, to in ((0, PW[v]), (1, PTMP)):
                            dve.tensor_scalar(to[:, b, :], iota[:, :], srel[:, j, b:b + 1], gates[:, j, b:b + 1],
                                              ALU.is_equal, ALU.mult).then_inc(M("place_steps"), 1)
                    dve.wait_ge(M("place_steps"), q * STEPS + 6)
                    dve.tensor_tensor(PW[v], PW[v], PTMP, ALU.add).then_inc(M("place_steps"), 1)
                    dve.tensor_scalar(srel, srel, float(-P), None, ALU.add).then_inc(M("place_steps"), 1)
                    dve.wait_ge(M("place_steps"), q * STEPS + 7)
                    dve.tensor_scalar(PP[v], PW[v], 0.0, None, ALU.not_equal).then_inc(M("places_ready"), 1)

                def hidden(q, v, first=False, second=False):
                    dve.wait_ge(M("gated"), q + 1)
                    if not first and not second:
                        dve.wait_ge(M("hidden_ps"), q - 1)
                    dve.tensor_tensor(HID[v], SGM[v], psum[:, 2, 256:512], ALU.mult).then_inc(M("hidden"), 1)
                    dve.wait_ge(M("hidden_ps"), q + 1)
                    if not first and not second:
                        dve.wait_ge(M("down"), q * 2 - 2)
                    dve.tensor_copy(HTS[v].rearrange("p k s -> p (k s)"), psum[:, 3, 0:256]).then_inc(M("hidden_t"), 1)

                def add_back(q, first=False):
                    for c in range(6):
                        b, n = divmod(c, 2)
                        dve.wait_ge(M("back_ps"), q * 6 + c + 1)
                        if not first and c == 0:
                            dve.wait_ge(M("added"), q * 6)
                        acc = ACC[:, b, n * 512:(n + 1) * 512]
                        dve.tensor_tensor(acc, acc, bank((6, 7, 4, 5, 6, 7)[c]), ALU.add).then_inc(M("added"), 1)

                def split(q):
                    dve.wait_ge(M("weights_sb"), q + 1)
                    dve.tensor_scalar(PPT, PWT, 0.0, None, ALU.not_equal).then_inc(M("slots_t"), 1)
                    dve.wait_ge(M("y_sb"), q * 2 + 2)
                    dve.tensor_copy(Y_HI, Y).then_inc(M("y_split"), 1)
                    dve.wait_ge(M("y_split"), q * 2 + 1)
                    dve.tensor_tensor(Y_LO, Y, Y_HI, ALU.subtract).then_inc(M("y_split"), 1)

                def pair(q, v, first=False, second=False):
                    places(q + 1, 1 - v, second=first)
                    hidden(q, v, first, second)
                    if not first:
                        add_back(q - 1, second)
                    split(q)

                places(0, 0, first=True)
                dve.wait_ge(S("counts_ps"), 2 * l + 2)
                link(dve.tensor_reduce(n_max, psum[:, 7, 0:32], AX.X, ALU.max))
                link(dve.scalar_tensor_tensor(n_tmp, n_max.broadcast_to([P, MAX_ROUNDS - 1]), 1.0 / HALF, iota[:, 1:MAX_ROUNDS], ALU.mult, ALU.is_gt))
                link(dve.tensor_reduce(n_rounds, n_tmp, AX.X, ALU.add))
                dve.tensor_copy(rounds.bitcast(U32), n_rounds).then_inc(S("rounds_ready"), 1)
                pair(0, 0, first=True)
                pair(1, 1, second=True)
                R = rounds_of(dve, l)
                with dve.Fori(1, R * (PAIRS // 2)) as i:
                    for v in range(2):
                        pair(i * 2 + v, v)
                add_back(R * PAIRS - 1)
                dve.wait_ge(M("added"), R * (PAIRS * 6))
                dve.wait_ge(M("x_sb"), R * (PAIRS * 2) + 2)
                dve.wait_ge(S("gate_in"), 16 * (u + 1))
                for b in range(NB):
                    link(dve.tensor_tensor(UPD_M[b % 2], ACC[:, b, :], GT[:, min(b, 1), :], ALU.mult))
                    dve.tensor_tensor(X[:, b, :], X[:, b, :], UPD_M[b % 2], ALU.add).then_inc(S("x_updated"), 1)

            experts(0)

            norm(2)
            dve.wait_ge(S("odd_small"), 16 * 5)
            for n in range(3):
                heads_ = KV_HEADS if n == 2 else 4
                dve.wait_ge(S("qkv_ready"), NB * (n + 1))
                if n > 0:
                    dve.wait_ge(S("qk_normed"), n)

                def by_head(v, b=NB):
                    return v.rearrange("p (b h n) -> p b h n", b=b, h=heads_)

                heads = QKV[:, :, n * 512:n * 512 + heads_ * HD].rearrange("p b (h n) -> p b h n", h=heads_)
                sq = by_head(SQ_QK[:, 0:NB * heads_ * HD])
                link(dve.tensor_tensor(sq, heads, heads, ALU.mult))
                link(dve.tensor_reduce(q_ms[n], SQ_QK[:, 0:NB * heads_ * HD].rearrange("p (i n) -> p i n", n=HD), AX.X, ALU.add))
                dve.tensor_scalar(q_ms[n], q_ms[n], 1.0 / HD, EPS, ALU.mult, ALU.add).then_inc(S("mean_squares"), 1)
                inverse_root(f"qk_{n}", q_ms[n], q_rs[n], q_rt[n])
                shape = [P, NB, heads_, HD]
                gain = (GK if n == 2 else GQ).rearrange("p (b h n) -> p b h n", b=1, h=1).broadcast_to(shape)
                link(dve.tensor_tensor(heads, heads, by_head(q_rs[n]).broadcast_to(shape), ALU.mult))
                link(dve.tensor_tensor(heads, heads, gain, ALU.mult))
                x1, x2 = heads[:, 1:3, :, 0:HD:2], heads[:, 1:3, :, 1:HD:2]
                cos, sin = (ROPE[:, :, i, :].rearrange("p b (h n) -> p b h n", h=1).broadcast_to([P, 2, heads_, HD // 2]) for i in range(2))
                t1, t2, t3, t4 = (by_head(t[:, 0:heads_ * HD], 2) for t in ROPE_TMP)
                dve.tensor_tensor(t1, x1, cos, ALU.mult)
                dve.tensor_tensor(t2, x2, sin, ALU.mult)
                dve.tensor_tensor(t3, x1, sin, ALU.mult)
                link(dve.tensor_tensor(t4, x2, cos, ALU.mult))
                dve.tensor_tensor(x1, t1, t2, ALU.subtract)
                dve.tensor_tensor(x2, t3, t4, ALU.add).then_inc(S("qk_normed"), 1)

            def score_max(i):
                for pair in range(2):
                    m = att_max[:, i, 2 * pair:2 * pair + 2]
                    dve.wait_ge(S("att_scores_ps"), 2 * i + pair + 1)
                    link(dve.tensor_reduce(m, psum[:, 2 * pair:2 * pair + 2, 0:P if i < 2 else 3 * P], AX.X, ALU.max))
                    dve.tensor_scalar(m, m, -HD ** -0.5, None, ALU.mult).then_inc(S("max_ready"), 1)

            score_max(0)
            for i in range(6):
                n = P if i < 2 else 3 * P
                blocks_ = n // P
                dve.wait_ge(S("exps_ready"), i + 1)
                link(dve.reciprocal(att_sum[:, i, :], att_sum[:, i, :]))
                pr = PR[i % 2][:, :, 0:n]
                inv = att_sum[:, i, :].rearrange("p (h o) -> p h o", o=1).broadcast_to([P, 4, n])
                dve.tensor_tensor(pr, pr, inv, ALU.mult).then_inc(S("probs_ready"), 1)
                if i < 5:
                    score_max(i + 1)
                dve.wait_ge(S("probs_turned"), i + 1)
                if i >= 1:
                    dve.wait_ge(S("probs_t_used"), i)
                dve.tensor_copy(PT[:, 0:blocks_, :], psum[:, 4:4 + blocks_, :]).then_inc(S("probs_t_ready"), 1)
            update(2, "odd_out_ps", lambda c: c, UPD_O)
            experts(1)
            norm(4)


_INS = ["x_prompt", "x_sample", "state_gla", "cache_k", "cache_v", "c", "c_ctx", "w_mod", "b_mod", "norm1_g", "norm2_g",
        "w_in_even", "w_gate_up", "b_gate_up", "gla_norm_g", "w_spatial", "b_spatial", "w_out_even", "w_in_odd", "q_norm_g",
        "k_norm_g", "w_out_odd", "w_router_group", "b_router_group", "w_router_expert", "b_router_expert", "w_exp_gate",
        "w_exp_up", "w_exp_down", "final_norm_g"]
_OUTS = {"y_prompt": (1, 128, 1024), "y_sample": (1, 256, 1024), "new_state_gla": (1, 1, 2, 4, 64, 128),
         "new_cache_k": (1, 1, 128, 2, 128), "new_cache_v": (1, 1, 128, 2, 128)}


def kernel(**inputs):
    import concourse.bacc as _bacc
    from concourse.bass_utils import run_bass_kernel_spmd as _run

    nc = _bacc.Bacc("TRN2", target_bir_lowering=False, num_devices=1)
    arrays = {f"in_{n}": np.ascontiguousarray(inputs[n]) for n in _INS}
    arrays.update({f"in_{n}": a for n, a in shape_constants().items()})
    d = {n[3:]: nc.dram_tensor(n, a.shape, mybir.dt.from_np(a.dtype), kind="ExternalInput").ap() for n, a in arrays.items()}
    outs = {n: nc.dram_tensor(f"out_{n}", s, F32, kind="ExternalOutput").ap() for n, s in _OUTS.items()}
    build(nc, d, outs)
    r = _run(nc, [arrays], core_ids=[0])
    return tuple(r.results[0][f"out_{n}"] for n in _OUTS)
```
